# Optimizing a Trainium2 kernel written in Bass

```python
import jax, jax.numpy as jnp
from jax import lax
import numpy as np
import math

D_MODEL = 1024
BATCH = 1
SEQ = 512
DEPTH = 1

CHUNK = 64
Q_BLOCK = 128
POOL_WIDTH = D_MODEL // 2
POOL_WINDOWS = (2, 4, 8, 16)
N_POOL_GROUPS = len(POOL_WINDOWS)
POOL_GROUP = POOL_WIDTH // N_POOL_GROUPS
SB_HEAD_DIM = 64
SB_HEADS = (D_MODEL // 2) // SB_HEAD_DIM
SB_WIDTH = SB_HEADS * SB_HEAD_DIM
IN_WIDTH = POOL_WIDTH + 3 * SB_WIDTH
N_BRANCHES = 2
D_FF = 4 * D_MODEL
RMS_EPS = 1e-6


def rmsnorm(x, gain):
    xf = x.astype(jnp.float32)
    y = xf * lax.rsqrt(jnp.mean(xf * xf, axis=-1, keepdims=True) + RMS_EPS)
    return (y * gain.astype(jnp.float32)).astype(x.dtype)

def multiscale_pool(u, w_pool_mix, pool_scale):
    S = u.shape[1]
    uf = u.astype(jnp.float32)
    cs = jnp.concatenate([jnp.zeros_like(uf[:, :1]), jnp.cumsum(uf, axis=1)], axis=1)
    hi = jnp.arange(S) + 1
    outs = []
    for g, w in enumerate(POOL_WINDOWS):
        c0, c1 = g * POOL_GROUP, (g + 1) * POOL_GROUP
        lo = jnp.maximum(hi - w, 0)
        csg = cs[:, :, c0:c1]
        win_sum = csg[:, hi] - csg[:, lo]
        count = (hi - lo).astype(jnp.float32)[None, :, None]
        pooled = win_sum / count - uf[:, :, c0:c1]
        outs.append(jnp.einsum('bsc,cd->bsd', pooled.astype(u.dtype), w_pool_mix[g]))
    y = jnp.concatenate(outs, axis=-1)
    return y * pool_scale

def stick_breaking_attention(q, k, v):
    S = q.shape[2]
    scale = SB_HEAD_DIM ** -0.5
    outs = []
    for blk in range(S // Q_BLOCK):
        t0, t1 = blk * Q_BLOCK, (blk + 1) * Q_BLOCK
        qb, kb, vb = q[:, :, t0:t1], k[:, :, :t1], v[:, :, :t1]
        z = jnp.einsum('bhqd,bhkd->bhqk', qb, kb).astype(jnp.float32) * scale
        mask = jnp.arange(t1)[None, :] < jnp.arange(t0, t1)[:, None]
        log_1mb = jnp.where(mask, jax.nn.log_sigmoid(-z), 0.0)
        tail = lax.cumsum(log_1mb, axis=3, reverse=True) - log_1mb
        attn = jnp.where(mask, jnp.exp(jax.nn.log_sigmoid(z) + tail), 0.0)
        outs.append(jnp.einsum('bhqk,bhkd->bhqd', attn.astype(vb.dtype), vb))
    return jnp.concatenate(outs, axis=2)

def first_inputs(seed: int = 0) -> dict:
    key = jax.random.key(seed)
    ks = jax.random.split(key, 20)
    f32 = jnp.float32
    nrm = lambda k, shape, fan_in: jax.random.normal(k, shape, f32) * (fan_in ** -0.5)
    gain = lambda k, n: 1.0 + 0.02 * jax.random.normal(k, (n,), f32)
    return {
        "x": jax.random.normal(ks[0], (BATCH, SEQ, D_MODEL), f32),
        "g_pre_mix": gain(ks[1], D_MODEL),
        "w_in": nrm(ks[2], (D_MODEL, IN_WIDTH), D_MODEL),
        "w_pool_mix": nrm(ks[3], (N_POOL_GROUPS, POOL_GROUP, POOL_GROUP), POOL_GROUP),
        "pool_scale": gain(ks[4], POOL_WIDTH),
        "w_br_pool": nrm(ks[5], (POOL_WIDTH, D_MODEL), POOL_WIDTH),
        "w_br_sb": nrm(ks[6], (SB_WIDTH, D_MODEL), SB_WIDTH),
        "w_gate": nrm(ks[7], (D_MODEL, N_BRANCHES * D_MODEL), D_MODEL),
        "b_gate": 0.01 * jax.random.normal(ks[8], (N_BRANCHES * D_MODEL,), f32),
        "w_out": nrm(ks[9], (D_MODEL, D_MODEL), D_MODEL),
        "g_post_mix": gain(ks[10], D_MODEL),
        "g_pre_mlp": gain(ks[11], D_MODEL),
        "w_up": nrm(ks[12], (D_MODEL, D_FF), D_MODEL),
        "w_down": nrm(ks[13], (D_FF, D_MODEL), D_FF),
        "g_post_mlp": gain(ks[14], D_MODEL),
    }

def first_block(x, g_pre_mix, w_in, w_pool_mix, pool_scale, w_br_pool, w_br_sb,
              w_gate, b_gate, w_out, g_post_mix, g_pre_mlp, w_up, w_down, g_post_mlp):
    B, S, _ = x.shape
    for _layer in range(DEPTH):
        h = rmsnorm(x, g_pre_mix)
        proj = jnp.einsum('bsd,de->bse', h, w_in)
        u_pool = proj[..., :POOL_WIDTH]
        qkv = proj[..., POOL_WIDTH:].reshape(B, S, 3, SB_HEADS, SB_HEAD_DIM)
        q, k, v = (jnp.transpose(qkv[:, :, i], (0, 2, 1, 3)) for i in range(3))

        y_pool = jnp.einsum('bsc,cd->bsd', multiscale_pool(u_pool, w_pool_mix, pool_scale), w_br_pool)
        o_sb = stick_breaking_attention(q, k, v)
        o_sb = jnp.transpose(o_sb, (0, 2, 1, 3)).reshape(B, S, SB_WIDTH)
        y_sb = jnp.einsum('bsc,cd->bsd', o_sb, w_br_sb)

        gates = jax.nn.sigmoid(jnp.einsum('bsd,de->bse', h, w_gate) + b_gate)
        merged = gates[..., :D_MODEL] * y_pool + gates[..., D_MODEL:] * y_sb
        mix = jnp.einsum('bsd,de->bse', merged, w_out)
        x = x + rmsnorm(mix, g_post_mix)

        h2 = rmsnorm(x, g_pre_mlp)
        a = jnp.square(jax.nn.relu(jnp.einsum('bsd,df->bsf', h2, w_up)))
        ff = jnp.einsum('bsf,fd->bsd', a, w_down)
        x = x + rmsnorm(ff, g_post_mlp)
    return x


DEPTH_2 = 2

MIX_WIDTH = D_MODEL
MLA_HEADS = 8
MLA_NOPE_DIM = 64
MLA_ROPE_DIM = 32
MLA_V_DIM = 64
MLA_Q_LORA = 384
MLA_KV_LORA = 256
MLA_WIDTH = MLA_HEADS * MLA_V_DIM
ROPE_THETA = 10000.0
CONV_CH = MIX_WIDTH - MLA_WIDTH
CONV_GROUPS = 8
CONV_K = 31
IN_COLS = MLA_Q_LORA + MLA_KV_LORA + MLA_ROPE_DIM + 2 * CONV_CH
D_FF_2 = 2816
FFN_CONV_K = 3
EPS = 1e-6


def _rmsnorm(x, g):
    xf = x.astype(jnp.float32)
    y = xf * lax.rsqrt(jnp.mean(xf * xf, axis=-1, keepdims=True) + EPS)
    return (y * g.astype(jnp.float32)).astype(x.dtype)

def _layernorm(x, g, b):
    xf = x.astype(jnp.float32)
    mu = jnp.mean(xf, axis=-1, keepdims=True)
    var = jnp.mean(jnp.square(xf - mu), axis=-1, keepdims=True)
    y = (xf - mu) * lax.rsqrt(var + EPS)
    return (y * g.astype(jnp.float32) + b.astype(jnp.float32)).astype(x.dtype)

def _dwconv(x, w, b):
    k = w.shape[0]
    pad = k // 2
    y = lax.conv_general_dilated(
        x, w[:, None, :].astype(x.dtype), window_strides=(1,),
        padding=[(pad, pad)], dimension_numbers=("NWC", "WIO", "NWC"),
        feature_group_count=x.shape[-1])
    return y + b.astype(x.dtype)

def _rope_tables(positions):
    inv_freq = 1.0 / (ROPE_THETA ** (jnp.arange(0, MLA_ROPE_DIM, 2, dtype=jnp.float32) / MLA_ROPE_DIM))
    ang = positions.astype(jnp.float32)[..., None] * inv_freq
    return jnp.cos(ang), jnp.sin(ang)

def _apply_rope(t, cos, sin):
    half = t.shape[-1] // 2
    t1, t2 = t[..., :half], t[..., half:]
    cos = cos.astype(t.dtype)
    sin = sin.astype(t.dtype)
    return jnp.concatenate([t1 * cos - t2 * sin, t2 * cos + t1 * sin], axis=-1)

def _mla_attention(q_nope, q_rope, k_nope, k_rope, v):
    b, s, h, dn = q_nope.shape
    nb = s // Q_BLOCK
    scale = 1.0 / math.sqrt(dn + q_rope.shape[-1])

    def to_blocks(t):
        return jnp.moveaxis(t.reshape(b, nb, Q_BLOCK, *t.shape[2:]), 1, 0)

    def block(args):
        qn, qr = args
        sc = (jnp.einsum("bqhd,bkhd->bhqk", qn, k_nope)
              + jnp.einsum("bqhr,bkr->bhqk", qr, k_rope))
        p = jax.nn.softmax(sc.astype(jnp.float32) * scale, axis=-1).astype(v.dtype)
        return jnp.einsum("bhqk,bkhd->bqhd", p, v)

    o = lax.map(block, (to_blocks(q_nope), to_blocks(q_rope)))
    return jnp.moveaxis(o, 0, 1).reshape(b, s, h * v.shape[-1])

def second_inputs(seed: int = 0) -> dict:
    key = jax.random.key(seed)
    ks = jax.random.split(key, 24)
    f32 = jnp.float32

    def w(k, shape, fan_in, gain=1.0):
        return jax.random.normal(k, shape, f32) * (gain * fan_in ** -0.5)

    def gain(k, shape):
        return 1.0 + 0.02 * jax.random.normal(k, shape, f32)

    def bias(k, shape):
        return 0.02 * jax.random.normal(k, shape, f32)

    x = jax.random.normal(ks[0], (BATCH, SEQ, D_MODEL), f32)
    offs = jax.random.randint(ks[1], (BATCH, 1), 0, 4096, dtype=jnp.int32)
    positions = (jnp.arange(SEQ, dtype=jnp.int32)[None, :] + offs).astype(jnp.int32)
    return {
        "x": x,
        "positions": positions,
        "g_mix": gain(ks[2], (DEPTH_2, D_MODEL)),
        "w_in": w(ks[3], (DEPTH_2, D_MODEL, IN_COLS), D_MODEL),
        "g_q": gain(ks[4], (DEPTH_2, MLA_Q_LORA)),
        "w_uq": w(ks[5], (DEPTH_2, MLA_Q_LORA, MLA_HEADS * (MLA_NOPE_DIM + MLA_ROPE_DIM)), MLA_Q_LORA),
        "g_kv": gain(ks[6], (DEPTH_2, MLA_KV_LORA)),
        "w_ukv": w(ks[7], (DEPTH_2, MLA_KV_LORA, MLA_HEADS * (MLA_NOPE_DIM + MLA_V_DIM)), MLA_KV_LORA),
        "w_dw_conv": w(ks[8], (DEPTH_2, CONV_K, CONV_CH), CONV_K),
        "b_dw_conv": bias(ks[9], (DEPTH_2, CONV_CH)),
        "g_conv_ln": gain(ks[10], (DEPTH_2, CONV_CH)),
        "b_conv_ln": bias(ks[11], (DEPTH_2, CONV_CH)),
        "w_o": w(ks[12], (DEPTH_2, MIX_WIDTH, D_MODEL), MIX_WIDTH, 0.5),
        "g_ffn": gain(ks[13], (DEPTH_2, D_MODEL)),
        "w_up": w(ks[14], (DEPTH_2, D_MODEL, 2 * D_FF_2), D_MODEL),
        "w_dw_ffn": w(ks[15], (DEPTH_2, FFN_CONV_K, 2 * D_FF_2), FFN_CONV_K),
        "b_dw_ffn": bias(ks[16], (DEPTH_2, 2 * D_FF_2)),
        "w_down": w(ks[17], (DEPTH_2, D_FF_2, D_MODEL), D_FF_2, 0.5),
        "g_final": gain(ks[18], (D_MODEL,)),
    }

def second_block(x, positions, g_mix, w_in, g_q, w_uq, g_kv, w_ukv, w_dw_conv, b_dw_conv,
              g_conv_ln, b_conv_ln, w_o, g_ffn, w_up, w_dw_ffn, b_dw_ffn, w_down, g_final):
    b, s, _ = x.shape
    cos, sin = _rope_tables(positions)
    cos_h, sin_h = cos[:, :, None, :], sin[:, :, None, :]
    o1 = MLA_Q_LORA
    o2 = o1 + MLA_KV_LORA
    o3 = o2 + MLA_ROPE_DIM
    for l in range(DEPTH_2):
        h = _rmsnorm(x, g_mix[l])
        p = h @ w_in[l].astype(h.dtype)
        c_q = _rmsnorm(p[..., :o1], g_q[l])
        q = (c_q @ w_uq[l].astype(h.dtype)).reshape(b, s, MLA_HEADS, MLA_NOPE_DIM + MLA_ROPE_DIM)
        q_nope = q[..., :MLA_NOPE_DIM]
        q_rope = _apply_rope(q[..., MLA_NOPE_DIM:], cos_h, sin_h)
        c_kv = _rmsnorm(p[..., o1:o2], g_kv[l])
        kv = (c_kv @ w_ukv[l].astype(h.dtype)).reshape(b, s, MLA_HEADS, MLA_NOPE_DIM + MLA_V_DIM)
        k_nope = kv[..., :MLA_NOPE_DIM]
        v = kv[..., MLA_NOPE_DIM:]
        k_rope = _apply_rope(p[..., o2:o3], cos, sin)
        y_attn = _mla_attention(q_nope, q_rope, k_nope, k_rope, v)
        a, gt = jnp.split(p[..., o3:], 2, axis=-1)
        u = a * jax.nn.sigmoid(gt)
        u = _dwconv(u, w_dw_conv[l], b_dw_conv[l])
        u = jax.nn.silu(_layernorm(u, g_conv_ln[l], b_conv_ln[l]))
        y = jnp.concatenate([y_attn, u], axis=-1) @ w_o[l].astype(h.dtype)
        x = x + y
        h2 = _rmsnorm(x, g_ffn[l])
        z = _dwconv(h2 @ w_up[l].astype(h2.dtype), w_dw_ffn[l], b_dw_ffn[l])
        zg, zv = jnp.split(z, 2, axis=-1)
        x = x + (jax.nn.silu(zg) * zv) @ w_down[l].astype(h2.dtype)
    return _rmsnorm(x, g_final)


def setup_inputs(seed=0):
    out = dict(first_inputs(seed))
    for name, value in second_inputs(seed + 1).items():
        if name != "x":
            out[name + "_2"] = value
    return out


def reference(
    x, g_pre_mix, w_in, w_pool_mix, pool_scale, w_br_pool, w_br_sb, w_gate, b_gate, w_out,
    g_post_mix, g_pre_mlp, w_up, w_down, g_post_mlp, positions_2, g_mix_2, w_in_2, g_q_2,
    w_uq_2, g_kv_2, w_ukv_2, w_dw_conv_2, b_dw_conv_2, g_conv_ln_2, b_conv_ln_2, w_o_2, g_ffn_2,
    w_up_2, w_dw_ffn_2, b_dw_ffn_2, w_down_2, g_final_2,
):
    x = first_block(
        x, g_pre_mix, w_in, w_pool_mix, pool_scale, w_br_pool, w_br_sb, w_gate, b_gate, w_out,
        g_post_mix, g_pre_mlp, w_up, w_down, g_post_mlp,
    )
    return second_block(
        x, positions_2, g_mix_2, w_in_2, g_q_2, w_uq_2, g_kv_2, w_ukv_2, w_dw_conv_2,
        b_dw_conv_2, g_conv_ln_2, b_conv_ln_2, w_o_2, g_ffn_2, w_up_2, w_dw_ffn_2, b_dw_ffn_2,
        w_down_2, g_final_2,
    )


_drawn_inputs = setup_inputs


def setup_inputs(seed=0):
    import zlib

    import numpy as np

    out = dict(_drawn_inputs(seed))
    spreads = {}
    factors = {'g_pre_mix': 2.958,
     'pool_scale': 4.649,
     'b_gate': 8.0,
     'g_post_mix': 3.762,
     'g_pre_mlp': 4.089,
     'g_post_mlp': 4.772,
     'g_mix_2': 8.0,
     'g_q_2': 8.0,
     'g_kv_2': 8.0,
     'b_dw_conv_2': 7.993,
     'g_conv_ln_2': 32.679,
     'b_conv_ln_2': 29.356,
     'g_ffn_2': 7.875,
     'b_dw_ffn_2': 8.0,
     'g_final_2': 7.784}
    for name, (base, spread) in spreads.items():
        noise = np.random.default_rng([zlib.crc32(name.encode()), seed]).standard_normal(out[name].shape)
        drawn = base * np.exp(spread * noise) if base else spread * noise
        out[name] = __import__('jax').numpy.asarray(drawn.astype(out[name].dtype))
    for name, factor in factors.items():
        out[name] = (out[name] * factor).astype(out[name].dtype)
    return out
```

```python
from contextlib import ExitStack

import concourse.bass as bass
from concourse import mybir

P = 128
D = 1024
S = 512
KT = D // P
TT = S // P
EPS = 1e-6
SLOTS = 4
CW = 512

HALF = D // 2
HT = HALF // P
HEAD = 64
PAIRS = HALF // (2 * HEAD)
WINDOWS = (2, 4, 8, 16)
LEFT = 16
FF1 = 4096
F1T = FF1 // P
F1G = FF1 // CW
Q_SCALE = HEAD ** -0.5

DEPTH2 = 2
QL, KVL, RD = 384, 256, 32
QT, KVT = QL // P, KVL // P
ND = 64
MLA_SCALE = (ND + RD) ** -0.5
CONV_K = 31
HALO = CONV_K // 2
FF2 = 2816
F2T = FF2 // P
F2G = FF2 // 256

F32 = mybir.dt.float32
F32R = mybir.dt.float32r
I32 = mybir.dt.int32
ALU = mybir.AluOpType
ACT = mybir.ActivationFunctionType
AX_X = mybir.AxisListType.X
LN_EXP = "natural_log_exp_and_others"
BIG = 3.0e38

C_PRE, C_PSC, C_BG, C_POST, C_PMLP, C_QMLP, C_FIN = 0, 8, 12, 28, 36, 44, 52
N_ROWS1 = 60
L_MIX, L_GQ, L_GKV, L_BDW, L_GLN, L_BLN, L_FFN, L_BFF = 0, 8, 11, 13, 17, 21, 25, 33
N_ROWS2 = 77
L_TAP, L_FTAP = 128, 256
N_COLS2 = L_FTAP + 3 * 2 * F2T

N_PAIR = 0
N_SB0 = N_PAIR + PAIRS * 2 * KT
N_MIX = N_SB0 + HT
N_PB0 = N_MIX + 1
N_SB1 = N_PB0 + HT
N_PB1 = N_SB1 + HT
N_OUT = N_PB1 + HT
N_UP = N_OUT + 2 * KT
N_DOWN = N_UP + F1G * KT
N_END1 = N_DOWN + 2 * F1T
M_KV = 0
M_Q = M_KV + KT
M_A = M_Q + KT
M_G = M_A + KT
M_PAIR = M_G + KT
M_WO = M_PAIR + PAIRS * SLOTS
M_UP = M_WO + 2 * KT
M_DOWN = M_UP + F2G * KT
M_END = M_DOWN + 2 * F2T

KV_COLS = KVL + 2 * RD


def pieces2(n):
    if n < M_Q:
        return 3
    if M_PAIR <= n < M_WO + SLOTS and (n - M_PAIR) % SLOTS < QT:
        return 3
    return 1


def width2(n):
    if n < M_Q:
        return KV_COLS
    if n < M_A:
        return QL
    return CW


def landed2(n):
    return 16 * sum(pieces2(m) for m in range(n % SLOTS, n + 1, SLOTS))


def two_blocks(nc, x, g_pre_mix, w_in, w_pool_mix, pool_scale, w_br_pool, w_br_sb, w_gate, b_gate,
               w_out, g_post_mix, g_pre_mlp, w_up, w_down, g_post_mlp, positions, g_mix, w_in2,
               g_q, w_uq, g_kv, w_ukv, w_dw_conv, b_dw_conv, g_conv_ln, b_conv_ln, w_o, g_ffn,
               w_up2, w_dw_ffn, b_dw_ffn, w_down2, g_final, shape_consts, out):
    with ExitStack() as ctx:
        def sb(name, shape, dt=F32):
            return ctx.enter_context(nc.sbuf_tensor(name, shape, dt))

        sems = []

        def sem(name):
            s = ctx.enter_context(nc.semaphore(name))
            sems.append(s)
            return s

        x_v = x.rearrange("b (t p) d -> p (b t) d", p=P)
        out_v = out.rearrange("b (t p) d -> p (b t) d", p=P)
        in_v = w_in.rearrange("(k p) (b i n) -> p k b i n", p=P, b=4, n=P)
        gate_v = w_gate.rearrange("(k p) (i n) -> p k i n", p=P, n=CW)
        sb_v = w_br_sb.rearrange("(k p) (h n) -> p k h n", p=P, n=CW)
        pb_v = w_br_pool.rearrange("(k p) (h n) -> p k h n", p=P, n=CW)
        mix_v = w_pool_mix.rearrange("g c d -> c g d")
        out_w_v = w_out.rearrange("(k p) (h n) -> p k h n", p=P, n=CW)
        up_v = w_up.rearrange("(k p) (g n) -> p k g n", p=P, n=CW)
        down_v = w_down.rearrange("(k p) (h n) -> p k h n", p=P, n=CW)
        in2_v = w_in2.rearrange("l (k p) c -> l p k c", p=P)
        uq_v = w_uq.rearrange("l (k p) (i h c) -> l p k i h c", p=P, h=2, c=ND + RD)
        ukv_v = w_ukv.rearrange("l (k p) (i n) -> l p k i n", p=P, n=4 * ND)
        wo_v = w_o.rearrange("l (k p) (h n) -> l p k h n", p=P, n=CW)
        up2_v = w_up2.rearrange("l (k p) (v g n) -> l p k v g n", p=P, v=2, n=256)
        down2_v = w_down2.rearrange("l (k p) (h n) -> l p k h n", p=P, n=CW)

        x_t = sb("x_t", [P, KT, S])
        h_hi = sb("h_hi", [P, KT, S], F32R)
        h_lo = sb("h_lo", [P, KT, S], F32R)
        w_raw = sb("w_raw", [P, SLOTS, CW])
        w_hi = sb("w_hi", [P, SLOTS, CW], F32R)
        w_lo = sb("w_lo", [P, SLOTS, CW], F32R)
        arena = sb("arena", [P, 32, S])
        split = sb("split", [P, 20, S], F32R)
        ident = sb("ident", [P, P])
        ones = sb("ones", [P, P])
        tri = sb("tri", [P, 2, P], F32R)
        later = sb("later", [P, P])
        rows1 = sb("rows1", [N_ROWS1, P])
        cols1 = sb("cols1", [P, N_ROWS1])
        rows2 = sb("rows2", [N_ROWS2, P])
        rows_tap = sb("rows_tap", [CONV_K, HALF])
        rows_ftap = sb("rows_ftap", [2 * F2T, 3, P])
        cols2 = sb("cols2", [P, N_COLS2])
        consts = sb("consts", [P, 4 + LEFT])
        trig = sb("trig", [P, S])
        sq = sb("sq", [P, 4, S])
        tri_f = sq[:, 3, 0:2 * P].rearrange("p (a n) -> p a n", a=2)
        ssum = sb("ssum", [P, S])
        var = sb("var", [P, S])
        rs0 = sb("rs0", [P, S])
        rs1 = sb("rs1", [P, S])
        rstd = sb("rstd", [P, 2, S])
        soft = sb("soft", [P, 4, 4])

        x_in = arena[:, 0:8, :].rearrange("p (t a) n -> p t (a n)", t=TT)
        pos_i = arena[:, 8, :].bitcast(I32)
        ang, turns, pos_f = arena[:, 9, :], arena[:, 10, :], arena[:, 11, :]
        hf = arena[:, 12:14, :]
        arena_flat = arena[:, :, :].rearrange("p a n -> p (a n)")
        u_pad = arena_flat[:, 0:HT * (LEFT + S)].rearrange("p (g n) -> p g n", g=HT)
        gates = arena[:, 5:21, :]
        o_f = arena[:, 21:25, :]
        la = arena[:, 25:27, :]
        sp = arena[:, 27:29, :]
        at = arena[:, 29:31, :]
        wsum = arena_flat[:, 25 * S:25 * S + 2 * (LEFT + S)].rearrange("p (a n) -> p a n", a=2)
        pooled = arena[:, 28:30, :]
        head16 = arena[:, 30, 0:LEFT]
        t_sb = arena[:, 21:25, :]
        t_pb = arena[:, 25:27, :]
        merged = arena[:, 27:29, :]
        mixg = arena[:, 0:8, :]
        xinc = arena[:, 8:10, :]
        act1 = arena
        relu = sq

        q_hi, q_lo, k_hi, k_lo, v_hi, v_lo = (split[:, n, :] for n in range(6))
        l_hi = split[:, 6:11, :].rearrange("p a n -> p (a n)").rearrange("p (h n) -> p h n", h=2)
        l_lo = split[:, 11:16, :].rearrange("p a n -> p (a n)").rearrange("p (h n) -> p h n", h=2)
        at_hi, at_lo = split[:, 16:18, :], split[:, 18:20, :]
        o_hi, o_lo = split[:, 6:10, :], split[:, 10:14, :]
        pool_hi, pool_lo = split[:, 0:4, :], split[:, 14:18, :]
        as_hi, as_lo = split[:, 0:2, :], split[:, 2:4, :]

        ckv_f = arena[:, 0:2, :]
        cq_f = arena[:, 2:5, :]
        af = arena[:, 5:9, :]
        gf = arena[:, 9:13, :]
        o2_f = arena[:, 9:13, :]
        CPAD = S + 2 * HALO
        upad = arena_flat[:, 13 * S:13 * S + 4 * CPAD].rearrange("p (j n) -> p j n", j=4)
        conv = arena[:, 18:22, :]
        conv_odd = arena[:, 22, :]
        prob = arena[:, 23:27, :]
        qf = arena[:, 27:29, :]
        rot = arena[:, 29:31, :]
        krf = arena[:, 31, :]
        un = arena[:, 0:4, :]
        kq_hi = split[:, 0:2, :]
        kq_lo = split[:, 2:4, :]
        kk_hi = split[:, 4:6, :]
        kk_lo = split[:, 6:8, :]
        vv_hi, vv_lo = split[:, 8, :], split[:, 9, :]
        pt_hi, pt_lo = split[:, 10:14, :], split[:, 14:18, :]
        act2 = arena
        ZPAD = S + 2
        zp = arena_flat[:, 22 * S:22 * S + 4 * ZPAD].rearrange("p (j n) -> p j n", j=4)
        cz = arena[:, 27:31, :]
        yfin = arena[:, 0:8, :]
        y_out = arena[:, 8:16, :].rearrange("p (t a) n -> p t (a n)", t=TT)

        bank_a = ctx.enter_context(nc.psum_tensor("bank_a", [P, 4, S], F32))
        bank_b = ctx.enter_context(nc.psum_tensor("bank_b", [P, 4, S], F32))
        sets = (bank_a, bank_b)

        x_land = [ctx.enter_context(nc.semaphore(f"x_land{t}")) for t in range(TT)]
        rows1_land = ctx.enter_context(nc.semaphore("rows1_land"))
        rows2_land = ctx.enter_context(nc.semaphore("rows2_land"))
        pos_land = ctx.enter_context(nc.semaphore("pos_land"))
        consts_made = ctx.enter_context(nc.semaphore("consts_made"))
        tri_made = ctx.enter_context(nc.semaphore("tri_made"))
        trig_step = ctx.enter_context(nc.semaphore("trig_step"))
        trig_sin = ctx.enter_context(nc.semaphore("trig_sin"))
        seg_done = ctx.enter_context(nc.semaphore("seg_done"))
        seg_quiet = ctx.enter_context(nc.semaphore("seg_quiet"))
        seg_open = ctx.enter_context(nc.semaphore("seg_open"))
        y_stored = ctx.enter_context(nc.semaphore("y_stored"))

        w_land = [sem(f"w_land{s}") for s in range(SLOTS)]
        w_round = sem("w_round")
        w_split = sem("w_split")
        w_used = sem("w_used")
        xt_made = sem("xt_made")
        xt_out = sem("xt_out")
        xt_out_b = sem("xt_out_b")
        cols_made = sem("cols_made")
        cols_out = sem("cols_out")
        sq_ready = sem("sq_ready")
        sq_added = sem("sq_added")
        stat_ready = sem("stat_ready")
        var_ready = sem("var_ready")
        ln_ready = sem("ln_ready")
        guess_ready = sem("guess_ready")
        newton = sem("newton")
        rstd_ready = sem("rstd_ready")
        hf_ready = sem("hf_ready")
        h_round = sem("h_round")
        h_ready = sem("h_ready")
        stage_round = sem("stage_round")
        stage_ready = sem("stage_ready")
        u_out = sem("u_out")
        z_ready = sem("z_ready")
        soft_step = sem("soft_step")
        soft_ready = sem("soft_ready")
        sp_step = sem("sp_step")
        l_round = sem("l_round")
        l_ready = sem("l_ready")
        c_ready = sem("c_ready")
        attn_exp = sem("attn_exp")
        attn_masked = sem("attn_masked")
        attn_round = sem("attn_round")
        attn_ready = sem("attn_ready")
        av_done = sem("av_done")
        o_out = sem("o_out")
        gate_out = sem("gate_out")
        gate_ready = sem("gate_ready")
        o_round = sem("o_round")
        o_split = sem("o_split")
        pool_step = sem("pool_step")
        pool_ready = sem("pool_ready")
        pool_round = sem("pool_round")
        pool_split = sem("pool_split")
        y_round = sem("y_round")
        y_ready = sem("y_ready")
        sb_out = sem("sb_out")
        pb_out = sem("pb_out")
        merge_ready = sem("merge_ready")
        merge_round = sem("merge_round")
        merge_split = sem("merge_split")
        mix_out = sem("mix_out")
        xinc_ready = sem("xinc_ready")
        x_new = sem("x_new")
        xg_round = sem("xg_round")
        xg_ready = sem("xg_ready")
        r2_ready = sem("r2_ready")
        relu_out = sem("relu_out")
        relu_sq = sem("relu_sq")
        a_ready = sem("a_ready")
        as_round = sem("as_round")
        as_ready = sem("as_ready")

        proj_out = sem("proj_out")
        cn_ready = sem("cn_ready")
        kr_step = sem("kr_step")
        kr_round = sem("kr_round")
        kr_ready = sem("kr_ready")
        glu_sig = sem("glu_sig")
        u_ready = sem("u_ready")
        pad_zero = sem("pad_zero")
        lat_round = sem("lat_round")
        lat_ready = sem("lat_ready")
        q_made = sem("q_made")
        kv_made = sem("kv_made")
        qn_out = sem("qn_out")
        qr_step = sem("qr_step")
        qk_round = sem("qk_round")
        qk_ready = sem("qk_ready")
        s_ready = sem("s_ready")
        mx_step = sem("mx_step")
        p_exp = sem("p_exp")
        p_step = sem("p_step")
        p_ready = sem("p_ready")
        pt_made = sem("pt_made")
        pt_round = sem("pt_round")
        pt_ready = sem("pt_ready")
        pv_done = sem("pv_done")
        o2_out = sem("o2_out")
        tap_done = sem("tap_done")
        conv_ready = sem("conv_ready")
        mean_ready = sem("mean_ready")
        dev_ready = sem("dev_ready")
        ln_out = sem("ln_out")
        silu_ready = sem("silu_ready")
        cu_round = sem("cu_round")
        cu_ready = sem("cu_ready")
        zp_zero = sem("zp_zero")
        z_out = sem("z_out")
        z_mid = sem("z_mid")
        z_tap = sem("z_tap")
        z_conv = sem("z_conv")
        z_silu = sem("z_silu")
        y_made = sem("y_made")
        yt_made = sem("yt_made")
        yt_out = sem("yt_out")
        yt_out_b = sem("yt_out_b")

        block = ctx.enter_context(nc.Block())

        def meet(eng, number):
            eng.drain().then_inc(seg_done, 1)
            eng.wait_ge(seg_open, number + 1)

        @block.sync
        def _(sp_):
            def load1(n, src, i=0, per=0):
                dst = w_raw[:, n % SLOTS, :]
                if len(src.shape) == 3:
                    dst = dst.rearrange("p (a b) -> p a b", a=src.shape[1])
                if n >= SLOTS:
                    sp_.wait_ge(w_split, i * per + (n - SLOTS + 1))
                sp_.dma_start(dst, src).then_inc(w_land[n % SLOTS], 16)

            for t in range(TT):
                sp_.dma_start(x_in[:, t, :], x_v[:, t, :]).then_inc(x_land[t], 16)
            for k in range(SLOTS):
                sp_.dma_start(w_raw[:, k, :].rearrange("p (b n) -> p b n", b=4),
                              in_v[:, k, :, 0, :]).then_inc(w_land[k], 16)
            at_row = 0
            for vec in (g_pre_mix, pool_scale, b_gate, g_post_mix, g_pre_mlp, g_post_mlp, g_final):
                rows = vec.shape[0] // P
                sp_.dma_start(rows1[at_row:at_row + rows, :],
                              vec.rearrange("(r p) -> r p", p=P)).then_inc(rows1_land, 16)
                at_row += rows
            sp_.dma_start(consts[:, :], shape_consts).then_inc(pos_land, 16)
            sp_.dma_start(pos_i, positions.broadcast_to((P, S))).then_inc(pos_land, 16)

            def load_rows2(layer):
                r = 0
                for vec in (g_mix, g_q, g_kv, b_dw_conv, g_conv_ln, b_conv_ln, g_ffn, b_dw_ffn):
                    rows = vec.shape[1] // P
                    sp_.dma_start(rows2[r:r + rows, :],
                                  vec[layer].rearrange("(r p) -> r p", p=P)).then_inc(rows2_land, 16)
                    r += rows
                sp_.dma_start(rows_tap[:, :], w_dw_conv[layer]).then_inc(rows2_land, 16)
                sp_.dma_start(rows_ftap[:, :, :],
                              w_dw_ffn[layer].rearrange("k (t p) -> t k p", p=P)).then_inc(rows2_land, 16)

            load_rows2(0)
            for k in range(SLOTS, KT):
                load1(N_PAIR + k, in_v[:, k, :, 0, :])
            for k in range(KT):
                load1(N_PAIR + KT + k, gate_v[:, k, 0, :])
            with sp_.Fori(1, PAIRS) as i:
                for k in range(KT):
                    sp_.wait_ge(w_split, i * (2 * KT) + (k - SLOTS + 1))
                    sp_.dma_start(w_raw[:, k % SLOTS, :].rearrange("p (b n) -> p b n", b=4),
                                  in_v[:, k, :, i, :]).then_inc(w_land[k % SLOTS], 16)
                for k in range(KT):
                    sp_.wait_ge(w_split, i * (2 * KT) + (KT + k - SLOTS + 1))
                    sp_.dma_start(w_raw[:, k % SLOTS, :], gate_v[:, k, i, :]).then_inc(w_land[k % SLOTS], 16)
            for k in range(HT):
                load1(N_SB0 + k, sb_v[:, k, 0, :])
            load1(N_MIX, mix_v)
            for k in range(HT):
                load1(N_PB0 + k, pb_v[:, k, 0, :])
            for k in range(HT):
                load1(N_SB1 + k, sb_v[:, k, 1, :])
            for k in range(HT):
                load1(N_PB1 + k, pb_v[:, k, 1, :])
            for half in range(2):
                for k in range(KT):
                    load1(N_OUT + half * KT + k, out_w_v[:, k, half, :])
            with sp_.Fori(0, F1G) as g:
                for k in range(KT):
                    load1(N_UP + k, up_v[:, k, g, :], g, KT)
            with sp_.Fori(0, F1T // 2) as kk:
                for k in range(2):
                    for half in range(2):
                        load1(N_DOWN + 2 * k + half,
                              down_v.rearrange("p (kk two) h n -> p kk two h n", two=2)[:, kk, k, half, :],
                              kk, 4)

            def clear(number):
                sp_.wait_ge(seg_done, number * 4 + 4)
                sp_.sem_inc(seg_quiet, 1)
                for s in sems:
                    sp_.sem_clear(s)
                sp_.sem_inc(seg_open, 1)

            clear(0)

            with sp_.Fori(0, DEPTH2) as l:
                def load2(n, parts, i=0, per=0):
                    if n >= SLOTS:
                        sp_.wait_ge(w_split, i * per + (n - SLOTS + 1))
                    for dst, src in parts:
                        sp_.dma_start(dst, src).then_inc(w_land[n % SLOTS], 16)

                for k in range(KT):
                    n = M_KV + k
                    slot = w_raw[:, n % SLOTS, :]
                    r0 = QL + KVL
                    load2(n, [(slot[:, 0:KVL + RD], in2_v[l, :, k, QL:r0 + RD]),
                              (slot[:, KVL + RD:KVL + RD + RD // 2], in2_v[l, :, k, r0 + RD // 2:r0 + RD]),
                              (slot[:, KVL + RD + RD // 2:KV_COLS], in2_v[l, :, k, r0:r0 + RD // 2])])
                for k in range(KT):
                    n = M_Q + k
                    load2(n, [(w_raw[:, n % SLOTS, 0:QL], in2_v[l, :, k, 0:QL])])
                for part in range(2):
                    c0 = QL + KVL + RD + part * CW
                    for k in range(KT):
                        n = M_A + part * KT + k
                        load2(n, [(w_raw[:, n % SLOTS, :], in2_v[l, :, k, c0:c0 + CW])])
                with sp_.Fori(0, PAIRS) as i:
                    for k in range(QT):
                        n = M_PAIR + k
                        slot = w_raw[:, n % SLOTS, 0:2 * P].rearrange("p (h c) -> p h c", h=2)
                        load2(n, [(slot[:, :, 0:ND + RD], uq_v[l, :, k, i, :, :]),
                                  (slot[:, :, ND + RD:ND + RD + RD // 2], uq_v[l, :, k, i, :, ND + RD // 2:ND + RD]),
                                  (slot[:, :, ND + RD + RD // 2:P], uq_v[l, :, k, i, :, ND:ND + RD // 2])],
                              i, SLOTS)
                    n = M_PAIR + QT
                    load2(n, [(w_raw[:, n % SLOTS, :].rearrange("p (k c) -> p k c", k=KVT), ukv_v[l, :, :, i, :])],
                          i, SLOTS)
                for half in range(2):
                    for k in range(KT):
                        n = M_WO + half * KT + k
                        cuts = (0, 256, 384, CW) if pieces2(n) == 3 else (0, CW)
                        load2(n, [(w_raw[:, n % SLOTS, a:b], wo_v[l, :, k, half, a:b])
                                  for a, b in zip(cuts, cuts[1:])])
                with sp_.Fori(0, F2G) as g:
                    for k in range(KT):
                        n = M_UP + k
                        load2(n, [(w_raw[:, n % SLOTS, :].rearrange("p (v c) -> p v c", v=2), up2_v[l, :, k, :, g, :])],
                              g, KT)
                d2 = down2_v.rearrange("l p (kk two) h n -> l p kk two h n", two=2)
                with sp_.Fori(0, F2T // 2) as kk:
                    for k in range(2):
                        for half in range(2):
                            n = M_DOWN + 2 * k + half
                            load2(n, [(w_raw[:, n % SLOTS, :], d2[l, :, kk, k, half, :])], kk, 4)
                sp_.wait_ge(cols_out, 3)
                load_rows2(1 - l)
                clear(l + 1)

            for t in range(TT):
                sp_.wait_ge(yt_out, t + 1)
                sp_.wait_ge(yt_out_b, t + 1)
                sp_.dma_start(out_v[:, t, :], y_out[:, t, :]).then_inc(y_stored, 16)
            sp_.wait_ge(rows2_land, 16 * 10 * (DEPTH2 + 1))
            sp_.wait_ge(y_stored, 16 * TT)

        @block.gpsimd
        def _(pool):
            steps = 0

            def made(ins):
                nonlocal steps
                steps += 1
                ins.then_inc(consts_made, 1)
                pool.wait_ge(consts_made, steps)

            made(nc.gpsimd.memset(ident[:, :], 0.0))
            made(nc.gpsimd.affine_select(out=ident[:, :], in_=ident[:, :], compare_op=ALU.not_equal, fill=1.0,
                                         base=0, pattern=[[-1, P]], channel_multiplier=1))
            made(nc.gpsimd.memset(ones[:, :], 1.0))
            made(nc.gpsimd.memset(tri_f, -1.0))
            made(nc.gpsimd.affine_select(out=tri_f[:, 0, :], in_=tri_f[:, 0, :], compare_op=ALU.is_ge, fill=0.0,
                                         base=0, pattern=[[-1, P]], channel_multiplier=1))
            made(nc.gpsimd.memset(later[:, :], 1.0))
            made(nc.gpsimd.affine_select(out=later[:, :], in_=later[:, :], compare_op=ALU.is_gt, fill=0.0,
                                         base=0, pattern=[[1, P]], channel_multiplier=-1))

            def add_squares(count, before_sq, before_add, before_stat):
                for t in range(1, count):
                    pool.wait_ge(sq_ready, before_sq + t + 1)
                    if t == 1 and before_stat:
                        pool.wait_ge(stat_ready, before_stat)
                    if t > 1:
                        pool.wait_ge(sq_added, before_add + t - 1)
                    nc.gpsimd.tensor_tensor(ssum[:, :], sq[:, 0, :] if t == 1 else ssum[:, :], sq[:, t % 4, :],
                                            ALU.add).then_inc(sq_added, 1)

            add_squares(KT, 2 * KT, 2 * (KT - 1), 2)
            meet(pool, 0)
            with pool.Fori(0, DEPTH2) as l:
                add_squares(KT, 0, 0, 0)
                add_squares(KVT, KT, KT - 1, 1)
                add_squares(QT, KT + KVT, KT + KVT - 2, 2)
                add_squares(KT, KT + KVT + QT + HT, KT + KVT + QT + HT - 4, 4)
                meet(pool, l + 1)

        @block.scalar
        def _(act):
            def split1(n, i=0, per=0):
                s = n % SLOTS
                act.wait_ge(w_land[s], i * (16 * per // SLOTS) + 16 * (n // SLOTS + 1))
                if n >= SLOTS:
                    act.wait_ge(w_used, i * per + (n - SLOTS + 1))
                nc.scalar.activation(w_hi[:, s, :], w_raw[:, s, :], ACT.Copy).then_inc(w_round, 1)

            def rsqrt_guess(number):
                act.wait_ge(var_ready, number)
                nc.scalar.activation(rs0[:, :], var[:, :], ACT.Ln).then_inc(ln_ready, 1)
                act.wait_ge(ln_ready, number)
                nc.scalar.activation(rs1[:, :], rs0[:, :], ACT.Exp, scale=-0.5).then_inc(guess_ready, 1)

            def square(src, t, before_sq, before_add):
                if t >= 4:
                    act.wait_ge(sq_added, before_add + max(t - 4, 1))
                nc.scalar.activation(sq[:, t % 4, :], src, ACT.Square).then_inc(sq_ready, 1)

            act.wait_ge(trig_step, 10)
            nc.scalar.activation(trig[:, :], ang, ACT.Sin).then_inc(trig_sin, 1)
            act.wait_ge(consts_made, 5)
            nc.scalar.activation(tri[:, :, :], tri_f, ACT.Copy).then_inc(tri_made, 1)
            nc.scalar.preload_act_table_set(LN_EXP)
            for n in range(SLOTS):
                split1(n)
            act.wait_ge(xt_made, 1)
            for f in range(4):
                nc.scalar.activation(x_t[:, f, :], bank_a[:, f, :], ACT.Copy).then_inc(xt_out, 1)
            for f in range(KT):
                if f < 4:
                    act.wait_ge(xt_out, f + 1)
                else:
                    act.wait_ge(xt_out_b, f - 3)
                square(x_t[:, f, :], f, 0, 0)
            rsqrt_guess(1)
            for f in range(KT):
                act.wait_ge(hf_ready, f + 1)
                nc.scalar.activation(h_hi[:, f, :], hf[:, f % 2, :], ACT.Copy).then_inc(h_round, 1)

            with act.Fori(0, PAIRS) as i:
                for k in range(KT):
                    split1(N_PAIR + SLOTS + k, i, 2 * KT)
                act.wait_ge(w_used, i * (2 * KT) + KT)
                nc.scalar.activation(q_hi, bank_a[:, 1, :], ACT.Copy, scale=Q_SCALE).then_inc(stage_round, 1)
                nc.scalar.activation(k_hi, bank_a[:, 2, :], ACT.Copy).then_inc(stage_round, 1)
                nc.scalar.activation(v_hi, bank_a[:, 3, :], ACT.Copy).then_inc(stage_round, 1)
                nc.scalar.activation(u_pad[:, i, LEFT:LEFT + S], bank_a[:, 0, :], ACT.Copy).then_inc(u_out, 1)
                for s in range(9):
                    if s < 8:
                        split1(N_PAIR + SLOTS + KT + s, i, 2 * KT)
                        kb = 3 - s % 4
                        n = S - P * kb
                        z = bank_a[:, s % 2, 0:n]
                        act.wait_ge(z_ready, i * 8 + (s + 1))
                        nc.scalar.activation(la[:, s % 2, 0:n], z, ACT.Abs).then_inc(soft_step, 1)
                        act.wait_ge(soft_step, i * 16 + (2 * s + 1))
                        nc.scalar.activation(la[:, s % 2, 0:n], la[:, s % 2, 0:n], ACT.Exp, scale=-1.0).then_inc(soft_step, 1)
                        act.wait_ge(soft_step, i * 16 + (2 * s + 2))
                        nc.scalar.activation(la[:, s % 2, 0:n], la[:, s % 2, 0:n], ACT.Ln, bias=1.0).then_inc(soft_ready, 1)
                    if s >= 1:
                        kb1 = 3 - (s - 1) % 4
                        n1 = S - P * kb1
                        act.wait_ge(c_ready, i * 8 + s)
                        nc.scalar.activation(at[:, (s - 1) % 2, 0:n1], bank_a[:, (s - 1) % 2, 0:n1], ACT.Exp).then_inc(attn_exp, 1)
                    if s < 8:
                        act.wait_ge(sp_step, i * 16 + (2 * s + 2))
                        off = (3 - kb) * (4 - kb) // 2 * P
                        nc.scalar.activation(l_hi[:, s // 4, off:off + n], sp[:, s % 2, 0:n], ACT.Copy).then_inc(l_round, 1)
                    if s >= 1:
                        act.wait_ge(attn_masked, i * 8 + s)
                        if s >= 3:
                            act.wait_ge(av_done, i * 8 + (s - 2))
                        nc.scalar.activation(at_hi[:, (s - 1) % 2, 0:n1], at[:, (s - 1) % 2, 0:n1], ACT.Copy).then_inc(attn_round, 1)
                    if s == 5 or s == 8:
                        hd = 0 if s == 5 else 1
                        rows = slice(HEAD * hd, HEAD * hd + HEAD)
                        act.wait_ge(av_done, i * 8 + 4 * (hd + 1))
                        nc.scalar.activation(o_f[rows, i, :], bank_a[rows, 2 + hd, :], ACT.Copy).then_inc(o_out, 1)
                act.wait_ge(w_used, i * (2 * KT) + 2 * KT)
                for j in range(4):
                    nc.scalar.activation(gates[:, i * 4 + j, :], bank_b[:, j, :], ACT.Identity,
                                         bias=cols1[:, bass.ds(i * 4 + (C_BG + j), 1)]).then_inc(gate_out, 1)

            act.wait_ge(o_out, 2 * PAIRS)
            for t in range(HT):
                nc.scalar.activation(o_hi[:, t, :], o_f[:, t, :], ACT.Copy).then_inc(o_round, 1)
            act.wait_ge(gate_out, 16)

            def sigmoid_gates(q):
                nc.scalar.activation(gates[:, 4 * q:4 * q + 4, :], gates[:, 4 * q:4 * q + 4, :],
                                     ACT.Sigmoid).then_inc(gate_ready, 1)

            def pool_hi_of(g):
                act.wait_ge(pool_ready, g + 1)
                nc.scalar.activation(pool_hi[:, g, :], pooled[:, g % 2, :], ACT.Copy).then_inc(pool_round, 1)

            sigmoid_gates(2)
            split1(N_MIX)
            pool_hi_of(0)
            pool_hi_of(1)
            split1(N_PB0)
            pool_hi_of(2)
            split1(N_PB0 + 1)
            pool_hi_of(3)
            split1(N_PB0 + 2)
            sigmoid_gates(0)
            split1(N_PB0 + 3)
            act.wait_ge(w_used, N_MIX + 1)
            for g in range(HT):
                nc.scalar.activation(h_hi[:, HT + g, :], bank_b[:, g, :], ACT.Copy,
                                     scale=cols1[:, C_PSC + g:C_PSC + g + 1]).then_inc(y_round, 1)
            sigmoid_gates(3)
            sigmoid_gates(1)

            def merge_hi(half):
                for j in range(4):
                    act.wait_ge(merge_ready, 4 * half + j + 1)
                    nc.scalar.activation(h_hi[:, 4 * half + j, :], merged[:, j % 2, :], ACT.Copy).then_inc(merge_round, 1)

            for k in range(HT):
                split1(N_SB1 + k)
            merge_hi(0)
            for k in range(HT):
                split1(N_PB1 + k)
            for k in range(HT):
                split1(N_OUT + k)
            act.wait_ge(w_used, N_PB1 + HT)
            merge_hi(1)
            for k in range(N_OUT + SLOTS, N_OUT + KT + SLOTS):
                split1(k)
            nc.scalar.preload_act_table_set(LN_EXP)

            def post_squares(last_chunk, tiles, before_sq, before_add):
                act.wait_ge(w_used, last_chunk + 1)
                for f in tiles:
                    square(sets[f // 4][:, f % 4, :], f, before_sq, before_add)

            post_squares(N_OUT + KT - 1, range(4), KT, KT - 1)
            for k in range(N_OUT + KT + SLOTS, N_UP + SLOTS):
                split1(k)
            post_squares(N_UP - 1, range(4, 8), KT, KT - 1)
            rsqrt_guess(2)
            for f in range(KT):
                act.wait_ge(x_new, f + 1)
                nc.scalar.activation(h_hi[:, f, :], x_t[:, f, :], ACT.Copy,
                                     scale=cols1[:, C_PMLP + f:C_PMLP + f + 1]).then_inc(xg_round, 1)
                square(x_t[:, f, :], f, 2 * KT, 2 * (KT - 1))

            def up1_out(set_, last, g_static, i=0, gper=0):
                act.wait_ge(w_used, i * (gper * KT) + last + 1)
                for j in range(4):
                    t = 4 * g_static + j
                    if t >= 4:
                        act.wait_ge(a_ready, i * (4 * gper) + (t - 3))
                    nc.scalar.activation(relu[:, j, :], set_[:, j, :], ACT.Relu).then_inc(relu_out, 1)
                for j in range(4):
                    t = 4 * g_static + j
                    act.wait_ge(relu_out, i * (4 * gper) + (t + 1))
                    nc.scalar.activation(relu[:, j, :], relu[:, j, :], ACT.Square).then_inc(relu_sq, 1)

            for g in range(2):
                for k in range(KT):
                    split1(N_UP + SLOTS + g * KT + k)
                if g == 0:
                    rsqrt_guess(3)
                up1_out(sets[g], N_UP + g * KT + KT - 1, g)
            with act.Fori(0, F1G // 2 - 1) as i:
                for g in range(2):
                    for k in range(KT):
                        split1(N_UP + SLOTS + (2 + g) * KT + k, i, 2 * KT)
                    up1_out(sets[g], N_UP + (2 + g) * KT + KT - 1, 2 + g, i, 2)

            def act_split(k, n, need_free, i=0):
                act.wait_ge(a_ready, i * 2 + (k + 1))
                if need_free:
                    act.wait_ge(w_used, i * 4 + n)
                nc.scalar.activation(as_hi[:, k % 2, :], act1[:, i * 2 + k, :], ACT.Copy).then_inc(as_round, 1)

            for k in range(2):
                act_split(k, 0, False)
            with act.Fori(0, F1T // 2 - 1) as kk:
                for k in range(2):
                    split1(N_DOWN + SLOTS + 2 * k, kk, 4)
                    split1(N_DOWN + SLOTS + 2 * k + 1, kk, 4)
                    act_split(k + 2, N_DOWN + 2 * k + 2, True, kk)
            post_squares(N_END1 - 2, range(4), 3 * KT, 3 * (KT - 1))
            post_squares(N_END1 - 1, range(4, 8), 3 * KT, 3 * (KT - 1))
            rsqrt_guess(4)
            meet(act, 0)

            with act.Fori(0, DEPTH2) as l:
                def split2(n, i=0, per=0):
                    s, c = n % SLOTS, width2(n)
                    act.wait_ge(w_land[s], i * (16 * pieces2(n) * per // SLOTS) + landed2(n))
                    if n >= SLOTS:
                        act.wait_ge(w_used, i * per + (n - SLOTS + 1))
                    nc.scalar.activation(w_hi[:, s, 0:c], w_raw[:, s, 0:c], ACT.Copy).then_inc(w_round, 1)

                nc.scalar.preload_act_table_set(LN_EXP)
                for n in range(SLOTS):
                    split2(n)
                act.wait_ge(cols_out, 1)
                for f in range(KT):
                    nc.scalar.activation(h_hi[:, f, :], x_t[:, f, :], ACT.Copy,
                                         scale=cols2[:, L_MIX + f:L_MIX + f + 1]).then_inc(xg_round, 1)
                    square(x_t[:, f, :], f, 0, 0)
                for k in range(KT):
                    split2(M_KV + SLOTS + k)
                rsqrt_guess(1)
                for t in range(KVT):
                    act.wait_ge(proj_out, t + 1)
                    square(ckv_f[:, t, :], t, KT, KT - 1)
                act.wait_ge(kr_step, 3)
                for hd in range(2):
                    nc.scalar.activation(kk_hi[ND:ND + RD, hd, :], rot[ND:ND + RD, 0, :], ACT.Copy).then_inc(kr_round, 1)
                for k in range(KT):
                    split2(M_Q + SLOTS + k)
                rsqrt_guess(2)
                for t in range(QT):
                    act.wait_ge(proj_out, 3 + t + 1)
                    square(cq_f[:, t, :], t, KT + KVT, KT + KVT - 2)
                for k in range(KT):
                    split2(M_A + SLOTS + k)
                rsqrt_guess(3)
                for k in range(KT):
                    split2(M_G + SLOTS + k)
                act.wait_ge(w_used, M_PAIR)
                act.wait_ge(cn_ready, KVT + QT)
                for t in range(KVT + QT):
                    src = cq_f[:, t, :] if t < QT else ckv_f[:, t - QT, :]
                    nc.scalar.activation(h_hi[:, t, :], src, ACT.Copy).then_inc(lat_round, 1)
                for j in range(4):
                    act.wait_ge(proj_out, 3 + QT + 4 + j + 1)
                    nc.scalar.activation(gf[:, j, :], gf[:, j, :], ACT.Sigmoid).then_inc(glu_sig, 1)
                nc.scalar.preload_act_table_set(LN_EXP)

                with act.Fori(0, PAIRS) as i:
                    act.wait_ge(w_used, i * SLOTS + (M_PAIR + QT))
                    for hd in range(2):
                        nc.scalar.activation(qf[0:ND, hd, :], bank_a[0:ND, hd, :], ACT.Copy).then_inc(qn_out, 1)
                    act.wait_ge(w_used, i * SLOTS + (M_PAIR + SLOTS))
                    for hd in range(2):
                        nc.scalar.activation(kk_hi[0:ND, hd, :], bank_a[0:ND, 2 + hd, :], ACT.Copy).then_inc(qk_round, 1)
                    nc.scalar.activation(vv_hi, bank_b[:, 0, :], ACT.Copy).then_inc(qk_round, 1)
                    for hd in range(2):
                        act.wait_ge(qr_step, i * 6 + 3 * (hd + 1))
                        act.wait_ge(qn_out, i * 2 + (hd + 1))
                        nc.scalar.activation(kq_hi[0:ND + RD, hd, :], qf[0:ND + RD, hd, :], ACT.Copy).then_inc(qk_round, 1)

                    def exps(hd):
                        for b in range(TT):
                            act.wait_ge(mx_step, i * 16 + (8 * hd + 2 * b + 2))
                            nc.scalar.activation(prob[:, b, :], bank_b[:, b, :], ACT.Exp, scale=MLA_SCALE,
                                                 bias=soft[:, 1, b:b + 1], accum_out=soft[:, 2, b:b + 1]).then_inc(p_exp, 1)

                    def pt_his(hd):
                        act.wait_ge(pt_made, i * 2 + (hd + 1))
                        for kb in range(TT):
                            nc.scalar.activation(pt_hi[:, kb, :], bank_a[:, kb, :], ACT.Copy).then_inc(pt_round, 1)

                    def out_of(hd):
                        rows = slice(ND * hd, ND * hd + ND)
                        act.wait_ge(pv_done, i * 2 + (hd + 1))
                        src = bank_a[rows, 0, :] if hd == 0 else bank_b[rows, 0, :]
                        nc.scalar.activation(o2_f[rows, i, :], src, ACT.Copy).then_inc(o2_out, 1)

                    exps(0)
                    pt_his(0)
                    exps(1)
                    out_of(0)
                    for k in range(SLOTS):
                        split2(M_PAIR + SLOTS + k, i, SLOTS)
                    pt_his(1)
                    out_of(1)

                act.wait_ge(w_used, M_WO)
                act.wait_ge(o2_out, 2 * PAIRS)
                for t in range(HT):
                    nc.scalar.activation(h_hi[:, t, :], o2_f[:, t, :], ACT.Copy).then_inc(o_round, 1)
                split2(M_WO + 4)
                for j in range(HT):
                    act.wait_ge(dev_ready, j + 1)
                    square(conv[:, j, :], j, KT + KVT + QT, KT + KVT + QT - 3)
                for k in range(5, 8):
                    split2(M_WO + k)
                rsqrt_guess(4)
                nc.scalar.preload_act_table(ACT.Silu)
                for j in range(HT):
                    act.wait_ge(ln_out, j + 1)
                    nc.scalar.activation(un[:, j, :], conv[:, j, :], ACT.Silu, scale=cols2[:, L_GLN + j:L_GLN + j + 1],
                                         bias=cols2[:, L_BLN + j:L_BLN + j + 1]).then_inc(silu_ready, 1)
                for j in range(HT):
                    act.wait_ge(silu_ready, j + 1)
                    nc.scalar.activation(h_hi[:, HT + j, :], un[:, j, :], ACT.Copy).then_inc(cu_round, 1)
                nc.scalar.preload_act_table_set(LN_EXP)
                for n in range(M_WO + 8, M_UP + SLOTS):
                    split2(n)
                act.wait_ge(w_used, M_UP)
                for f in range(KT):
                    act.wait_ge(x_new, f + 1)
                    nc.scalar.activation(h_hi[:, f, :], x_t[:, f, :], ACT.Copy,
                                         scale=cols2[:, L_FFN + f:L_FFN + f + 1]).then_inc(xg_round, 1)
                    square(x_t[:, f, :], f, KT + KVT + QT + HT, KT + KVT + QT + HT - 4)

                def mid_and_silu(g, i=0, gper=0):
                    if g:
                        act.wait_ge(a_ready, i * (2 * gper) + 2 * g)
                    for j in range(4):
                        tile = i * (2 * gper) + (2 * g + j % 2 + F2T * (j // 2))
                        act.wait_ge(z_out, i * (4 * gper) + (4 * g + j + 1))
                        nc.scalar.activation(cz[:, j, :], zp[:, j, 1:1 + S], ACT.Identity,
                                             scale=cols2[:, bass.ds(tile + (L_FTAP + 2 * F2T), 1)],
                                             bias=cols2[:, bass.ds(tile + L_BFF, 1)]).then_inc(z_mid, 1)
                    for j in range(2):
                        act.wait_ge(z_conv, i * (4 * gper) + (4 * g + j + 1))
                        nc.scalar.activation(cz[:, j, :], cz[:, j, :], ACT.Silu).then_inc(z_silu, 1)

                for k in range(KT):
                    split2(M_UP + SLOTS + k)
                rsqrt_guess(5)
                nc.scalar.preload_act_table(ACT.Silu)
                mid_and_silu(0)
                with act.Fori(0, F2G // 2) as i:
                    for g in range(2):
                        for k in range(KT):
                            split2(M_UP + SLOTS + (1 + g) * KT + k, i, 2 * KT)
                        mid_and_silu(1 + g, i, 2)

                def act_split2(k, n, need_free, i=0):
                    act.wait_ge(a_ready, i * 2 + (k + 1))
                    if need_free:
                        act.wait_ge(w_used, i * 4 + n)
                    nc.scalar.activation(as_hi[:, k % 2, :], act2[:, i * 2 + k, :], ACT.Copy).then_inc(as_round, 1)

                for k in range(2):
                    act_split2(k, 0, False)
                with act.Fori(0, F2T // 2 - 1) as kk:
                    for k in range(2):
                        split2(M_DOWN + SLOTS + 2 * k, kk, 4)
                        split2(M_DOWN + SLOTS + 2 * k + 1, kk, 4)
                        act_split2(k + 2, M_DOWN + 2 * k + 2, True, kk)
                meet(act, l + 1)

            nc.scalar.preload_act_table_set(LN_EXP)
            for f in range(KT):
                square(x_t[:, f, :], f, 0, 0)
            rsqrt_guess(1)
            for t in range(TT):
                act.wait_ge(yt_made, t + 1)
                nc.scalar.activation(y_out[:, t, 0:S], sets[t % 2][:, 2 * (t // 2), :], ACT.Copy).then_inc(yt_out, 1)

        @block.vector
        def _(dve):
            def tt(out_, a, b, op):
                return nc.vector.tensor_tensor(out_, a, b, op)

            def stt(out_, a, s, b, op0, op1):
                return nc.vector.scalar_tensor_tensor(out=out_, in0=a, scalar=s, in1=b, op0=op0, op1=op1)

            def rest(out_, full, hi):
                return tt(out_, full, hi.bitcast(F32), ALU.subtract)

            def split_lo(n, c=CW, i=0, per=0):
                s = n % SLOTS
                dve.wait_ge(w_round, i * per + (n + 1))
                rest(w_lo[:, s, 0:c], w_raw[:, s, 0:c], w_hi[:, s, 0:c]).then_inc(w_split, 1)

            def rstd_of(number, bank, width=D):
                dve.wait_ge(stat_ready, number)
                nc.vector.tensor_scalar(var[:, :], bank, 1.0 / width, EPS, ALU.mult, ALU.add).then_inc(var_ready, 1)
                dve.wait_ge(guess_ready, number)
                tt(rs0[:, :], rs1[:, :], rs1[:, :], ALU.mult).then_inc(newton, 1)
                dve.wait_ge(newton, 2 * number - 1)
                stt(rs0[:, :], rs0[:, :], -0.5, var[:, :], ALU.mult, ALU.mult).then_inc(newton, 1)
                dve.wait_ge(newton, 2 * number)
                stt(rstd[:, number % 2, :], rs0[:, :], 1.5, rs1[:, :], ALU.add, ALU.mult).then_inc(rstd_ready, 1)

            def rstd_into(number, bank, width):
                dve.wait_ge(stat_ready, number)
                nc.vector.tensor_scalar(var[:, :], bank, 1.0 / width, EPS, ALU.mult, ALU.add).then_inc(var_ready, 1)
                dve.wait_ge(guess_ready, number)
                tt(rs0[:, :], rs1[:, :], rs1[:, :], ALU.mult).then_inc(newton, 1)
                dve.wait_ge(newton, 2 * number - 1)
                stt(rs0[:, :], rs0[:, :], -0.5, var[:, :], ALU.mult, ALU.mult).then_inc(newton, 1)
                dve.wait_ge(newton, 2 * number)
                stt(rstd[:, 0, :], rs0[:, :], 1.5, rs1[:, :], ALU.add, ALU.mult).then_inc(rstd_ready, 1)
                dve.wait_ge(rstd_ready, number)

            def add_square(t, before_sq, before_add, before_stat):
                if t == 0:
                    return
                dve.wait_ge(sq_ready, before_sq + t + 1)
                if t == 1 and before_stat:
                    dve.wait_ge(stat_ready, before_stat)
                if t > 1:
                    dve.wait_ge(sq_added, before_add + t - 1)
                tt(ssum[:, :], sq[:, 0, :] if t == 1 else ssum[:, :], sq[:, t % 4, :], ALU.add).then_inc(sq_added, 1)

            dve.wait_ge(pos_land, 32)
            magic = 1.5 * 2.0 ** 23
            two_pi = (6.28125, 0.0019350051879882812, 3.0199159819e-07)
            steps = 0

            def step(ins):
                nonlocal steps
                steps += 1
                ins.then_inc(trig_step, 1)
                dve.wait_ge(trig_step, steps)

            step(nc.vector.tensor_copy(pos_f, pos_i))
            step(nc.vector.tensor_scalar(ang, pos_f, consts[:, 0:1], None, ALU.mult))
            step(nc.vector.tensor_scalar(turns, ang, 1.0 / 6.283185307179586, consts[:, 1:2], ALU.mult, ALU.add))
            step(nc.vector.tensor_scalar(turns, turns, magic, None, ALU.add))
            step(nc.vector.tensor_scalar(turns, turns, -magic, None, ALU.add))
            for part in two_pi:
                step(stt(ang, turns, -part, ang, ALU.mult, ALU.add))
            step(nc.vector.tensor_scalar(ang, ang, consts[:, 2:3], 3.1415925, ALU.add, ALU.min))
            step(nc.vector.tensor_scalar(ang, ang, -3.1415925, None, ALU.max))
            dve.wait_ge(trig_sin, 1)
            nc.vector.tensor_scalar(trig[:, :], trig[:, :], consts[:, 3:4], None, ALU.mult).then_inc(trig_step, 1)

            dve.wait_ge(consts_made, 7)
            dve.wait_ge(xt_made, 2)
            for f in range(4, KT):
                nc.vector.tensor_copy(x_t[:, f, :], bank_b[:, f - 4, :]).then_inc(xt_out_b, 1)
            dve.wait_ge(cols_made, 1)
            nc.vector.tensor_copy(cols1[:, :], bank_a[:, 0, 0:N_ROWS1]).then_inc(cols_out, 1)
            nc.vector.memset(u_pad[:, :, 0:LEFT], 0.0).then_inc(pool_step, 1)
            for n in range(SLOTS):
                split_lo(n)
            for t in range(KT):
                add_square(t, 0, 0, 0)
            rstd_of(1, bank_b[:, 0, :])
            dve.wait_ge(rstd_ready, 1)
            dve.wait_ge(cols_out, 1)
            for f in range(KT + 1):
                if f < KT:
                    if f >= 2:
                        dve.wait_ge(h_ready, f - 1)
                    stt(hf[:, f % 2, :], x_t[:, f, :], cols1[:, C_PRE + f:C_PRE + f + 1], rstd[:, 1, :],
                        ALU.mult, ALU.mult).then_inc(hf_ready, 1)
                if f >= 1:
                    dve.wait_ge(h_round, f)
                    rest(h_lo[:, f - 1, :], hf[:, (f - 1) % 2, :], h_hi[:, f - 1, :]).then_inc(h_ready, 1)

            with dve.Fori(0, PAIRS) as i:
                for k in range(KT):
                    split_lo(N_PAIR + SLOTS + k, CW, i, 2 * KT)
                dve.wait_ge(stage_round, i * 3 + 1)
                stt(q_lo, bank_a[:, 1, :], Q_SCALE, q_hi.bitcast(F32), ALU.mult, ALU.subtract).then_inc(stage_ready, 1)
                dve.wait_ge(stage_round, i * 3 + 2)
                rest(k_lo, bank_a[:, 2, :], k_hi).then_inc(stage_ready, 1)
                dve.wait_ge(stage_round, i * 3 + 3)
                rest(v_lo, bank_a[:, 3, :], v_hi).then_inc(stage_ready, 1)
                for s in range(9):
                    if s < 8:
                        split_lo(N_PAIR + SLOTS + KT + s, CW, i, 2 * KT)
                        kb = 3 - s % 4
                        n = S - P * kb
                        off = (3 - kb) * (4 - kb) // 2 * P
                        dve.wait_ge(soft_ready, i * 8 + (s + 1))
                        stt(sp[:, s % 2, 0:n], bank_a[:, s % 2, 0:n], 0.0, la[:, s % 2, 0:n],
                            ALU.max, ALU.add).then_inc(sp_step, 1)
                        dve.wait_ge(sp_step, i * 16 + (2 * s + 1))
                        tt(sp[:, s % 2, 0:P], sp[:, s % 2, 0:P], later[:, :], ALU.mult).then_inc(sp_step, 1)
                    if s >= 1:
                        kb1 = 3 - (s - 1) % 4
                        n1 = S - P * kb1
                        dve.wait_ge(attn_exp, i * 8 + s)
                        stt(at[:, (s - 1) % 2, 0:P], at[:, (s - 1) % 2, 0:P], BIG, later[:, :],
                            ALU.min, ALU.mult).then_inc(attn_masked, 1)
                    if s < 8:
                        dve.wait_ge(l_round, i * 8 + (s + 1))
                        rest(l_lo[:, s // 4, off:off + n], sp[:, s % 2, 0:n], l_hi[:, s // 4, off:off + n]).then_inc(l_ready, 1)
                    if s >= 1:
                        dve.wait_ge(attn_round, i * 8 + s)
                        rest(at_lo[:, (s - 1) % 2, 0:n1], at[:, (s - 1) % 2, 0:n1], at_hi[:, (s - 1) % 2, 0:n1]).then_inc(attn_ready, 1)

            for t in range(HT):
                dve.wait_ge(o_round, t + 1)
                rest(o_lo[:, t, :], o_f[:, t, :], o_hi[:, t, :]).then_inc(o_split, 1)
            pool_steps = 1

            def pool_group(g):
                nonlocal pool_steps

                def pstep(ins):
                    nonlocal pool_steps
                    pool_steps += 1
                    ins.then_inc(pool_step, 1)
                    dve.wait_ge(pool_step, pool_steps)

                w = WINDOWS[g]
                src, d, turn = u_pad[:, g, :], 1, 0
                while d < w:
                    lo = LEFT - (w - 2 * d)
                    dst = wsum[:, turn % 2, :]
                    pstep(tt(dst[:, lo:LEFT + S], src[:, lo:LEFT + S], src[:, lo - d:LEFT + S - d], ALU.add))
                    src, d, turn = dst, 2 * d, turn + 1
                if g >= 2:
                    dve.wait_ge(pool_split, g - 1)
                pstep(stt(pooled[:, g % 2, :], src[:, LEFT:LEFT + S], 1.0 / w, u_pad[:, g, LEFT:LEFT + S],
                          ALU.mult, ALU.subtract))
                pstep(tt(head16[:, 0:w], src[:, LEFT:LEFT + w], consts[:, 4:4 + w], ALU.mult))
                tt(pooled[:, g % 2, 0:w], head16[:, 0:w], u_pad[:, g, LEFT:LEFT + w], ALU.subtract).then_inc(pool_ready, 1)

            def pool_lo_of(g):
                dve.wait_ge(pool_round, g + 1)
                rest(pool_lo[:, g, :], pooled[:, g % 2, :], pool_hi[:, g, :]).then_inc(pool_split, 1)

            dve.wait_ge(u_out, PAIRS)
            pool_group(0)
            split_lo(N_MIX)
            pool_lo_of(0)
            pool_group(1)
            pool_lo_of(1)
            split_lo(N_PB0)
            pool_group(2)
            pool_lo_of(2)
            split_lo(N_PB0 + 1)
            pool_group(3)
            pool_lo_of(3)
            split_lo(N_PB0 + 2)

            def attention_gated(half):
                dve.wait_ge(w_used, (N_SB0, N_SB1)[half] + HT)
                dve.wait_ge(gate_ready, (1, 3)[half])
                for j in range(4):
                    tt(t_sb[:, j, :], bank_a[:, j, :], gates[:, 8 + 4 * half + j, :], ALU.mult).then_inc(sb_out, 1)

            def merge(half):
                dve.wait_ge(w_used, (N_PB0, N_PB1)[half] + HT)
                dve.wait_ge(gate_ready, (2, 4)[half])
                for j in range(5):
                    if j < 4:
                        tt(t_pb[:, j % 2, :], bank_b[:, j, :], gates[:, 4 * half + j, :], ALU.mult).then_inc(pb_out, 1)
                    if j >= 1:
                        dve.wait_ge(merge_round, 4 * half + j)
                        rest(h_lo[:, 4 * half + j - 1, :], merged[:, (j - 1) % 2, :],
                             h_hi[:, 4 * half + j - 1, :]).then_inc(merge_split, 1)
                    if j < 4:
                        dve.wait_ge(pb_out, 4 * half + j + 1)
                        dve.wait_ge(sb_out, 4 * half + j + 1)
                        tt(merged[:, j % 2, :], t_pb[:, j % 2, :], t_sb[:, j, :], ALU.add).then_inc(merge_ready, 1)

            attention_gated(0)
            split_lo(N_PB0 + 3)
            for g in range(HT):
                dve.wait_ge(y_round, g + 1)
                stt(h_lo[:, HT + g, :], bank_b[:, g, :], cols1[:, C_PSC + g:C_PSC + g + 1],
                    h_hi[:, HT + g, :].bitcast(F32), ALU.mult, ALU.subtract).then_inc(y_ready, 1)
            for k in range(HT):
                split_lo(N_SB1 + k)
            merge(0)
            for k in range(HT):
                split_lo(N_PB1 + k)
            attention_gated(1)
            for k in range(HT):
                split_lo(N_OUT + k)
            merge(1)
            for n in range(N_OUT + SLOTS, N_OUT + KT + SLOTS):
                split_lo(n)

            def post_out(tiles, col, before_sq, before_add, before_stat, before_mix):
                for f in tiles:
                    dve.wait_ge(sq_ready, before_sq + f + 1)
                    nc.vector.tensor_scalar(mixg[:, f, :], sets[f // 4][:, f % 4, :], cols1[:, col + f:col + f + 1],
                                            None, ALU.mult).then_inc(mix_out, 1)
                    add_square(f, before_sq, before_add, before_stat)

            def x_update(number, before_x, gain):
                dve.wait_ge(rstd_ready, number)
                dve.wait_ge(mix_out, before_x + KT)
                for f in range(KT + 2):
                    if f < KT:
                        if f >= 2:
                            dve.wait_ge(x_new, before_x + f - 1)
                        tt(xinc[:, f % 2, :], mixg[:, f, :], rstd[:, number % 2, :], ALU.mult).then_inc(xinc_ready, 1)
                    if 1 <= f <= KT:
                        dve.wait_ge(xinc_ready, before_x + f)
                        tt(x_t[:, f - 1, :], x_t[:, f - 1, :], xinc[:, (f - 1) % 2, :], ALU.add).then_inc(x_new, 1)
                    if f >= 2 and gain is not None:
                        dve.wait_ge(xg_round, f - 1)
                        stt(h_lo[:, f - 2, :], x_t[:, f - 2, :], cols1[:, gain + f - 2:gain + f - 1],
                            h_hi[:, f - 2, :].bitcast(F32), ALU.mult, ALU.subtract).then_inc(xg_ready, 1)

            post_out(range(4), C_POST, KT, KT - 1, 1, 0)
            for n in range(N_OUT + KT + SLOTS, N_UP + SLOTS):
                split_lo(n)
            post_out(range(4, 8), C_POST, KT, KT - 1, 1, 0)
            rstd_of(2, bank_a[:, 0, :])
            x_update(2, 0, C_PMLP)

            r2 = rstd[:, 0, :]

            def up1_act(g, i=0, gper=0):
                for j in range(4):
                    t = 4 * g + j
                    dve.wait_ge(relu_sq, i * (4 * gper) + (t + 1))
                    tt(act1[:, i * (4 * gper) + t, :], relu[:, j, :], r2, ALU.mult).then_inc(a_ready, 1)

            for g in range(2):
                for k in range(KT):
                    split_lo(N_UP + SLOTS + g * KT + k)
                if g == 0:
                    rstd_of(3, bank_b[:, 3, :])
                    dve.wait_ge(rstd_ready, 3)
                    tt(r2, rstd[:, 1, :], rstd[:, 1, :], ALU.mult).then_inc(r2_ready, 1)
                    dve.wait_ge(r2_ready, 1)
                up1_act(g)
            with dve.Fori(0, F1G // 2 - 1) as i:
                for g in range(2):
                    for k in range(KT):
                        split_lo(N_UP + SLOTS + (2 + g) * KT + k, CW, i, 2 * KT)
                    up1_act(2 + g, i, 2)

            def act_lo(acts, k, i=0):
                dve.wait_ge(as_round, i * 2 + (k + 1))
                rest(as_lo[:, k % 2, :], acts[:, i * 2 + k, :], as_hi[:, k % 2, :]).then_inc(as_ready, 1)

            for k in range(2):
                act_lo(act1, k)
            with dve.Fori(0, F1T // 2 - 1) as kk:
                for k in range(2):
                    split_lo(N_DOWN + SLOTS + 2 * k, CW, kk, 4)
                    split_lo(N_DOWN + SLOTS + 2 * k + 1, CW, kk, 4)
                    act_lo(act1, k + 2, kk)
            post_out(range(KT), C_QMLP, 3 * KT, 3 * (KT - 1), 3, KT)
            rstd_of(4, bank_a[:, 0, :])
            x_update(4, KT, None)
            meet(dve, 0)

            with dve.Fori(0, DEPTH2) as l:
                for n in range(SLOTS):
                    split_lo(n, width2(n))
                dve.wait_ge(cols_made, 1)
                nc.vector.tensor_copy(cols2[:, 0:N_ROWS2], bank_b[:, 0, 0:N_ROWS2]).then_inc(cols_out, 1)
                nc.vector.tensor_copy(cols2[:, L_TAP:L_FTAP].rearrange("p (c k) -> p c k", c=HT)[:, :, 0:CONV_K],
                                      bank_b[:, 0, L_TAP:L_FTAP].rearrange("p (c k) -> p c k", c=HT)[:, :, 0:CONV_K]
                                      ).then_inc(cols_out, 1)
                nc.vector.tensor_copy(cols2[:, L_FTAP:N_COLS2], bank_b[:, 0, L_FTAP:N_COLS2]).then_inc(cols_out, 1)
                nc.vector.memset(upad[:, :, 0:HALO], 0.0).then_inc(pad_zero, 1)
                nc.vector.memset(upad[:, :, HALO + S:CPAD], 0.0).then_inc(pad_zero, 1)
                dve.wait_ge(cols_out, 3)

                def xg_lo(f, col):
                    dve.wait_ge(xg_round, (0 if col == L_MIX else KT) + f + 1)
                    stt(h_lo[:, f, :], x_t[:, f, :], cols2[:, col + f:col + f + 1], h_hi[:, f, :].bitcast(F32),
                        ALU.mult, ALU.subtract).then_inc(xg_ready, 1)

                for f in range(KT):
                    xg_lo(f, L_MIX)
                for k in range(KT):
                    split_lo(M_KV + SLOTS + k, width2(M_KV + SLOTS + k))
                rstd_of(1, bank_b[:, 3, :])
                dve.wait_ge(rstd_ready, 1)
                norm = rstd[:, 1, :]

                def projected(dst, bank):
                    tt(dst, bank, norm[0:dst.shape[0], :], ALU.mult).then_inc(proj_out, 1)

                for t in range(KVT):
                    projected(ckv_f[:, t, :], bank_a[:, t, :])
                projected(krf[0:2 * RD, :], bank_a[0:2 * RD, 2, :])
                dve.wait_ge(proj_out, 3)
                dve.wait_ge(trig_step, 11)
                tt(rot[ND:ND + RD, 0, :], krf[0:RD, :], trig[0:RD, :], ALU.mult).then_inc(kr_step, 1)
                tt(rot[ND:ND + RD, 1, :], krf[RD:2 * RD, :], trig[RD:2 * RD, :], ALU.mult).then_inc(kr_step, 1)
                dve.wait_ge(kr_step, 2)
                tt(rot[ND:ND + RD, 0, :], rot[ND:ND + RD, 0, :], rot[ND:ND + RD, 1, :], ALU.add).then_inc(kr_step, 1)
                for hd in range(2):
                    dve.wait_ge(kr_round, hd + 1)
                    rest(kk_lo[ND:ND + RD, hd, :], rot[ND:ND + RD, 0, :], kk_hi[ND:ND + RD, hd, :]).then_inc(kr_ready, 1)
                for k in range(KT):
                    split_lo(M_Q + SLOTS + k, width2(M_Q + SLOTS + k))
                rstd_into(2, bank_b[:, 3, :], KVL)
                for t in range(KVT):
                    stt(ckv_f[:, t, :], ckv_f[:, t, :], cols2[:, L_GKV + t:L_GKV + t + 1], rstd[:, 0, :],
                        ALU.mult, ALU.mult).then_inc(cn_ready, 1)
                for t in range(QT):
                    projected(cq_f[:, t, :], bank_b[:, t, :])
                for k in range(KT):
                    split_lo(M_A + SLOTS + k)
                rstd_into(3, bank_b[:, 3, :], QL)
                for t in range(QT):
                    stt(cq_f[:, t, :], cq_f[:, t, :], cols2[:, L_GQ + t:L_GQ + t + 1], rstd[:, 0, :],
                        ALU.mult, ALU.mult).then_inc(cn_ready, 1)
                for j in range(4):
                    projected(af[:, j, :], bank_a[:, j, :])
                for k in range(KT):
                    split_lo(M_G + SLOTS + k)
                dve.wait_ge(w_used, M_PAIR)
                for j in range(4):
                    projected(gf[:, j, :], bank_b[:, j, :])
                for t in range(KVT + QT):
                    src = cq_f[:, t, :] if t < QT else ckv_f[:, t - QT, :]
                    dve.wait_ge(lat_round, t + 1)
                    rest(h_lo[:, t, :], src, h_hi[:, t, :]).then_inc(lat_ready, 1)
                for j in range(4):
                    dve.wait_ge(glu_sig, j + 1)
                    tt(upad[:, j, HALO:HALO + S], af[:, j, :], gf[:, j, :], ALU.mult).then_inc(u_ready, 1)
                dve.wait_ge(pad_zero, 2)

                with dve.Fori(0, PAIRS) as i:
                    tap = 0
                    dve.wait_ge(u_ready, i + 1)

                    def taps(count):
                        nonlocal tap
                        for _ in range(min(count, CONV_K - tap)):
                            m = tap
                            acc = conv_odd if m % 2 else conv[:, i, :]
                            src = upad[:, i, m:m + S]
                            w = cols2[:, bass.ds(i * 32 + (L_TAP + m), 1)]
                            if m == 0:
                                ins = nc.vector.tensor_scalar(acc, src, w, cols2[:, bass.ds(i + L_BDW, 1)], ALU.mult, ALU.add)
                            elif m == 1:
                                ins = nc.vector.tensor_scalar(acc, src, w, None, ALU.mult)
                            else:
                                dve.wait_ge(tap_done, i * CONV_K + (m - 1))
                                ins = stt(acc, src, w, acc, ALU.mult, ALU.add)
                            ins.then_inc(tap_done, 1)
                            tap += 1

                    dve.wait_ge(w_used, i * SLOTS + (M_PAIR + QT))
                    for hd in range(2):
                        tt(qf[ND:ND + RD, hd, :], bank_a[ND:ND + RD, hd, :], trig[ND:ND + RD, :], ALU.mult).then_inc(qr_step, 1)
                        tt(rot[ND:ND + RD, hd, :], bank_a[ND + RD:P, hd, :], trig[ND + RD:P, :], ALU.mult).then_inc(qr_step, 1)
                        dve.wait_ge(qr_step, i * 6 + (3 * hd + 2))
                        tt(qf[ND:ND + RD, hd, :], qf[ND:ND + RD, hd, :], rot[ND:ND + RD, hd, :], ALU.add).then_inc(qr_step, 1)
                    for hd in range(2):
                        dve.wait_ge(qk_round, i * 5 + (hd + 1))
                        rest(kk_lo[0:ND, hd, :], bank_a[0:ND, 2 + hd, :], kk_hi[0:ND, hd, :]).then_inc(qk_ready, 1)
                    dve.wait_ge(qk_round, i * 5 + 3)
                    rest(vv_lo, bank_b[:, 0, :], vv_hi).then_inc(qk_ready, 1)
                    for hd in range(2):
                        dve.wait_ge(qk_round, i * 5 + (4 + hd))
                        rest(kq_lo[0:ND + RD, hd, :], qf[0:ND + RD, hd, :], kq_hi[0:ND + RD, hd, :]).then_inc(qk_ready, 1)

                    def maxima(hd, b):
                        m0 = i * 16 + (8 * hd + 2 * b)
                        dve.wait_ge(s_ready, i * 8 + (4 * hd + b + 1))
                        nc.vector.tensor_reduce(soft[:, 0, b:b + 1], bank_b[:, b, :], AX_X, ALU.max).then_inc(mx_step, 1)
                        taps(1)
                        dve.wait_ge(mx_step, m0 + 1)
                        nc.vector.tensor_scalar(soft[:, 1, b:b + 1], soft[:, 0, b:b + 1], -MLA_SCALE, None,
                                                ALU.mult).then_inc(mx_step, 1)

                    def normalise(hd, b):
                        dve.wait_ge(p_exp, i * 8 + (4 * hd + b + 1))
                        nc.vector.reciprocal(soft[:, 3, b:b + 1], soft[:, 2, b:b + 1]).then_inc(p_step, 1)
                        taps(1)
                        dve.wait_ge(p_step, i * 8 + (4 * hd + b + 1))
                        nc.vector.tensor_scalar(prob[:, b, :], prob[:, b, :], soft[:, 3, b:b + 1], None,
                                                ALU.mult).then_inc(p_ready, 1)

                    def pt_los(hd):
                        for kb in range(TT):
                            dve.wait_ge(pt_round, i * 8 + (4 * hd + kb + 1))
                            rest(pt_lo[:, kb, :], bank_a[:, kb, :], pt_hi[:, kb, :]).then_inc(pt_ready, 1)

                    for hd in range(2):
                        for b in range(TT + 1):
                            if b < TT:
                                maxima(hd, b)
                            if b >= 1:
                                normalise(hd, b - 1)
                        if hd == 1:
                            for k in range(SLOTS):
                                split_lo(M_PAIR + SLOTS + k, CW, i, SLOTS)
                        pt_los(hd)
                    taps(CONV_K)
                    dve.wait_ge(tap_done, i * CONV_K + CONV_K)
                    tt(conv[:, i, :], conv[:, i, :], conv_odd, ALU.add).then_inc(conv_ready, 1)

                for t in range(HT):
                    dve.wait_ge(o_round, t + 1)
                    rest(h_lo[:, t, :], o2_f[:, t, :], h_hi[:, t, :]).then_inc(o_split, 1)
                dve.wait_ge(mean_ready, 1)
                dve.wait_ge(conv_ready, HT)
                for j in range(HT):
                    stt(conv[:, j, :], bank_b[:, 1, :], -1.0 / HALF, conv[:, j, :], ALU.mult, ALU.add).then_inc(dev_ready, 1)
                split_lo(M_WO + 4)
                for j in range(HT):
                    add_square(j, KT + KVT + QT, KT + KVT + QT - 3, 3)
                for k in range(5, 8):
                    split_lo(M_WO + k)
                rstd_into(4, bank_b[:, 2, :], HALF)
                for j in range(HT):
                    tt(conv[:, j, :], conv[:, j, :], rstd[:, 0, :], ALU.mult).then_inc(ln_out, 1)
                for j in range(HT):
                    dve.wait_ge(cu_round, j + 1)
                    rest(h_lo[:, HT + j, :], un[:, j, :], h_hi[:, HT + j, :]).then_inc(cu_ready, 1)
                for n in range(M_WO + 8, M_WO + 12):
                    split_lo(n)

                def x_add(f):
                    tt(x_t[:, f, :], x_t[:, f, :], sets[f // 4][:, f % 4, :], ALU.add).then_inc(x_new, 1)

                dve.wait_ge(w_used, M_WO + KT)
                for f in range(4):
                    x_add(f)
                for n in range(M_WO + 12, M_UP + SLOTS):
                    split_lo(n)
                dve.wait_ge(w_used, M_UP)
                for f in range(4, KT):
                    x_add(f)
                for f in range(KT):
                    xg_lo(f, L_FFN)
                nc.vector.memset(zp[:, :, 0:1], 0.0).then_inc(zp_zero, 1)
                nc.vector.memset(zp[:, :, S + 1:ZPAD], 0.0).then_inc(zp_zero, 1)

                def ffn_tiles(set_, g, i=0, gper=0):
                    z0 = i * (4 * gper) + 4 * g
                    for j in range(4):
                        tt(zp[:, j, 1:1 + S], set_[:, j, :], rstd[:, 1, :], ALU.mult).then_inc(z_out, 1)
                    for tap, done in ((0, z_tap), (2, z_conv)):
                        for j in range(4):
                            tile = i * (2 * gper) + (2 * g + j % 2 + F2T * (j // 2))
                            dve.wait_ge(z_tap if tap else z_mid, z0 + (j + 1))
                            stt(cz[:, j, :], zp[:, j, tap:tap + S],
                                cols2[:, bass.ds(tile + (L_FTAP + tap * 2 * F2T), 1)], cz[:, j, :],
                                ALU.mult, ALU.add).then_inc(done, 1)
                    for j in range(2):
                        dve.wait_ge(z_silu, i * (2 * gper) + (2 * g + j + 1))
                        dve.wait_ge(z_conv, z0 + (j + 3))
                        tt(act2[:, i * (2 * gper) + (2 * g + j), :], cz[:, j, :], cz[:, 2 + j, :],
                           ALU.mult).then_inc(a_ready, 1)

                for k in range(KT):
                    split_lo(M_UP + SLOTS + k)
                rstd_of(5, bank_b[:, 3, :])
                dve.wait_ge(rstd_ready, 5)
                dve.wait_ge(zp_zero, 2)
                dve.wait_ge(w_used, M_UP + KT)
                ffn_tiles(bank_a, 0)
                with dve.Fori(0, F2G // 2) as i:
                    for g in range(2):
                        for k in range(KT):
                            split_lo(M_UP + SLOTS + (1 + g) * KT + k, CW, i, 2 * KT)
                        dve.wait_ge(w_used, i * (2 * KT) + (M_UP + (2 + g) * KT))
                        ffn_tiles(sets[1 - g], 1 + g, i, 2)

                for k in range(2):
                    act_lo(act2, k)
                with dve.Fori(0, F2T // 2 - 1) as kk:
                    for k in range(2):
                        split_lo(M_DOWN + SLOTS + 2 * k, CW, kk, 4)
                        split_lo(M_DOWN + SLOTS + 2 * k + 1, CW, kk, 4)
                        act_lo(act2, k + 2, kk)
                dve.wait_ge(w_used, M_END - 1)
                for f in range(4):
                    x_add(f)
                dve.wait_ge(w_used, M_END)
                for f in range(4, KT):
                    x_add(f)
                meet(dve, l + 1)

            for t in range(KT):
                add_square(t, 0, 0, 0)
            rstd_of(1, bank_a[:, 0, :])
            dve.wait_ge(rstd_ready, 1)
            for f in range(KT):
                stt(yfin[:, f, :], x_t[:, f, :], cols1[:, C_FIN + f:C_FIN + f + 1], rstd[:, 1, :],
                    ALU.mult, ALU.mult).then_inc(y_made, 1)
            for t in range(TT):
                dve.wait_ge(yt_made, t + 1)
                nc.vector.tensor_copy(y_out[:, t, S:2 * S], sets[t % 2][:, 2 * (t // 2) + 1, :]).then_inc(yt_out_b, 1)

        @block.tensor
        def _(pe):
            def use(n, i=0, per=0):
                pe.wait_ge(w_split, i * per + (n + 1))
                return n % SLOTS

            def mm3(out_, a_hi, a_lo, b_hi, b_lo, start, stop, loose=False):
                nc.tensor.matmul(out_, a_hi, b_hi, start=start, stop=False, skip_group_check=loose)
                nc.tensor.matmul(out_, a_hi, b_lo, start=False, stop=False, skip_group_check=loose)
                return nc.tensor.matmul(out_, a_lo, b_hi, start=False, stop=stop, skip_group_check=loose)

            def wide(set_, s, b_hi, b_lo, start, stop, tiles=4):
                for j in range(tiles):
                    c = slice(j * P, j * P + P)
                    last = mm3(set_[:, j, :], w_hi[:, s, c], w_lo[:, s, c], b_hi, b_lo, start, stop)
                last.then_inc(w_used, 1)

            def total(bank, added):
                pe.wait_ge(sq_added, added)
                nc.tensor.matmul(bank, ones[:, :], ssum[:, :], start=True, stop=True).then_inc(stat_ready, 1)

            pe.wait_ge(consts_made, 2)
            for half in range(2):
                for f in range(4):
                    for t in range(TT):
                        if half == 0 and f == 0:
                            pe.wait_ge(x_land[t], 16)
                        c = (4 * half + f) * P
                        last = nc.tensor.transpose(sets[half][:, f, t * P:t * P + P], x_in[:, t, c:c + P], ident[:, :])
                last.then_inc(xt_made, 1)
            pe.wait_ge(rows1_land, 16 * 7)
            pe.wait_ge(xt_out, 1)
            nc.tensor.transpose(bank_a[:, 0, 0:N_ROWS1], rows1[:, :], ident[0:N_ROWS1, 0:N_ROWS1]).then_inc(cols_made, 1)
            pe.wait_ge(consts_made, 3)
            pe.wait_ge(xt_out_b, 4)
            total(bank_b[:, 0, :], KT - 1)
            pe.wait_ge(tri_made, 1)
            pe.wait_ge(xt_out, 4)
            pe.wait_ge(cols_out, 1)
            pe.wait_ge(var_ready, 1)

            with pe.Fori(0, PAIRS) as i:
                for k in range(KT):
                    s = use(N_PAIR + k, i, 2 * KT)
                    pe.wait_ge(h_ready, k + 1)
                    for b in range(3):
                        c = slice(b * P, b * P + P)
                        mm3(bank_a[:, b, :], w_hi[:, s, c], w_lo[:, s, c], h_hi[:, k, :], h_lo[:, k, :],
                            k == 0, k == KT - 1)
                    for j in range(TT):
                        c = slice(j * P, j * P + P)
                        last = mm3(bank_a[:, 3, c], h_hi[:, k, c], h_lo[:, k, c], w_hi[:, s, 3 * P:], w_lo[:, s, 3 * P:],
                                   k == 0 and j == 0, k == KT - 1, True)
                    last.then_inc(w_used, 1)

                def gate(k):
                    s = use(N_PAIR + KT + k, i, 2 * KT)
                    wide(bank_b, s, h_hi[:, k, :], h_lo[:, k, :], k == 0, k == KT - 1)

                def scores(s):
                    hd, kb = s // 4, 3 - s % 4
                    rows = slice(HEAD * hd, HEAD * hd + HEAD)
                    c = slice(kb * P, kb * P + P)
                    if s == 0:
                        pe.wait_ge(stage_ready, i * 3 + 2)
                        pe.wait_ge(u_out, i + 1)
                    if s >= 2:
                        pe.wait_ge(attn_exp, i * 8 + (s - 1))
                    mm3(bank_a[:, s % 2, 0:S - kb * P], k_hi[rows, c], k_lo[rows, c], q_hi[rows, kb * P:S],
                        q_lo[rows, kb * P:S], True, True).then_inc(z_ready, 1)

                def log_sums(s):
                    hd, kb = s // 4, 3 - s % 4
                    pe.wait_ge(l_ready, i * 8 + (s + 1))
                    for kb2 in range(kb, TT):
                        off, n = (3 - kb2) * (4 - kb2) // 2 * P, S - P * kb2
                        z0 = P * (kb2 - kb)
                        for part in (l_hi, l_lo):
                            last = nc.tensor.matmul(bank_a[:, s % 2, z0:z0 + n], tri[:, 0 if kb2 == kb else 1, :],
                                                    part[:, hd, off:off + n], start=False,
                                                    stop=kb2 == TT - 1 and part is l_lo, skip_group_check=True)
                    last.then_inc(c_ready, 1)

                def values(s):
                    hd, kb = s // 4, 3 - s % 4
                    c = slice(kb * P, kb * P + P)
                    n = S - kb * P
                    if s == 0:
                        pe.wait_ge(stage_ready, i * 3 + 3)
                    pe.wait_ge(attn_ready, i * 8 + (s + 1))
                    mm3(bank_a[:, 2 + hd, kb * P:S], v_hi[:, c], v_lo[:, c], at_hi[:, s % 2, 0:n], at_lo[:, s % 2, 0:n],
                        kb == TT - 1, kb == 0, True).then_inc(av_done, 1)

                gate(0)
                scores(0)
                for s in range(8):
                    if s < 7:
                        gate(s + 1)
                        scores(s + 1)
                    log_sums(s)
                    if s >= 1:
                        values(s - 1)
                values(7)
                pe.wait_ge(attn_exp, i * 8 + 8)
                pe.wait_ge(o_out, i * 2 + 2)

            for k in range(HT):
                s = use(N_SB0 + k)
                pe.wait_ge(o_split, k + 1)
                wide(bank_a, s, o_hi[:, k, :], o_lo[:, k, :], k == 0, k == HT - 1)
            s = use(N_MIX)
            pe.wait_ge(gate_out, 16)
            for g in range(HT):
                pe.wait_ge(pool_split, g + 1)
                c = slice(g * P, g * P + P)
                last = mm3(bank_b[:, g, :], w_hi[:, s, c], w_lo[:, s, c], pool_hi[:, g, :], pool_lo[:, g, :], True, True)
            last.then_inc(w_used, 1)
            pe.wait_ge(y_ready, HT)
            for k in range(HT):
                s = use(N_PB0 + k)
                wide(bank_b, s, h_hi[:, HT + k, :], h_lo[:, HT + k, :], k == 0, k == HT - 1)
            pe.wait_ge(sb_out, 4)
            for k in range(HT):
                s = use(N_SB1 + k)
                wide(bank_a, s, o_hi[:, k, :], o_lo[:, k, :], k == 0, k == HT - 1)
            pe.wait_ge(pb_out, 4)
            for k in range(HT):
                s = use(N_PB1 + k)
                wide(bank_b, s, h_hi[:, HT + k, :], h_lo[:, HT + k, :], k == 0, k == HT - 1)
            for half, branch_out in enumerate((sb_out, pb_out)):
                pe.wait_ge(branch_out, 8)
                for k in range(KT):
                    s = use(N_OUT + half * KT + k)
                    pe.wait_ge(merge_split, k + 1)
                    wide(sets[half], s, h_hi[:, k, :], h_lo[:, k, :], k == 0, k == KT - 1)
            pe.wait_ge(mix_out, 4)
            total(bank_a[:, 0, :], 2 * (KT - 1))

            def up1(set_, g, i=0, gper=0):
                for k in range(KT):
                    s = use(N_UP + g * KT + k, i, gper * KT)
                    if g == 0:
                        pe.wait_ge(xg_ready, k + 1)
                    wide(set_, s, h_hi[:, k, :], h_lo[:, k, :], k == 0, k == KT - 1)

            pe.wait_ge(var_ready, 2)
            up1(bank_a, 0)
            pe.wait_ge(mix_out, 8)
            total(bank_b[:, 3, :], 3 * (KT - 1))
            pe.wait_ge(var_ready, 3)
            up1(bank_b, 1)
            with pe.Fori(0, F1G // 2 - 1) as i:
                for g in range(2):
                    pe.wait_ge(relu_out, i * 8 + 4 * (g + 1))
                    up1(sets[g], 2 + g, i, 2)

            def down(n, k, half, start, stop, i=0):
                s = use(n + 2 * k + half, i, 4)
                pe.wait_ge(as_ready, i * 2 + (k + 1))
                wide(sets[half], s, as_hi[:, k % 2, :], as_lo[:, k % 2, :], start, stop)

            def down_all(n, count):
                for k in range(2):
                    for half in range(2):
                        down(n, k, half, k == 0, False)
                with pe.Fori(0, count // 2 - 2) as kk:
                    for k in range(2, 4):
                        for half in range(2):
                            down(n, k, half, False, False, kk)
                for k in range(count - 2, count):
                    for half in range(2):
                        down(n, k, half, False, k == count - 1)

            pe.wait_ge(relu_out, 4 * F1G)
            down_all(N_DOWN, F1T)
            pe.wait_ge(mix_out, KT + 4)
            total(bank_a[:, 0, :], 4 * (KT - 1))
            meet(pe, 0)

            with pe.Fori(0, DEPTH2) as l:
                pe.wait_ge(rows2_land, l * 160 + 160)
                nc.tensor.transpose(bank_b[:, 0, 0:N_ROWS2], rows2[:, :], ident[0:N_ROWS2, 0:N_ROWS2])
                for c in range(HT):
                    nc.tensor.transpose(bank_b[:, 0, L_TAP + 32 * c:L_TAP + 32 * c + CONV_K],
                                        rows_tap[:, c * P:c * P + P], ident[0:CONV_K, 0:CONV_K])
                for tap in range(3):
                    c = L_FTAP + tap * 2 * F2T
                    last = nc.tensor.transpose(bank_b[:, 0, c:c + 2 * F2T], rows_ftap[:, tap, :],
                                               ident[0:2 * F2T, 0:2 * F2T])
                last.then_inc(cols_made, 1)

                for k in range(KT):
                    s = use(M_KV + k)
                    pe.wait_ge(xg_ready, k + 1)
                    for j in range(KVT):
                        c = slice(j * P, j * P + P)
                        mm3(bank_a[:, j, :], w_hi[:, s, c], w_lo[:, s, c], h_hi[:, k, :], h_lo[:, k, :],
                            k == 0, k == KT - 1)
                    c = slice(KVL, KV_COLS)
                    mm3(bank_a[0:2 * RD, 2, :], w_hi[:, s, c], w_lo[:, s, c], h_hi[:, k, :], h_lo[:, k, :],
                        k == 0, k == KT - 1).then_inc(w_used, 1)
                total(bank_b[:, 3, :], KT - 1)
                pe.wait_ge(cols_out, 3)
                for k in range(KT):
                    s = use(M_Q + k)
                    wide(bank_b, s, h_hi[:, k, :], h_lo[:, k, :], k == 0, k == KT - 1, QT)
                pe.wait_ge(var_ready, 1)
                total(bank_b[:, 3, :], KT + KVT - 2)
                pe.wait_ge(proj_out, KVT + 1)
                for k in range(KT):
                    s = use(M_A + k)
                    wide(bank_a, s, h_hi[:, k, :], h_lo[:, k, :], k == 0, k == KT - 1)
                pe.wait_ge(var_ready, 2)
                total(bank_b[:, 3, :], KT + KVT + QT - 3)
                pe.wait_ge(proj_out, KVT + 1 + QT)
                pe.wait_ge(var_ready, 3)
                for k in range(KT):
                    s = use(M_G + k)
                    wide(bank_b, s, h_hi[:, k, :], h_lo[:, k, :], k == 0, k == KT - 1)

                pe.wait_ge(proj_out, KVT + 1 + QT + 8)
                with pe.Fori(0, PAIRS) as i:
                    for k in range(QT):
                        s = use(M_PAIR + k, i, SLOTS)
                        pe.wait_ge(lat_ready, k + 1)
                        for hd in range(2):
                            c = slice(hd * P, hd * P + P)
                            last = mm3(bank_a[:, hd, :], w_hi[:, s, c], w_lo[:, s, c], h_hi[:, k, :], h_lo[:, k, :],
                                       k == 0, k == QT - 1)
                        last.then_inc(w_used, 1)
                    s = use(M_PAIR + QT, i, SLOTS)
                    pe.wait_ge(lat_ready, QT + KVT)
                    for hd in range(2):
                        for kk in range(KVT):
                            c = slice(kk * 4 * ND + hd * 2 * ND, kk * 4 * ND + hd * 2 * ND + P)
                            mm3(bank_a[:, 2 + hd, :], w_hi[:, s, c], w_lo[:, s, c], h_hi[:, QT + kk, :],
                                h_lo[:, QT + kk, :], kk == 0, kk == KVT - 1)
                    for kk in range(KVT):
                        wv_hi, wv_lo = (w[:, s, kk * 4 * ND:(kk + 1) * 4 * ND].rearrange(
                            "p (h c) -> p h c", h=2)[:, :, ND:2 * ND] for w in (w_hi, w_lo))
                        for j in range(TT):
                            c = slice(j * P, j * P + P)
                            last = mm3(bank_b[:, 0, c], h_hi[:, QT + kk, c], h_lo[:, QT + kk, c], wv_hi, wv_lo,
                                       kk == 0 and j == 0, kk == KVT - 1, True)
                    last.then_inc(w_used, 1)

                    def scores2(hd):
                        pe.wait_ge(qk_ready, i * 5 + (4 + hd))
                        pe.wait_ge(kr_ready, 2)
                        for b in range(TT):
                            c = slice(b * P, b * P + P)
                            if hd == 1:
                                pe.wait_ge(p_exp, i * 8 + (b + 1))
                            mm3(bank_b[:, b, :], kq_hi[0:ND + RD, hd, c], kq_lo[0:ND + RD, hd, c], kk_hi[0:ND + RD, hd, :],
                                kk_lo[0:ND + RD, hd, :], True, True).then_inc(s_ready, 1)

                    def transposed(hd):
                        if hd == 0:
                            pe.wait_ge(qk_ready, i * 5 + 5)
                        else:
                            pe.wait_ge(pt_ready, i * 8 + 4)
                            pe.wait_ge(o2_out, i * 2 + 1)
                        for b in range(TT):
                            pe.wait_ge(p_ready, i * 8 + (4 * hd + b + 1))
                            for kb in range(TT):
                                last = nc.tensor.transpose(bank_a[:, kb, b * P:b * P + P], prob[:, b, kb * P:kb * P + P],
                                                           ident[:, :])
                        last.then_inc(pt_made, 1)

                    def values2(hd):
                        for kb in range(TT):
                            if kb == 0:
                                pe.wait_ge(pt_ready, i * 8 + (4 * hd + 4))
                            c = slice(kb * P, kb * P + P)
                            last = mm3(sets[hd][:, 0, :], vv_hi[:, c], vv_lo[:, c], pt_hi[:, kb, :], pt_lo[:, kb, :],
                                       kb == 0, kb == TT - 1)
                        last.then_inc(pv_done, 1)

                    scores2(0)
                    transposed(0)
                    scores2(1)
                    values2(0)
                    transposed(1)
                    values2(1)
                    pe.wait_ge(pt_ready, i * 8 + 8)
                    pe.wait_ge(o2_out, i * 2 + 2)

                pe.wait_ge(p_exp, 8 * PAIRS)
                for j in range(HT):
                    pe.wait_ge(conv_ready, j + 1)
                    last = nc.tensor.matmul(bank_b[:, 1, :], ones[:, :], conv[:, j, :], start=j == 0, stop=j == HT - 1)
                last.then_inc(mean_ready, 1)
                for k in range(KT):
                    s = use(M_WO + k)
                    if k == HT:
                        total(bank_b[:, 2, :], KT + KVT + QT + HT - 4)
                    pe.wait_ge(o_split if k < HT else cu_ready, k % HT + 1)
                    wide(bank_a, s, h_hi[:, k, :], h_lo[:, k, :], k == 0, k == KT - 1)
                pe.wait_ge(dev_ready, HT)
                pe.wait_ge(var_ready, 4)
                for k in range(KT):
                    s = use(M_WO + KT + k)
                    wide(bank_b, s, h_hi[:, k, :], h_lo[:, k, :], k == 0, k == KT - 1)

                def up2(set_, g, i=0, gper=0):
                    for k in range(KT):
                        s = use(M_UP + g * KT + k, i, gper * KT)
                        if g == 0:
                            pe.wait_ge(xg_ready, KT + k + 1)
                        wide(set_, s, h_hi[:, k, :], h_lo[:, k, :], k == 0, k == KT - 1)

                pe.wait_ge(x_new, 4)
                up2(bank_a, 0)
                pe.wait_ge(x_new, KT)
                total(bank_b[:, 3, :], KT + KVT + QT + HT - 4 + KT - 1)
                pe.wait_ge(var_ready, 5)
                with pe.Fori(0, F2G // 2) as i:
                    up2(bank_b, 1, i, 2)
                    pe.wait_ge(z_out, i * 8 + 4)
                    up2(bank_a, 2, i, 2)
                    pe.wait_ge(z_out, i * 8 + 8)
                pe.wait_ge(z_out, 4 * F2G)
                down_all(M_DOWN, F2T)
                meet(pe, l + 1)

            total(bank_a[:, 0, :], KT - 1)
            pe.wait_ge(var_ready, 1)
            pe.wait_ge(y_made, KT)
            for t in range(TT):
                for f in range(KT):
                    last = nc.tensor.transpose(sets[t % 2][:, 2 * (t // 2) + f // 4, (f % 4) * P:(f % 4) * P + P],
                                               yfin[:, f, t * P:t * P + P], ident[:, :])
                last.then_inc(yt_made, 1)


_BLOCK1 = ["x", "g_pre_mix", "w_in", "w_pool_mix", "pool_scale", "w_br_pool", "w_br_sb", "w_gate", "b_gate", "w_out",
           "g_post_mix", "g_pre_mlp", "w_up", "w_down", "g_post_mlp"]
_BLOCK2 = ["positions_2", "g_mix_2", "w_in_2", "g_q_2", "w_uq_2", "g_kv_2", "w_ukv_2", "w_dw_conv_2", "b_dw_conv_2",
           "g_conv_ln_2", "b_conv_ln_2", "w_o_2", "g_ffn_2", "w_up_2", "w_dw_ffn_2", "b_dw_ffn_2", "w_down_2",
           "g_final_2"]


def shape_constants(np):
    row = np.arange(P)
    cosine = (row // RD) % 2 == 0
    freq = 1.0 / (np.float32(10000.0) ** (np.arange(0, RD, 2, dtype=np.float32) / np.float32(RD)))
    c = np.zeros((P, 4 + LEFT), np.float32)
    c[:, 0] = freq[row % (RD // 2)]
    c[:, 1] = np.where(cosine, 0.25, 0.0)
    c[:, 2] = np.where(cosine, np.pi / 2, 0.0)
    c[:, 3] = np.where(cosine | (row % RD >= RD // 2), 1.0, -1.0)
    c[:, 4:] = 1.0 / (np.arange(LEFT) + 1.0)
    return c


def kernel(**inputs):
    import numpy as _np
    import concourse.bacc as _bacc
    from concourse import mybir as _mybir
    from concourse.bass_utils import run_bass_kernel_spmd as _run

    nc = _bacc.Bacc("TRN2", target_bir_lowering=False, num_devices=1)
    arrays, args = {}, []
    given = [(name, _np.ascontiguousarray(inputs[name])) for name in _BLOCK1 + _BLOCK2]
    given.append(("shape_consts", shape_constants(_np)))
    for name, a in given:
        arrays[f"in_{name}_dram"] = a
        args.append(nc.dram_tensor(f"in_{name}_dram", a.shape, _mybir.dt.from_np(a.dtype), kind="ExternalInput").ap())
    args.append(nc.dram_tensor("out_dram", (1, S, D), _mybir.dt.float32, kind="ExternalOutput").ap())
    two_blocks(nc, *args)
    r = _run(nc, [arrays], core_ids=[0])
    return r.results[0]["out_dram"]
```

```python
from contextlib import ExitStack

import concourse.bass as bass
from concourse import mybir

P = 128
D = 1024
S = 512
KT = D // P
HALF_TILES = KT // 2
TT = S // P
EPS = 1e-6
SLOTS = 4
CW = 512

HALF = D // 2
HT = HALF // P
HEAD = 64
PAIRS = HALF // (2 * HEAD)
WINDOWS = (2, 4, 8, 16)
LEFT = 16
FF1 = 4096
F1T = FF1 // P
F1G = FF1 // CW
Q0 = (0, P, P, 3 * P)
L_OFF = (P + 6 * P, P + 3 * P, P, 0)
L_ALL = P + 6 * P + S
Q_SCALE = HEAD ** -0.5

DEPTH2 = 2
QL, KVL, RD = 384, 256, 32
QT, KVT = QL // P, KVL // P
ND = 64
MLA_SCALE = (ND + RD) ** -0.5
CONV_K = 31
POOL_TAPS = 20
DVE_TAPS = CONV_K - POOL_TAPS
HALO = CONV_K // 2
BLOCKS = PAIRS * 2 * TT
FF2 = 2816
F2T = FF2 // P
F2G = FF2 // 256

F32 = mybir.dt.float32
F32R = mybir.dt.float32r
I32 = mybir.dt.int32
ALU = mybir.AluOpType
ACT = mybir.ActivationFunctionType
AX_X = mybir.AxisListType.X
LN_EXP = "natural_log_exp_and_others"
BIG = 3.0e38

C_PRE, C_PSC, C_BG, C_POST, C_PMLP, C_QMLP, C_FIN = 0, 8, 12, 28, 36, 44, 52
N_ROWS1 = 60
L_MIX, L_GQ, L_GKV, L_BDW, L_GLN, L_BLN, L_FFN, L_BFF = 0, 8, 11, 13, 17, 21, 25, 33
N_ROWS2 = 77
L_TAP, L_FTAP = 128, 256
N_COLS2 = L_FTAP + 3 * 2 * F2T

N_PAIR = 0
N_SB0 = N_PAIR + PAIRS * 2 * KT
N_MIX = N_SB0 + HT
N_PB0 = N_MIX + 1
N_SB1 = N_PB0 + HT
N_PB1 = N_SB1 + HT
N_OUT = N_PB1 + HT
N_UP = N_OUT + 2 * KT
N_DOWN = N_UP + F1G * KT
N_END1 = N_DOWN + 2 * F1T
M_A = 0
M_G = M_A + KT
M_Q = M_G + KT
M_KV = M_Q + KT
M_PAIR = M_KV + KT
M_WO = M_PAIR + PAIRS * SLOTS
M_UP = M_WO + 2 * KT
M_DOWN = M_UP + F2G * KT
M_END = M_DOWN + 2 * F2T

KV_COLS = KVL + 2 * RD


def pieces2(n):
    if M_KV <= n < M_PAIR or M_PAIR <= n < M_WO and (n - M_PAIR) % SLOTS < QT:
        return 3
    return 1


def width2(n):
    if M_Q <= n < M_KV:
        return QL
    if M_KV <= n < M_PAIR:
        return KV_COLS
    if M_PAIR <= n < M_WO and (n - M_PAIR) % SLOTS < QT:
        return 2 * P
    return CW


def landed2(n):
    return 16 * sum(pieces2(m) for m in range(n % SLOTS, n + 1, SLOTS))


def two_blocks(nc, x, g_pre_mix, w_in, w_pool_mix, pool_scale, w_br_pool, w_br_sb, w_gate, b_gate,
               w_out, g_post_mix, g_pre_mlp, w_up, w_down, g_post_mlp, positions, g_mix, w_in2,
               g_q, w_uq, g_kv, w_ukv, w_dw_conv, b_dw_conv, g_conv_ln, b_conv_ln, w_o, g_ffn,
               w_up2, w_dw_ffn, b_dw_ffn, w_down2, g_final, shape_consts, out):
    with ExitStack() as ctx:
        def sb(name, shape, dt=F32):
            return ctx.enter_context(nc.sbuf_tensor(name, shape, dt))

        sems = []

        def sem(name):
            s = ctx.enter_context(nc.semaphore(name))
            sems.append(s)
            return s

        def sem1(name):
            return ctx.enter_context(nc.semaphore(name))

        x_v = x.rearrange("b (t p) d -> p (b t) d", p=P)
        out_v = out.rearrange("b (t p) d -> p (b t) d", p=P)
        in_v = w_in.rearrange("(k p) (b i n) -> p k b i n", p=P, b=4, n=P)
        gate_v = w_gate.rearrange("(k p) (i n) -> p k i n", p=P, n=CW)
        sb_v = w_br_sb.rearrange("(k p) (h n) -> p k h n", p=P, n=CW)
        pb_v = w_br_pool.rearrange("(k p) (h n) -> p k h n", p=P, n=CW)
        mix_v = w_pool_mix.rearrange("g c d -> c g d")
        out_w_v = w_out.rearrange("(k p) (h n) -> p k h n", p=P, n=CW)
        up_v = w_up.rearrange("(k p) (g n) -> p k g n", p=P, n=CW)
        down_v = w_down.rearrange("(k p) (h n) -> p k h n", p=P, n=CW)
        in2_v = w_in2.rearrange("l (k p) c -> l p k c", p=P)
        uq_v = w_uq.rearrange("l (k p) (i h c) -> l p k i h c", p=P, h=2, c=ND + RD)
        ukv_v = w_ukv.rearrange("l (k p) (i n) -> l p k i n", p=P, n=4 * ND)
        wo_v = w_o.rearrange("l (k p) (h n) -> l p k h n", p=P, n=CW)
        up2_v = w_up2.rearrange("l (k p) (v g n) -> l p k v g n", p=P, v=2, n=256)
        down2_v = w_down2.rearrange("l (k p) (h n) -> l p k h n", p=P, n=CW)

        x_t = sb("x_t", [P, KT, S])
        h_hi = sb("h_hi", [P, KT, S], F32R)
        h_lo = sb("h_lo", [P, KT, S], F32R)
        w_raw = sb("w_raw", [P, SLOTS, CW])
        w_hi = sb("w_hi", [P, SLOTS, CW], F32R)
        w_lo = sb("w_lo", [P, SLOTS, CW], F32R)
        arena = sb("arena", [P, 32, S])
        split = sb("split", [P, 21, S], F32R)
        ident = sb("ident", [P, P])
        ones = sb("ones", [P, P])
        tri = sb("tri", [P, 2, P], F32R)
        cols1 = sb("cols1", [P, N_ROWS1])
        cols_all = sb("cols_all", [P, DEPTH2, N_COLS2])
        cols2 = sb("cols2", [P, N_COLS2])
        later = cols2[:, 0:2 * P]
        consts = sb("consts", [P, 4 + LEFT])
        trig = sb("trig", [P, S])
        sq = sb("sq", [P, 4, S])
        tri_f = sq[:, 3, 0:2 * P].rearrange("p (a n) -> p a n", a=2)
        ssum = sb("ssum", [P, S])
        var = sb("var", [P, S])
        rs0 = sb("rs0", [P, S])
        rs1 = sb("rs1", [P, S])
        rstd = sb("rstd", [P, 2, S])
        soft = sb("soft", [P, 4, 4])

        x_in = arena[:, 0:8, :].rearrange("p (t a) n -> p t (a n)", t=TT)
        pos_i = arena[:, 8, :].bitcast(I32)
        ang, turns, pos_f = arena[:, 9, :], arena[:, 10, :], arena[:, 11, :]
        hf = arena[:, 12:14, :]
        rows1 = arena[0:N_ROWS1, 14, 0:P]
        rows2 = [arena[0:N_ROWS2, 15, n * P:n * P + P] for n in range(DEPTH2)]
        rows_tap = [arena[0:CONV_K, 16 + n, :] for n in range(DEPTH2)]
        rows_ftap = [arena[0:2 * F2T, 18 + n, 0:3 * P].rearrange("p (k n) -> p k n", k=3) for n in range(DEPTH2)]
        arena_flat = arena[:, :, :].rearrange("p a n -> p (a n)")
        u_pad = arena_flat[:, 0:HT * (LEFT + S)].rearrange("p (g n) -> p g n", g=HT)
        gates = arena[:, 5:21, :]
        o_f = arena[:, 21:25, :]
        la = arena[:, 25:27, :]
        sp = arena[:, 27:29, :]
        at = arena[:, 29:31, :]
        wsum = arena_flat[:, 25 * S:25 * S + 2 * (LEFT + S)].rearrange("p (a n) -> p a n", a=2)
        pooled = arena[:, 28:30, :]
        head16 = arena[:, 30, 0:LEFT]
        t_sb = arena[:, 21:25, :]
        t_pb = arena[:, 25:27, :]
        merged = arena[:, 27:29, :]
        mixg = arena[:, 0:8, :]
        xinc = arena[:, 8:12, :]
        act1 = arena
        relu = sq

        split_flat = split[:, :, :].rearrange("p a n -> p (a n)")
        q_hi, q_lo, k_hi, k_lo, v_hi, v_lo = (split[:, n, :] for n in range(6))
        l_hi = split_flat[:, 6 * S:6 * S + 2 * L_ALL].rearrange("p (h n) -> p h n", h=2)
        l_lo = split_flat[:, 6 * S + 2 * L_ALL:6 * S + 4 * L_ALL].rearrange("p (h n) -> p h n", h=2)
        at_hi, at_lo = split[:, 17:19, :], split[:, 19:21, :]
        v_f = arena[:, 31, :]
        o_hi, o_lo = split[:, 6:10, :], split[:, 10:14, :]
        pool_hi, pool_lo = split[:, 0:4, :], split[:, 14:18, :]
        as_hi, as_lo = split[:, 0:2, :], split[:, 2:4, :]

        ckv_f = arena[:, 0:2, :]
        cq_f = arena[:, 2:5, :]
        af = arena[:, 5:9, :]
        gf = arena[:, 9:13, :]
        o2_f = arena[:, 9:13, :]
        CPAD = S + 2 * HALO
        upad = arena_flat[:, 13 * S:13 * S + 4 * CPAD].rearrange("p (j n) -> p j n", j=4)
        conv = arena[:, 18:22, :]
        conv_odd = (arena[:, 22, :], arena[:, 8, :])
        prob = arena[:, 23:27, :]
        qf = arena[:, 27:29, :]
        krf = arena[:, 5, :]
        vt_f = arena[:, 5, :]
        rot = arena[:, 6:8, :]
        prod = arena[:, 29:32, :]
        conv_pool = sq[:, 3, :]
        un = arena[:, 0:4, :]
        lat_hi, lat_lo = split[:, 0:5, :], split[:, 5:10, :]
        vv_hi, vv_lo = split[:, 18, :], split[:, 19, :]
        kq_hi, kq_lo = ([[h[:, 2 * q + hd, :] for hd in range(2)] for q in range(2)] for h in (h_hi, h_lo))
        kk_hi, kk_lo = ([[h[:, 4 + 2 * q + hd, :] for hd in range(2)] for q in range(2)] for h in (h_hi, h_lo))
        O_TILES, C_TILES = (0, 1, 4, 5), (2, 3, 6, 7)
        pt_hi, pt_lo = split[:, 10:14, :], split[:, 14:18, :]
        act2 = arena
        ZPAD = S + 2
        zp = arena_flat[:, 22 * S:22 * S + 4 * ZPAD].rearrange("p (j n) -> p j n", j=4)
        cz = arena[:, 27:31, :]
        yfin = arena[:, 0:8, :]
        y_out = arena[:, 8:16, :].rearrange("p (t a) n -> p t (a n)", t=TT)

        bank_a = ctx.enter_context(nc.psum_tensor("bank_a", [P, 4, S], F32))
        bank_b = ctx.enter_context(nc.psum_tensor("bank_b", [P, 4, S], F32))
        sets = (bank_a, bank_b)
        s_banks = (bank_a[:, 2, :], bank_a[:, 3, :])
        first_banks = ((bank_a[:, 0, :], bank_a[:, 1, :]), (bank_a[:, 2, :], bank_a[:, 3, :]), bank_b[:, 0, :])
        next_banks = ((bank_b[:, 2, :], bank_b[:, 3, :]), (bank_b[:, 0, :], bank_b[:, 2, :]), bank_b[:, 0, :])

        x_land = [ctx.enter_context(nc.semaphore(f"x_land{t}")) for t in range(TT)]
        rows1_land = ctx.enter_context(nc.semaphore("rows1_land"))
        rows2_land = ctx.enter_context(nc.semaphore("rows2_land"))
        pos_land = ctx.enter_context(nc.semaphore("pos_land"))
        consts_made = ctx.enter_context(nc.semaphore("consts_made"))
        tri_made = ctx.enter_context(nc.semaphore("tri_made"))
        trig_step = ctx.enter_context(nc.semaphore("trig_step"))
        trig_sin = ctx.enter_context(nc.semaphore("trig_sin"))
        seg_done = ctx.enter_context(nc.semaphore("seg_done"))
        seg_quiet = ctx.enter_context(nc.semaphore("seg_quiet"))
        seg_open = ctx.enter_context(nc.semaphore("seg_open"))
        y_stored = ctx.enter_context(nc.semaphore("y_stored"))

        w_land = [sem1(f"w_land{s}") for s in range(SLOTS)]
        w_round = sem("w_round")
        w_split = sem("w_split")
        w_used = sem("w_used")
        xt_made = sem1("xt_made")
        xt_out = sem1("xt_out")
        xt_out_b = sem1("xt_out_b")
        cols_zero = sem1("cols_zero")
        cols_made = sem1("cols_made")
        cols_out = sem("cols_out")
        sq_ready = sem("sq_ready")
        sq_added = sem("sq_added")
        stat_ready = sem("stat_ready")
        var_ready = sem("var_ready")
        ln_ready = sem("ln_ready")
        guess_ready = sem("guess_ready")
        newton = sem("newton")
        rstd_ready = sem("rstd_ready")
        hf_ready = sem1("hf_ready")
        h_round = sem1("h_round")
        h_ready = sem1("h_ready")
        stage_round = sem1("stage_round")
        stage_ready = sem1("stage_ready")
        u_out = sem1("u_out")
        v_out = sem1("v_out")
        vt_made = sem1("vt_made")
        z_ready = sem1("z_ready")
        soft_step = sem1("soft_step")
        soft_ready = sem1("soft_ready")
        sp_step = sem1("sp_step")
        l_round = sem1("l_round")
        l_ready = sem1("l_ready")
        c_ready = sem1("c_ready")
        attn_exp = sem1("attn_exp")
        attn_masked = sem1("attn_masked")
        attn_round = sem1("attn_round")
        attn_ready = sem1("attn_ready")
        av_done = sem1("av_done")
        o_out = sem1("o_out")
        gate_out = sem1("gate_out")
        gate_ready = sem1("gate_ready")
        o_round = sem("o_round")
        o_split = sem("o_split")
        pool_step = sem1("pool_step")
        pool_ready = sem1("pool_ready")
        pool_round = sem1("pool_round")
        pool_split = sem1("pool_split")
        y_round = sem1("y_round")
        y_ready = sem1("y_ready")
        sb_out = sem1("sb_out")
        pb_out = sem1("pb_out")
        merge_ready = sem1("merge_ready")
        merge_round = sem1("merge_round")
        merge_split = sem1("merge_split")
        mix_out = sem1("mix_out")
        xinc_ready = sem1("xinc_ready")
        x_new = sem("x_new")
        x_new_p = sem1("x_new_p")
        xg_round = sem("xg_round")
        xg_ready = sem("xg_ready")
        r2_ready = sem1("r2_ready")
        relu_out = sem1("relu_out")
        relu_sq = sem1("relu_sq")
        a_ready = sem("a_ready")
        as_round = sem("as_round")
        as_ready = sem("as_ready")

        proj_out = sem("proj_out")
        cn_ready = sem("cn_ready")
        kr_step = sem("kr_step")
        kr_round = sem("kr_round")
        kr_ready = sem("kr_ready")
        glu_sig = sem("glu_sig")
        u_ready = sem("u_ready")
        pad_zero = sem("pad_zero")
        lat_round = sem("lat_round")
        lat_ready = sem("lat_ready")
        q_made = sem("q_made")
        qk_round = sem("qk_round")
        qk_ready = sem("qk_ready")
        s_ready = sem("s_ready")
        mx_step = sem("mx_step")
        p_exp = sem("p_exp")
        p_step = sem("p_step")
        p_ready = sem("p_ready")
        pt_made = sem("pt_made")
        pt_round = sem("pt_round")
        pt_ready = sem("pt_ready")
        pv_done = sem("pv_done")
        o2_out = sem("o2_out")
        tap_done = sem("tap_done")
        prod_ready = sem("prod_ready")
        prod_used = sem("prod_used")
        conv_sum = sem("conv_sum")
        k_done = sem("k_done")
        vt_out = sem("vt_out")
        v_turned = sem("v_turned")
        conv_ready = sem("conv_ready")
        mean_ready = sem("mean_ready")
        dev_ready = sem("dev_ready")
        ln_out = sem("ln_out")
        silu_ready = sem("silu_ready")
        cu_round = sem("cu_round")
        cu_ready = sem("cu_ready")
        zp_zero = sem("zp_zero")
        z_out = sem("z_out")
        z_mid = sem("z_mid")
        z_tap = sem("z_tap")
        z_conv = sem("z_conv")
        z_silu = sem("z_silu")
        y_made = sem("y_made")
        yt_made = sem("yt_made")
        yt_out = sem("yt_out")
        yt_out_b = sem("yt_out_b")

        block = ctx.enter_context(nc.Block())

        def meet(eng, number):
            eng.drain().then_inc(seg_done, 1)
            eng.wait_ge(seg_open, number + 1)

        @block.sync
        def _(sp_):
            def load1(n, src, i=0, per=0):
                dst = w_raw[:, n % SLOTS, :]
                if len(src.shape) == 3:
                    dst = dst.rearrange("p (a b) -> p a b", a=src.shape[1])
                if n >= SLOTS:
                    sp_.wait_ge(w_split, i * per + (n - SLOTS + 1))
                sp_.dma_start(dst, src).then_inc(w_land[n % SLOTS], 16)

            for t in range(TT):
                sp_.dma_start(x_in[:, t, :], x_v[:, t, :]).then_inc(x_land[t], 16)
            for k in range(SLOTS):
                sp_.dma_start(w_raw[:, k, :].rearrange("p (b n) -> p b n", b=4),
                              in_v[:, k, :, 0, :]).then_inc(w_land[k], 16)
            at_row = 0
            for vec in (g_pre_mix, pool_scale, b_gate, g_post_mix, g_pre_mlp, g_post_mlp, g_final):
                rows = vec.shape[0] // P
                sp_.dma_start(rows1[at_row:at_row + rows, :],
                              vec.rearrange("(r p) -> r p", p=P)).then_inc(rows1_land, 16)
                at_row += rows
            sp_.dma_start(consts[:, :], shape_consts).then_inc(pos_land, 16)
            sp_.dma_start(pos_i, positions.broadcast_to((P, S))).then_inc(pos_land, 16)

            def load_rows2(layer):
                r = 0
                for vec in (g_mix, g_q, g_kv, b_dw_conv, g_conv_ln, b_conv_ln, g_ffn, b_dw_ffn):
                    rows = vec.shape[1] // P
                    sp_.dma_start(rows2[layer][r:r + rows, :],
                                  vec[layer].rearrange("(r p) -> r p", p=P)).then_inc(rows2_land, 16)
                    r += rows
                sp_.dma_start(rows_tap[layer], w_dw_conv[layer]).then_inc(rows2_land, 16)
                sp_.dma_start(rows_ftap[layer],
                              w_dw_ffn[layer].rearrange("k (t p) -> t k p", p=P)).then_inc(rows2_land, 16)

            for layer in range(DEPTH2):
                load_rows2(layer)
            for k in range(SLOTS, KT):
                load1(N_PAIR + k, in_v[:, k, :, 0, :])
            for k in range(KT):
                load1(N_PAIR + KT + k, gate_v[:, k, 0, :])
            with sp_.Fori(1, PAIRS) as i:
                for k in range(KT):
                    sp_.wait_ge(w_split, i * (2 * KT) + (k - SLOTS + 1))
                    sp_.dma_start(w_raw[:, k % SLOTS, :].rearrange("p (b n) -> p b n", b=4),
                                  in_v[:, k, :, i, :]).then_inc(w_land[k % SLOTS], 16)
                for k in range(KT):
                    sp_.wait_ge(w_split, i * (2 * KT) + (KT + k - SLOTS + 1))
                    sp_.dma_start(w_raw[:, k % SLOTS, :], gate_v[:, k, i, :]).then_inc(w_land[k % SLOTS], 16)
            for k in range(HT):
                load1(N_SB0 + k, sb_v[:, k, 0, :])
            load1(N_MIX, mix_v)
            for k in range(HT):
                load1(N_PB0 + k, pb_v[:, k, 0, :])
            for k in range(HT):
                load1(N_SB1 + k, sb_v[:, k, 1, :])
            for k in range(HT):
                load1(N_PB1 + k, pb_v[:, k, 1, :])
            for half in range(2):
                for k in range(KT):
                    load1(N_OUT + half * KT + k, out_w_v[:, k, half, :])
            with sp_.Fori(0, F1G) as g:
                for k in range(KT):
                    load1(N_UP + k, up_v[:, k, g, :], g, KT)
            with sp_.Fori(0, F1T // 2) as kk:
                for k in range(2):
                    for half in range(2):
                        load1(N_DOWN + 2 * k + half,
                              down_v.rearrange("p (kk two) h n -> p kk two h n", two=2)[:, kk, k, half, :],
                              kk, 4)

            def quiet(engines):
                sp_.wait_ge(seg_done, engines)
                sp_.sem_inc(seg_quiet, 1)
                for s in w_land:
                    sp_.sem_clear(s)

            def reopen():
                for s in sems:
                    sp_.sem_clear(s)
                sp_.sem_inc(seg_open, 1)

            quiet(4)

            with sp_.Fori(0, DEPTH2) as l:
                def load2(n, parts, i=0, per=0):
                    if n >= SLOTS:
                        sp_.wait_ge(w_split, i * per + (n - SLOTS + 1))
                    for dst, src in parts:
                        sp_.dma_start(dst, src).then_inc(w_land[n % SLOTS], 16)

                for part in range(2):
                    c0 = QL + KVL + RD + part * CW
                    for k in range(KT):
                        n = M_A + part * KT + k
                        load2(n, [(w_raw[:, n % SLOTS, :], in2_v[l, :, k, c0:c0 + CW])])
                        if n == SLOTS - 1:
                            reopen()
                for k in range(KT):
                    n = M_Q + k
                    load2(n, [(w_raw[:, n % SLOTS, 0:QL], in2_v[l, :, k, 0:QL])])
                for k in range(KT):
                    n = M_KV + k
                    slot = w_raw[:, n % SLOTS, :]
                    r0 = QL + KVL
                    load2(n, [(slot[:, 0:KVL + RD], in2_v[l, :, k, QL:r0 + RD]),
                              (slot[:, KVL + RD:KVL + RD + RD // 2], in2_v[l, :, k, r0 + RD // 2:r0 + RD]),
                              (slot[:, KVL + RD + RD // 2:KV_COLS], in2_v[l, :, k, r0:r0 + RD // 2])])
                for i in range(PAIRS):
                    for k in range(QT):
                        n = M_PAIR + i * SLOTS + k
                        slot = w_raw[:, n % SLOTS, 0:2 * P].rearrange("p (h c) -> p h c", h=2)
                        load2(n, [(slot[:, :, 0:ND + RD], uq_v[l, :, k, i, :, :]),
                                  (slot[:, :, ND + RD:ND + RD + RD // 2], uq_v[l, :, k, i, :, ND + RD // 2:ND + RD]),
                                  (slot[:, :, ND + RD + RD // 2:P], uq_v[l, :, k, i, :, ND:ND + RD // 2])])
                    n = M_PAIR + i * SLOTS + QT
                    load2(n, [(w_raw[:, n % SLOTS, :].rearrange("p (k c) -> p k c", k=KVT), ukv_v[l, :, :, i, :])])
                for half in range(2):
                    for k in range(KT):
                        n = M_WO + half * KT + k
                        load2(n, [(w_raw[:, n % SLOTS, :], wo_v[l, :, k, half, :])])
                with sp_.Fori(0, F2G) as g:
                    for k in range(KT):
                        n = M_UP + k
                        load2(n, [(w_raw[:, n % SLOTS, :].rearrange("p (v c) -> p v c", v=2), up2_v[l, :, k, :, g, :])],
                              g, KT)
                d2 = down2_v.rearrange("l p (kk two) h n -> l p kk two h n", two=2)
                with sp_.Fori(0, F2T // 2) as kk:
                    for k in range(2):
                        for half in range(2):
                            n = M_DOWN + 2 * k + half
                            load2(n, [(w_raw[:, n % SLOTS, :], d2[l, :, kk, k, half, :])], kk, 4)
                quiet(l * 4 + 8)

            reopen()
            for t in range(TT):
                sp_.wait_ge(yt_out, t + 1)
                sp_.wait_ge(yt_out_b, t + 1)
                sp_.dma_start(out_v[:, t, :], y_out[:, t, :]).then_inc(y_stored, 16)
            sp_.wait_ge(y_stored, 16 * TT)

        @block.gpsimd
        def _(pool):
            steps = 0

            def made(ins):
                nonlocal steps
                steps += 1
                ins.then_inc(consts_made, 1)
                pool.wait_ge(consts_made, steps)

            made(nc.gpsimd.memset(ident[:, :], 0.0))
            made(nc.gpsimd.affine_select(out=ident[:, :], in_=ident[:, :], compare_op=ALU.not_equal, fill=1.0,
                                         base=0, pattern=[[-1, P]], channel_multiplier=1))
            made(nc.gpsimd.memset(ones[:, :], 1.0))
            made(nc.gpsimd.memset(tri_f, -1.0))
            made(nc.gpsimd.affine_select(out=tri_f[:, 0, :], in_=tri_f[:, 0, :], compare_op=ALU.is_ge, fill=0.0,
                                         base=0, pattern=[[-1, P]], channel_multiplier=1))
            made(nc.gpsimd.memset(later, 1.0))
            made(nc.gpsimd.affine_select(out=later, in_=later, compare_op=ALU.is_gt, fill=0.0,
                                         base=-P, pattern=[[1, 2 * P]], channel_multiplier=-1))

            def add_squares(count, before_sq, before_add, before_stat):
                for t in range(1, count):
                    pool.wait_ge(sq_ready, before_sq + t + 1)
                    if t == 1 and before_stat:
                        pool.wait_ge(stat_ready, before_stat)
                    if t > 1:
                        pool.wait_ge(sq_added, before_add + t - 1)
                    nc.gpsimd.tensor_tensor(ssum[:, :], sq[:, 0, :] if t == 1 else ssum[:, :], sq[:, t % 4, :],
                                            ALU.add).then_inc(sq_added, 1)

            def x_update(turn):
                for f in range(1, KT, 2):
                    pool.wait_ge(xinc_ready, turn * KT + f + 1)
                    nc.gpsimd.tensor_tensor(x_t[:, f, :], x_t[:, f, :], xinc[:, f % 4, :], ALU.add).then_inc(x_new_p, 1)

            x_update(0)
            add_squares(KT, 2 * KT, 2 * (KT - 1), 2)
            x_update(1)
            pool.wait_ge(x_new_p, KT)
            meet(pool, 0)
            with pool.Fori(0, DEPTH2) as l:
                add_squares(KT, 0, 0, 0)
                for i in range(HT):
                    for r in range(1, POOL_TAPS):
                        pool.wait_ge(prod_ready, i * POOL_TAPS + r + 1)
                        if i > 0 and r == 1:
                            pool.wait_ge(conv_ready, i)
                        if r > 1:
                            pool.wait_ge(prod_used, i * (POOL_TAPS - 1) + r - 1)
                        nc.gpsimd.tensor_tensor(conv_pool, prod[:, i * POOL_TAPS % 3, :] if r == 1 else conv_pool,
                                                prod[:, (i * POOL_TAPS + r) % 3, :], ALU.add).then_inc(prod_used, 1)
                    pool.wait_ge(tap_done, (i + 1) * DVE_TAPS)
                    pool.wait_ge(prod_used, (i + 1) * (POOL_TAPS - 1))
                    nc.gpsimd.tensor_tensor(conv_pool, conv_pool, conv_odd[i % 2], ALU.add).then_inc(conv_sum, 1)
                    pool.wait_ge(conv_sum, i + 1)
                    nc.gpsimd.tensor_tensor(conv[:, i, :], conv[:, i, :], conv_pool, ALU.add).then_inc(conv_ready, 1)
                add_squares(KT, KT + KVT + QT + HT, KT + KVT + QT + HT - 4, 4)
                meet(pool, l + 1)

        @block.scalar
        def _(act):
            def split1(n, i=0, per=0):
                s = n % SLOTS
                act.wait_ge(w_land[s], i * (16 * per // SLOTS) + 16 * (n // SLOTS + 1))
                if n >= SLOTS:
                    act.wait_ge(w_used, i * per + (n - SLOTS + 1))
                nc.scalar.activation(w_hi[:, s, :], w_raw[:, s, :], ACT.Copy).then_inc(w_round, 1)

            def rsqrt_guess(number):
                act.wait_ge(var_ready, number)
                nc.scalar.activation(rs0[:, :], var[:, :], ACT.Ln).then_inc(ln_ready, 1)
                act.wait_ge(ln_ready, number)
                nc.scalar.activation(rs1[:, :], rs0[:, :], ACT.Exp, scale=-0.5).then_inc(guess_ready, 1)

            def square(src, t, before_sq, before_add, on_pe=False):
                if t >= 4:
                    act.wait_ge(sq_added, before_add + (t - 3 if on_pe else max(t - 4, 1)))
                nc.scalar.activation(sq[:, t % 4, :], src, ACT.Square).then_inc(sq_ready, 1)

            act.wait_ge(trig_step, 10)
            nc.scalar.activation(trig[ND:P, :], ang[ND:P, :], ACT.Sin).then_inc(trig_sin, 1)
            act.wait_ge(consts_made, 5)
            nc.scalar.activation(tri[:, :, :], tri_f, ACT.Copy).then_inc(tri_made, 1)
            nc.scalar.preload_act_table_set(LN_EXP)
            for n in range(SLOTS):
                split1(n)
            act.wait_ge(xt_made, 1)
            for f in range(4):
                nc.scalar.activation(x_t[:, f, :], bank_a[:, f, :], ACT.Copy).then_inc(xt_out, 1)
            for f in range(KT):
                if f < 4:
                    act.wait_ge(xt_out, f + 1)
                else:
                    act.wait_ge(xt_out_b, f - 3)
                square(x_t[:, f, :], f, 0, 0)
            rsqrt_guess(1)
            for f in range(KT):
                act.wait_ge(hf_ready, f + 1)
                nc.scalar.activation(h_hi[:, f, :], hf[:, f % 2, :], ACT.Copy).then_inc(h_round, 1)

            with act.Fori(0, PAIRS) as i:
                for k in range(KT):
                    split1(N_PAIR + SLOTS + k, i, 2 * KT)
                act.wait_ge(w_used, i * (2 * KT) + KT)
                nc.scalar.activation(q_hi, bank_a[:, 1, :], ACT.Copy, scale=Q_SCALE).then_inc(stage_round, 1)
                nc.scalar.activation(k_hi, bank_a[:, 2, :], ACT.Copy).then_inc(stage_round, 1)
                nc.scalar.activation(u_pad[:, i, LEFT:LEFT + S], bank_a[:, 0, :], ACT.Copy).then_inc(u_out, 1)
                nc.scalar.activation(v_f, bank_a[:, 3, :], ACT.Copy).then_inc(v_out, 1)
                act.wait_ge(vt_made, i + 1)
                nc.scalar.activation(v_hi, bank_a[:, 3, :], ACT.Copy).then_inc(stage_round, 1)
                for s in range(9):
                    if s < 8:
                        split1(N_PAIR + SLOTS + KT + s, i, 2 * KT)
                        kb = 3 - s % 4
                        n = S - Q0[kb]
                        z = bank_a[:, s % 2, 0:n]
                        act.wait_ge(z_ready, i * 8 + (s + 1))
                        nc.scalar.activation(la[:, s % 2, 0:n], z, ACT.Abs).then_inc(soft_step, 1)
                        act.wait_ge(soft_step, i * 16 + (2 * s + 1))
                        nc.scalar.activation(la[:, s % 2, 0:n], la[:, s % 2, 0:n], ACT.Exp, scale=-1.0).then_inc(soft_step, 1)
                        act.wait_ge(soft_step, i * 16 + (2 * s + 2))
                        nc.scalar.activation(la[:, s % 2, 0:n], la[:, s % 2, 0:n], ACT.Ln, bias=1.0).then_inc(soft_ready, 1)
                    if s >= 1:
                        kb1 = 3 - (s - 1) % 4
                        n1 = S - Q0[kb1]
                        act.wait_ge(c_ready, i * 8 + s)
                        nc.scalar.activation(at[:, (s - 1) % 2, 0:n1], bank_a[:, (s - 1) % 2, 0:n1], ACT.Exp).then_inc(attn_exp, 1)
                    if s < 8:
                        act.wait_ge(sp_step, i * 16 + (2 * s + 2))
                        off = L_OFF[kb]
                        nc.scalar.activation(l_hi[:, s // 4, off:off + n], sp[:, s % 2, 0:n], ACT.Copy).then_inc(l_round, 1)
                    if s >= 1:
                        act.wait_ge(attn_masked, i * 8 + s)
                        if s >= 3:
                            act.wait_ge(av_done, i * 8 + (s - 2))
                        nc.scalar.activation(at_hi[:, (s - 1) % 2, 0:n1], at[:, (s - 1) % 2, 0:n1], ACT.Copy).then_inc(attn_round, 1)
                    if s == 5 or s == 8:
                        hd = 0 if s == 5 else 1
                        rows = slice(HEAD * hd, HEAD * hd + HEAD)
                        act.wait_ge(av_done, i * 8 + 4 * (hd + 1))
                        nc.scalar.activation(o_f[rows, i, :], bank_a[rows, 2 + hd, :], ACT.Copy).then_inc(o_out, 1)
                act.wait_ge(w_used, i * (2 * KT) + 2 * KT)
                for j in range(4):
                    nc.scalar.activation(gates[:, i * 4 + j, :], bank_b[:, j, :], ACT.Identity,
                                         bias=cols1[:, bass.ds(i * 4 + (C_BG + j), 1)]).then_inc(gate_out, 1)

            act.wait_ge(o_out, 2 * PAIRS)
            for t in range(HT):
                nc.scalar.activation(o_hi[:, t, :], o_f[:, t, :], ACT.Copy).then_inc(o_round, 1)
            act.wait_ge(gate_out, 16)

            def sigmoid_gates(q):
                nc.scalar.activation(gates[:, 4 * q:4 * q + 4, :], gates[:, 4 * q:4 * q + 4, :],
                                     ACT.Sigmoid).then_inc(gate_ready, 1)

            def pool_hi_of(g):
                act.wait_ge(pool_ready, g + 1)
                nc.scalar.activation(pool_hi[:, g, :], pooled[:, g % 2, :], ACT.Copy).then_inc(pool_round, 1)

            sigmoid_gates(2)
            split1(N_MIX)
            pool_hi_of(0)
            pool_hi_of(1)
            split1(N_PB0)
            pool_hi_of(2)
            split1(N_PB0 + 1)
            pool_hi_of(3)
            split1(N_PB0 + 2)
            sigmoid_gates(0)
            split1(N_PB0 + 3)
            act.wait_ge(w_used, N_MIX + 1)
            for g in range(HT):
                nc.scalar.activation(h_hi[:, HT + g, :], bank_b[:, g, :], ACT.Copy,
                                     scale=cols1[:, C_PSC + g:C_PSC + g + 1]).then_inc(y_round, 1)
            sigmoid_gates(3)
            sigmoid_gates(1)

            def merge_hi(half):
                for j in range(4):
                    act.wait_ge(merge_ready, 4 * half + j + 1)
                    nc.scalar.activation(h_hi[:, 4 * half + j, :], merged[:, j % 2, :], ACT.Copy).then_inc(merge_round, 1)

            for k in range(HT):
                split1(N_SB1 + k)
            merge_hi(0)
            for k in range(HT):
                split1(N_PB1 + k)
            for k in range(HT):
                split1(N_OUT + k)
            act.wait_ge(w_used, N_PB1 + HT)
            merge_hi(1)
            for k in range(N_OUT + SLOTS, N_OUT + KT + SLOTS):
                split1(k)
            nc.scalar.preload_act_table_set(LN_EXP)

            def post_squares(last_chunk, tiles, before_sq, before_add):
                act.wait_ge(w_used, last_chunk + 1)
                for f in tiles:
                    square(sets[f // 4][:, f % 4, :], f, before_sq, before_add, True)

            post_squares(N_OUT + KT - 1, range(4), KT, KT - 1)
            for k in range(N_OUT + KT + SLOTS, N_UP + SLOTS):
                split1(k)
            post_squares(N_UP - 1, range(4, 8), KT, KT - 1)
            rsqrt_guess(2)
            for f in range(KT):
                act.wait_ge(x_new_p if f % 2 else x_new, f // 2 + 1)
                nc.scalar.activation(h_hi[:, f, :], x_t[:, f, :], ACT.Copy,
                                     scale=cols1[:, C_PMLP + f:C_PMLP + f + 1]).then_inc(xg_round, 1)
                square(x_t[:, f, :], f, 2 * KT, 2 * (KT - 1))

            def up1_out(g, i=0, gper=0):
                set_ = sets[g % 2]
                act.wait_ge(w_used, i * (gper * KT) + (N_UP + g * KT + KT))
                for j in range(4):
                    t = 4 * g + j
                    if t >= 4:
                        act.wait_ge(a_ready, i * (4 * gper) + (t - 3))
                    nc.scalar.activation(relu[:, j, :], set_[:, j, :], ACT.Relu).then_inc(relu_out, 1)
                split1(N_UP + SLOTS + (1 + g) * KT, i, gper * KT)
                for j in range(4):
                    t = 4 * g + j
                    act.wait_ge(relu_out, i * (4 * gper) + (t + 1))
                    nc.scalar.activation(relu[:, j, :], relu[:, j, :], ACT.Square).then_inc(relu_sq, 1)
                for k in range(1, 4):
                    split1(N_UP + SLOTS + (1 + g) * KT + k, i, gper * KT)

            for k in range(KT):
                split1(N_UP + SLOTS + k)
            rsqrt_guess(3)
            up1_out(0)
            with act.Fori(0, F1G // 2 - 1) as i:
                for g in range(1, 3):
                    for k in range(4, KT):
                        split1(N_UP + SLOTS + g * KT + k, i, 2 * KT)
                    up1_out(g, i, 2)
            for k in range(4, KT):
                split1(N_UP + SLOTS + (F1G - 1) * KT + k)

            def act_split(k, n, need_free, i=0):
                act.wait_ge(a_ready, i * 2 + (k + 1))
                if need_free:
                    act.wait_ge(w_used, i * 4 + n)
                nc.scalar.activation(as_hi[:, k % 2, :], act1[:, i * 2 + k, :], ACT.Copy).then_inc(as_round, 1)

            for k in range(2):
                act_split(k, 0, False)
            up1_out(F1G - 1)
            for k in range(2):
                act_split(k + 2, N_DOWN + 2 * k + 2, True)
            with act.Fori(0, F1T // 2 - 2) as kk:
                for k in range(2):
                    split1(N_DOWN + 2 * SLOTS + 2 * k, kk, 4)
                    split1(N_DOWN + 2 * SLOTS + 2 * k + 1, kk, 4)
                    act_split(k + 4, N_DOWN + SLOTS + 2 * k + 2, True, kk)
            post_squares(N_END1 - 2, range(4), 3 * KT, 3 * (KT - 1))
            post_squares(N_END1 - 1, range(4, 8), 3 * KT, 3 * (KT - 1))
            rsqrt_guess(4)
            meet(act, 0)

            with act.Fori(0, DEPTH2) as l:
                def split2(n, i=0, per=0):
                    s, c = n % SLOTS, width2(n)
                    act.wait_ge(w_land[s], i * (16 * pieces2(n) * per // SLOTS) + landed2(n))
                    if n >= SLOTS:
                        act.wait_ge(w_used, i * per + (n - SLOTS + 1))
                    nc.scalar.activation(w_hi[:, s, 0:c], w_raw[:, s, 0:c], ACT.Copy).then_inc(w_round, 1)

                act.wait_ge(cols_out, 1)
                for f in range(KT):
                    nc.scalar.activation(h_hi[:, f, :], x_t[:, f, :], ACT.Copy,
                                         scale=cols2[:, L_MIX + f:L_MIX + f + 1]).then_inc(xg_round, 1)
                    if f < SLOTS:
                        split2(f)
                for f in range(KT):
                    square(x_t[:, f, :], f, 0, 0)
                    if f >= 4:
                        split2(M_A + f)
                for k in range(4, KT):
                    split2(M_A + SLOTS + k)
                rsqrt_guess(1)
                for k in range(KT):
                    split2(M_G + SLOTS + k)
                for j in range(4):
                    act.wait_ge(proj_out, 4 + j + 1)
                    nc.scalar.activation(gf[:, j, :], gf[:, j, :], ACT.Sigmoid).then_inc(glu_sig, 1)
                nc.scalar.preload_act_table_set(LN_EXP)
                prods = 0

                def products(count):
                    nonlocal prods
                    for n in range(prods, min(prods + count, HT * POOL_TAPS)):
                        i, r = n // POOL_TAPS, n % POOL_TAPS
                        if r == 0:
                            act.wait_ge(u_ready, i + 1)
                            act.wait_ge(pad_zero, 2)
                        if n >= 3:
                            i3, r3 = (n - 3) // POOL_TAPS, (n - 3) % POOL_TAPS
                            act.wait_ge(prod_used, i3 * (POOL_TAPS - 1) + max(r3, 1))
                        nc.scalar.activation(prod[:, n % 3, :], upad[:, i, DVE_TAPS + r:DVE_TAPS + r + S], ACT.Copy,
                                             scale=cols2[:, L_TAP + i * 32 + DVE_TAPS + r:L_TAP + i * 32 + DVE_TAPS + r + 1]
                                             ).then_inc(prod_ready, 1)
                        prods += 1

                for k in range(KT):
                    split2(M_Q + SLOTS + k)
                    if k >= 4:
                        products(1)
                for t in range(QT):
                    act.wait_ge(proj_out, 8 + t + 1)
                    square(cq_f[:, t, :], t, KT, KT - 1)
                for k in range(4):
                    split2(M_KV + SLOTS + k)
                    products(1)
                rsqrt_guess(2)
                for k in range(4):
                    split2(M_PAIR + k)
                    products(1)
                for t in range(QT):
                    act.wait_ge(cn_ready, t + 1)
                    nc.scalar.activation(lat_hi[:, t, :], cq_f[:, t, :], ACT.Copy).then_inc(lat_round, 1)
                for t in range(KVT):
                    act.wait_ge(proj_out, 8 + QT + t + 1)
                    square(ckv_f[:, t, :], t, KT + QT, KT + QT - 2)
                rsqrt_guess(3)
                act.wait_ge(kr_step, 4)
                for q in range(2):
                    for hd in range(2):
                        nc.scalar.activation(kk_hi[q][hd][ND:P, :], rot[ND:P, 0, :], ACT.Copy).then_inc(kr_round, 1)
                for t in range(KVT):
                    act.wait_ge(cn_ready, QT + t + 1)
                    nc.scalar.activation(lat_hi[:, QT + t, :], ckv_f[:, t, :], ACT.Copy).then_inc(lat_round, 1)

                def stage_q(i):
                    for hd in range(2):
                        act.wait_ge(q_made, 2 * i + hd + 1)
                        nc.scalar.activation(kq_hi[i % 2][hd], qf[:, hd, :], ACT.Copy).then_inc(qk_round, 1)

                def stage_k(i, hd, bank):
                    if hd == 0:
                        act.wait_ge(k_done, i + 1)
                    else:
                        act.wait_ge(w_used, M_PAIR + (i + 1) * SLOTS)
                    nc.scalar.activation(kk_hi[i % 2][hd][0:ND, :], bank[0:ND, :], ACT.Copy).then_inc(qk_round, 1)
                    nc.scalar.activation(vt_f[hd * ND:hd * ND + ND, :], bank[ND:P, :], ACT.Copy).then_inc(vt_out, 1)

                def stage_v(i, bank):
                    act.wait_ge(v_turned, i + 1)
                    nc.scalar.activation(vv_hi, bank, ACT.Copy).then_inc(qk_round, 1)

                products(2)
                stage_q(0)
                for hd in range(2):
                    stage_k(0, hd, first_banks[1][hd])
                stage_v(0, first_banks[2])
                for k in range(SLOTS):
                    split2(M_PAIR + SLOTS + k)

                def out_of(i, hd):
                    rows = slice(ND * hd, ND * hd + ND)
                    act.wait_ge(pv_done, i * 2 + hd + 1)
                    nc.scalar.activation(o2_f[rows, i, :], bank_b[rows, 1, :], ACT.Copy).then_inc(o2_out, 1)

                for g in range(BLOCKS + 2):
                    i, m = g // (2 * TT), g % (2 * TT)
                    if g < BLOCKS:
                        b = g % TT
                        act.wait_ge(mx_step, g + 1)
                        nc.scalar.activation(prob[:, b, :], s_banks[g % 2], ACT.Exp,
                                             bias=soft[:, 1, b:b + 1], accum_out=soft[:, 2, b:b + 1]).then_inc(p_exp, 1)
                    if g >= 2:
                        b = (g - 2) % TT
                        act.wait_ge(pt_made, g - 1)
                        if b == 0 and g >= TT + 2:
                            act.wait_ge(pv_done, (g - 2) // TT)
                        nc.scalar.activation(pt_hi[:, :, b * P:b * P + P],
                                             bank_a[:, g % 2, :].rearrange("p (k q) -> p k q", k=TT),
                                             ACT.Copy).then_inc(pt_round, 1)
                    if m == TT + 2:
                        out_of(i, 0)
                    if m == 2 and i >= 1:
                        out_of(i - 1, 1)
                        if i < PAIRS:
                            stage_v(i, next_banks[2])
                    if i + 1 < PAIRS:
                        if m == 5:
                            stage_q(i + 1)
                            stage_k(i + 1, 0, next_banks[1][0])
                        if m == 6:
                            stage_k(i + 1, 1, next_banks[1][1])
                        if m in (2, 3, 4, 7):
                            split2(M_PAIR + (i + 2) * SLOTS + (2, 3, 4, 7).index(m))
                    elif m in (3, 4, 5) and i < PAIRS:
                        t = m - 3
                        act.wait_ge(o2_out, 2 * t + 2)
                        nc.scalar.activation(h_hi[:, O_TILES[t], :], o2_f[:, t, :], ACT.Copy).then_inc(o_round, 1)
                    products(2)
                out_of(PAIRS - 1, 1)
                products(HT * POOL_TAPS)

                act.wait_ge(o2_out, 2 * PAIRS)
                nc.scalar.activation(h_hi[:, O_TILES[3], :], o2_f[:, 3, :], ACT.Copy).then_inc(o_round, 1)
                split2(M_WO + 4)
                for j in range(HT):
                    act.wait_ge(dev_ready, j + 1)
                    square(conv[:, j, :], j, KT + KVT + QT, KT + KVT + QT - 3)
                for k in range(5, 8):
                    split2(M_WO + k)
                rsqrt_guess(4)
                nc.scalar.preload_act_table(ACT.Silu)
                for j in range(HT):
                    act.wait_ge(ln_out, j + 1)
                    nc.scalar.activation(un[:, j, :], conv[:, j, :], ACT.Silu, scale=cols2[:, L_GLN + j:L_GLN + j + 1],
                                         bias=cols2[:, L_BLN + j:L_BLN + j + 1]).then_inc(silu_ready, 1)
                for j in range(HT):
                    act.wait_ge(silu_ready, j + 1)
                    nc.scalar.activation(h_hi[:, C_TILES[j], :], un[:, j, :], ACT.Copy).then_inc(cu_round, 1)
                nc.scalar.preload_act_table_set(LN_EXP)
                for n in range(M_WO + 8, M_UP + SLOTS):
                    split2(n)
                act.wait_ge(w_used, M_UP)
                for f in range(KT):
                    act.wait_ge(x_new, f + 1)
                    nc.scalar.activation(h_hi[:, f, :], x_t[:, f, :], ACT.Copy,
                                         scale=cols2[:, L_FFN + f:L_FFN + f + 1]).then_inc(xg_round, 1)
                    square(x_t[:, f, :], f, KT + KVT + QT + HT, KT + KVT + QT + HT - 4)

                def mid_and_silu(g, i=0, gper=0):
                    if g:
                        act.wait_ge(a_ready, i * (2 * gper) + 2 * g)
                    for j in range(4):
                        tile = i * (2 * gper) + (2 * g + j % 2 + F2T * (j // 2))
                        act.wait_ge(z_out, i * (4 * gper) + (4 * g + j + 1))
                        nc.scalar.activation(cz[:, j, :], zp[:, j, 1:1 + S], ACT.Identity,
                                             scale=cols2[:, bass.ds(tile + (L_FTAP + 2 * F2T), 1)],
                                             bias=cols2[:, bass.ds(tile + L_BFF, 1)]).then_inc(z_mid, 1)
                    for k in range(2):
                        split2(M_UP + SLOTS + (1 + g) * KT + k, i, gper * KT)
                    for j in range(2):
                        act.wait_ge(z_conv, i * (4 * gper) + (4 * g + j + 1))
                        nc.scalar.activation(cz[:, j, :], cz[:, j, :], ACT.Silu).then_inc(z_silu, 1)
                    for k in range(2, 4):
                        split2(M_UP + SLOTS + (1 + g) * KT + k, i, gper * KT)

                for k in range(KT):
                    split2(M_UP + SLOTS + k)
                rsqrt_guess(5)
                nc.scalar.preload_act_table(ACT.Silu)
                mid_and_silu(0)
                with act.Fori(0, F2G // 2 - 1) as i:
                    for g in range(1, 3):
                        for k in range(4, KT):
                            split2(M_UP + SLOTS + g * KT + k, i, 2 * KT)
                        mid_and_silu(g, i, 2)
                for k in range(4, KT):
                    split2(M_UP + SLOTS + (F2G - 2) * KT + k)
                mid_and_silu(F2G - 2)
                for k in range(4, KT):
                    split2(M_UP + SLOTS + (F2G - 1) * KT + k)

                def act_split2(k, n, need_free, i=0):
                    act.wait_ge(a_ready, i * 2 + (k + 1))
                    if need_free:
                        act.wait_ge(w_used, i * 4 + n)
                    nc.scalar.activation(as_hi[:, k % 2, :], act2[:, i * 2 + k, :], ACT.Copy).then_inc(as_round, 1)

                for k in range(2):
                    act_split2(k, 0, False)
                mid_and_silu(F2G - 1)
                for k in range(2):
                    act_split2(k + 2, M_DOWN + 2 * k + 2, True)
                with act.Fori(0, F2T // 2 - 2) as kk:
                    for k in range(2):
                        split2(M_DOWN + 2 * SLOTS + 2 * k, kk, 4)
                        split2(M_DOWN + 2 * SLOTS + 2 * k + 1, kk, 4)
                        act_split2(k + 4, M_DOWN + SLOTS + 2 * k + 2, True, kk)
                nc.scalar.preload_act_table_set(LN_EXP)
                meet(act, l + 1)

            for f in range(KT):
                square(x_t[:, f, :], f, 0, 0)
            rsqrt_guess(1)
            for t in range(TT):
                act.wait_ge(yt_made, t + 1)
                nc.scalar.activation(y_out[:, t, 0:S], sets[t % 2][:, 2 * (t // 2), :], ACT.Copy).then_inc(yt_out, 1)

        @block.vector
        def _(dve):
            def tt(out_, a, b, op):
                return nc.vector.tensor_tensor(out_, a, b, op)

            def stt(out_, a, s, b, op0, op1):
                return nc.vector.scalar_tensor_tensor(out=out_, in0=a, scalar=s, in1=b, op0=op0, op1=op1)

            def rest(out_, full, hi):
                return tt(out_, full, hi.bitcast(F32), ALU.subtract)

            def split_lo(n, c=CW, i=0, per=0):
                s = n % SLOTS
                dve.wait_ge(w_round, i * per + (n + 1))
                rest(w_lo[:, s, 0:c], w_raw[:, s, 0:c], w_hi[:, s, 0:c]).then_inc(w_split, 1)

            def rstd_of(number, bank, width=D):
                dve.wait_ge(stat_ready, number)
                nc.vector.tensor_scalar(var[:, :], bank, 1.0 / width, EPS, ALU.mult, ALU.add).then_inc(var_ready, 1)
                dve.wait_ge(guess_ready, number)
                tt(rs0[:, :], rs1[:, :], rs1[:, :], ALU.mult).then_inc(newton, 1)
                dve.wait_ge(newton, 2 * number - 1)
                stt(rs0[:, :], rs0[:, :], -0.5, var[:, :], ALU.mult, ALU.mult).then_inc(newton, 1)
                dve.wait_ge(newton, 2 * number)
                stt(rstd[:, number % 2, :], rs0[:, :], 1.5, rs1[:, :], ALU.add, ALU.mult).then_inc(rstd_ready, 1)

            def rstd_into(number, bank, width):
                dve.wait_ge(stat_ready, number)
                nc.vector.tensor_scalar(var[:, :], bank, 1.0 / width, EPS, ALU.mult, ALU.add).then_inc(var_ready, 1)
                dve.wait_ge(guess_ready, number)
                tt(rs0[:, :], rs1[:, :], rs1[:, :], ALU.mult).then_inc(newton, 1)
                dve.wait_ge(newton, 2 * number - 1)
                stt(rs0[:, :], rs0[:, :], -0.5, var[:, :], ALU.mult, ALU.mult).then_inc(newton, 1)
                dve.wait_ge(newton, 2 * number)
                stt(rstd[:, 0, :], rs0[:, :], 1.5, rs1[:, :], ALU.add, ALU.mult).then_inc(rstd_ready, 1)
                dve.wait_ge(rstd_ready, number)

            def add_square(t, before_sq, before_add, before_stat):
                if t == 0:
                    return
                dve.wait_ge(sq_ready, before_sq + t + 1)
                if t == 1 and before_stat:
                    dve.wait_ge(stat_ready, before_stat)
                if t > 1:
                    dve.wait_ge(sq_added, before_add + t - 1)
                tt(ssum[:, :], sq[:, 0, :] if t == 1 else ssum[:, :], sq[:, t % 4, :], ALU.add).then_inc(sq_added, 1)

            dve.wait_ge(pos_land, 32)
            magic = 1.5 * 2.0 ** 23
            two_pi = (6.28125, 0.0019350051879882812, 3.0199159819e-07)
            steps = 0

            def step(ins):
                nonlocal steps
                steps += 1
                ins.then_inc(trig_step, 1)
                dve.wait_ge(trig_step, steps)

            step(nc.vector.tensor_copy(pos_f, pos_i))
            step(nc.vector.tensor_scalar(ang, pos_f, consts[:, 0:1], None, ALU.mult))
            step(nc.vector.tensor_scalar(turns, ang, 1.0 / 6.283185307179586, consts[:, 1:2], ALU.mult, ALU.add))
            step(nc.vector.tensor_scalar(turns, turns, magic, None, ALU.add))
            step(nc.vector.tensor_scalar(turns, turns, -magic, None, ALU.add))
            for part in two_pi:
                step(stt(ang, turns, -part, ang, ALU.mult, ALU.add))
            step(nc.vector.tensor_scalar(ang, ang, consts[:, 2:3], 3.1415925, ALU.add, ALU.min))
            step(nc.vector.tensor_scalar(ang, ang, -3.1415925, None, ALU.max))
            dve.wait_ge(trig_sin, 1)
            nc.vector.tensor_scalar(trig[ND:P, :], trig[ND:P, :], consts[ND:P, 3:4], MLA_SCALE, ALU.mult, ALU.mult).then_inc(trig_step, 1)
            nc.vector.memset(trig[0:ND, :], MLA_SCALE).then_inc(trig_step, 1)

            dve.wait_ge(consts_made, 7)
            dve.wait_ge(xt_made, 2)
            for f in range(4, KT):
                nc.vector.tensor_copy(x_t[:, f, :], bank_b[:, f - 4, :]).then_inc(xt_out_b, 1)
            dve.wait_ge(cols_made, 1)
            nc.vector.tensor_copy(cols1[:, :], bank_a[:, 0, 0:N_ROWS1]).then_inc(cols_out, 1)
            nc.vector.memset(cols_all[:, :, :], 0.0).then_inc(cols_zero, 1)
            dve.wait_ge(cols_zero, 1)
            for n in range(DEPTH2):
                dve.wait_ge(cols_made, n + 2)
                bank, cols = bank_a[:, 1 + n, :], cols_all[:, n, :]
                taps_in, taps_out = (v[:, L_TAP:L_FTAP].rearrange("p (c k) -> p c k", c=HT)[:, :, 0:CONV_K]
                                     for v in (bank, cols))
                nc.vector.tensor_copy(cols[:, 0:N_ROWS2], bank[:, 0:N_ROWS2]).then_inc(cols_out, 1)
                nc.vector.tensor_copy(taps_out, taps_in).then_inc(cols_out, 1)
                nc.vector.tensor_copy(cols[:, L_FTAP:N_COLS2], bank[:, L_FTAP:N_COLS2]).then_inc(cols_out, 1)
            nc.vector.memset(u_pad[:, :, 0:LEFT], 0.0).then_inc(pool_step, 1)
            for n in range(SLOTS):
                split_lo(n)
            for t in range(KT):
                add_square(t, 0, 0, 0)
            rstd_of(1, bank_b[:, 0, :])
            dve.wait_ge(rstd_ready, 1)
            dve.wait_ge(cols_out, 1)
            for f in range(KT + 1):
                if f < KT:
                    if f >= 2:
                        dve.wait_ge(h_ready, f - 1)
                    stt(hf[:, f % 2, :], x_t[:, f, :], cols1[:, C_PRE + f:C_PRE + f + 1], rstd[:, 1, :],
                        ALU.mult, ALU.mult).then_inc(hf_ready, 1)
                if f >= 1:
                    dve.wait_ge(h_round, f)
                    rest(h_lo[:, f - 1, :], hf[:, (f - 1) % 2, :], h_hi[:, f - 1, :]).then_inc(h_ready, 1)

            with dve.Fori(0, PAIRS) as i:
                for k in range(KT):
                    split_lo(N_PAIR + SLOTS + k, CW, i, 2 * KT)
                dve.wait_ge(stage_round, i * 3 + 1)
                stt(q_lo, bank_a[:, 1, :], Q_SCALE, q_hi.bitcast(F32), ALU.mult, ALU.subtract).then_inc(stage_ready, 1)
                dve.wait_ge(stage_round, i * 3 + 2)
                rest(k_lo, bank_a[:, 2, :], k_hi).then_inc(stage_ready, 1)
                dve.wait_ge(stage_round, i * 3 + 3)
                rest(v_lo, bank_a[:, 3, :], v_hi).then_inc(stage_ready, 1)
                for s in range(9):
                    if s < 8:
                        split_lo(N_PAIR + SLOTS + KT + s, CW, i, 2 * KT)
                        kb = 3 - s % 4
                        n = S - Q0[kb]
                        off = L_OFF[kb]
                        d = kb * P - Q0[kb] + P
                        dve.wait_ge(soft_ready, i * 8 + (s + 1))
                        stt(sp[:, s % 2, 0:n], bank_a[:, s % 2, 0:n], 0.0, la[:, s % 2, 0:n],
                            ALU.max, ALU.add).then_inc(sp_step, 1)
                        dve.wait_ge(sp_step, i * 16 + (2 * s + 1))
                        tt(sp[:, s % 2, 0:d], sp[:, s % 2, 0:d], later[:, 2 * P - d:], ALU.mult).then_inc(sp_step, 1)
                    if s >= 1:
                        kb1 = 3 - (s - 1) % 4
                        n1 = S - Q0[kb1]
                        dve.wait_ge(attn_exp, i * 8 + s)
                        d = kb1 * P - Q0[kb1] + P
                        stt(at[:, (s - 1) % 2, 0:d], at[:, (s - 1) % 2, 0:d], BIG, later[:, 2 * P - d:],
                            ALU.min, ALU.mult).then_inc(attn_masked, 1)
                    if s < 8:
                        dve.wait_ge(l_round, i * 8 + (s + 1))
                        rest(l_lo[:, s // 4, off:off + n], sp[:, s % 2, 0:n], l_hi[:, s // 4, off:off + n]).then_inc(l_ready, 1)
                    if s >= 1:
                        dve.wait_ge(attn_round, i * 8 + s)
                        rest(at_lo[:, (s - 1) % 2, 0:n1], at[:, (s - 1) % 2, 0:n1], at_hi[:, (s - 1) % 2, 0:n1]).then_inc(attn_ready, 1)

            for t in range(HT):
                dve.wait_ge(o_round, t + 1)
                rest(o_lo[:, t, :], o_f[:, t, :], o_hi[:, t, :]).then_inc(o_split, 1)
            pool_steps = 1

            def pool_group(g):
                nonlocal pool_steps

                def pstep(ins):
                    nonlocal pool_steps
                    pool_steps += 1
                    ins.then_inc(pool_step, 1)
                    dve.wait_ge(pool_step, pool_steps)

                w = WINDOWS[g]
                src, d, turn = u_pad[:, g, :], 1, 0
                while d < w:
                    lo = LEFT - (w - 2 * d)
                    dst = wsum[:, turn % 2, :]
                    pstep(tt(dst[:, lo:LEFT + S], src[:, lo:LEFT + S], src[:, lo - d:LEFT + S - d], ALU.add))
                    src, d, turn = dst, 2 * d, turn + 1
                if g >= 2:
                    dve.wait_ge(pool_split, g - 1)
                pstep(stt(pooled[:, g % 2, :], src[:, LEFT:LEFT + S], 1.0 / w, u_pad[:, g, LEFT:LEFT + S],
                          ALU.mult, ALU.subtract))
                pstep(tt(head16[:, 0:w], src[:, LEFT:LEFT + w], consts[:, 4:4 + w], ALU.mult))
                tt(pooled[:, g % 2, 0:w], head16[:, 0:w], u_pad[:, g, LEFT:LEFT + w], ALU.subtract).then_inc(pool_ready, 1)

            def pool_lo_of(g):
                dve.wait_ge(pool_round, g + 1)
                rest(pool_lo[:, g, :], pooled[:, g % 2, :], pool_hi[:, g, :]).then_inc(pool_split, 1)

            dve.wait_ge(u_out, PAIRS)
            pool_group(0)
            split_lo(N_MIX)
            pool_lo_of(0)
            pool_group(1)
            pool_lo_of(1)
            split_lo(N_PB0)
            pool_group(2)
            pool_lo_of(2)
            split_lo(N_PB0 + 1)
            pool_group(3)
            pool_lo_of(3)
            split_lo(N_PB0 + 2)

            def attention_gated(half):
                dve.wait_ge(w_used, (N_SB0, N_SB1)[half] + HT)
                dve.wait_ge(gate_ready, (1, 3)[half])
                for j in range(4):
                    tt(t_sb[:, j, :], bank_a[:, j, :], gates[:, 8 + 4 * half + j, :], ALU.mult).then_inc(sb_out, 1)

            def merge(half):
                dve.wait_ge(w_used, (N_PB0, N_PB1)[half] + HT)
                dve.wait_ge(gate_ready, (2, 4)[half])
                for j in range(5):
                    if j < 4:
                        tt(t_pb[:, j % 2, :], bank_b[:, j, :], gates[:, 4 * half + j, :], ALU.mult).then_inc(pb_out, 1)
                    if j >= 1:
                        dve.wait_ge(merge_round, 4 * half + j)
                        rest(h_lo[:, 4 * half + j - 1, :], merged[:, (j - 1) % 2, :],
                             h_hi[:, 4 * half + j - 1, :]).then_inc(merge_split, 1)
                    if j < 4:
                        dve.wait_ge(pb_out, 4 * half + j + 1)
                        dve.wait_ge(sb_out, 4 * half + j + 1)
                        tt(merged[:, j % 2, :], t_pb[:, j % 2, :], t_sb[:, j, :], ALU.add).then_inc(merge_ready, 1)

            attention_gated(0)
            split_lo(N_PB0 + 3)
            for g in range(HT):
                dve.wait_ge(y_round, g + 1)
                stt(h_lo[:, HT + g, :], bank_b[:, g, :], cols1[:, C_PSC + g:C_PSC + g + 1],
                    h_hi[:, HT + g, :].bitcast(F32), ALU.mult, ALU.subtract).then_inc(y_ready, 1)
            for k in range(HT):
                split_lo(N_SB1 + k)
            merge(0)
            for k in range(HT):
                split_lo(N_PB1 + k)
            attention_gated(1)
            for k in range(HT):
                split_lo(N_OUT + k)
            merge(1)
            for n in range(N_OUT + SLOTS, N_OUT + KT + SLOTS):
                split_lo(n)

            def post_out(tiles, col, before_sq):
                for f in tiles:
                    dve.wait_ge(sq_ready, before_sq + f + 1)
                    nc.vector.tensor_scalar(mixg[:, f, :], sets[f // 4][:, f % 4, :], cols1[:, col + f:col + f + 1],
                                            None, ALU.mult).then_inc(mix_out, 1)

            def x_update(number, turn, gain):
                dve.wait_ge(rstd_ready, number)
                dve.wait_ge(mix_out, KT * (turn + 1))
                for f in range(KT + 3):
                    if f < KT:
                        if f >= 4 and f % 2 == 1:
                            dve.wait_ge(x_new_p, turn * HALF_TILES + (f - 4) // 2 + 1)
                        tt(xinc[:, f % 4, :], mixg[:, f, :], rstd[:, number % 2, :], ALU.mult).then_inc(xinc_ready, 1)
                    e = f - 1
                    if 0 <= e < KT and e % 2 == 0:
                        dve.wait_ge(xinc_ready, turn * KT + e + 1)
                        tt(x_t[:, e, :], x_t[:, e, :], xinc[:, e % 4, :], ALU.add).then_inc(x_new, 1)
                    e = f - 3
                    if e >= 0 and gain is not None:
                        dve.wait_ge(xg_round, e + 1)
                        stt(h_lo[:, e, :], x_t[:, e, :], cols1[:, gain + e:gain + e + 1],
                            h_hi[:, e, :].bitcast(F32), ALU.mult, ALU.subtract).then_inc(xg_ready, 1)

            post_out(range(4), C_POST, KT)
            for n in range(N_OUT + KT + SLOTS, N_UP + SLOTS):
                split_lo(n)
            post_out(range(4, 8), C_POST, KT)
            rstd_of(2, bank_a[:, 0, :])
            x_update(2, 0, C_PMLP)

            r2 = rstd[:, 0, :]

            def up1_act(g, i=0, gper=0):
                for j in range(4):
                    t = 4 * g + j
                    if j == 1:
                        split_lo(N_UP + SLOTS + (1 + g) * KT, CW, i, gper * KT)
                    dve.wait_ge(relu_sq, i * (4 * gper) + (t + 1))
                    tt(act1[:, i * (4 * gper) + t, :], relu[:, j, :], r2, ALU.mult).then_inc(a_ready, 1)
                for k in range(1, 4):
                    split_lo(N_UP + SLOTS + (1 + g) * KT + k, CW, i, gper * KT)

            for k in range(KT):
                split_lo(N_UP + SLOTS + k)
            rstd_of(3, bank_b[:, 3, :])
            dve.wait_ge(rstd_ready, 3)
            tt(r2, rstd[:, 1, :], rstd[:, 1, :], ALU.mult).then_inc(r2_ready, 1)
            dve.wait_ge(r2_ready, 1)
            up1_act(0)
            with dve.Fori(0, F1G // 2 - 1) as i:
                for g in range(1, 3):
                    for k in range(4, KT):
                        split_lo(N_UP + SLOTS + g * KT + k, CW, i, 2 * KT)
                    up1_act(g, i, 2)
            for k in range(4, KT):
                split_lo(N_UP + SLOTS + (F1G - 1) * KT + k)

            def act_lo(acts, k, i=0):
                dve.wait_ge(as_round, i * 2 + (k + 1))
                rest(as_lo[:, k % 2, :], acts[:, i * 2 + k, :], as_hi[:, k % 2, :]).then_inc(as_ready, 1)

            for k in range(2):
                act_lo(act1, k)
            up1_act(F1G - 1)
            for k in range(2):
                act_lo(act1, k + 2)
            with dve.Fori(0, F1T // 2 - 2) as kk:
                for k in range(2):
                    split_lo(N_DOWN + 2 * SLOTS + 2 * k, CW, kk, 4)
                    split_lo(N_DOWN + 2 * SLOTS + 2 * k + 1, CW, kk, 4)
                    act_lo(act1, k + 4, kk)
            post_out(range(KT), C_QMLP, 3 * KT)
            rstd_of(4, bank_a[:, 0, :])
            x_update(4, 1, None)
            meet(dve, 0)

            with dve.Fori(0, DEPTH2) as l:
                nc.vector.tensor_copy(cols2[:, :], cols_all[:, bass.ds(l, 1), :].rearrange("p a n -> p (a n)")).then_inc(cols_out, 1)
                dve.wait_ge(cols_out, 1)
                def xg_lo(f, col):
                    dve.wait_ge(xg_round, (0 if col == L_MIX else KT) + f + 1)
                    stt(h_lo[:, f, :], x_t[:, f, :], cols2[:, col + f:col + f + 1], h_hi[:, f, :].bitcast(F32),
                        ALU.mult, ALU.subtract).then_inc(xg_ready, 1)

                for f in range(KT):
                    xg_lo(f, L_MIX)
                    if f < SLOTS:
                        split_lo(f)
                nc.vector.memset(upad[:, :, 0:HALO], 0.0).then_inc(pad_zero, 1)
                nc.vector.memset(upad[:, :, HALO + S:CPAD], 0.0).then_inc(pad_zero, 1)
                def split2_lo(n):
                    split_lo(n, width2(n))

                for k in range(KT):
                    split2_lo(M_A + SLOTS + k)
                rstd_of(1, bank_b[:, 3, :])
                dve.wait_ge(rstd_ready, 1)
                norm = rstd[:, 1, :]

                def projected(dst, bank):
                    tt(dst, bank, norm, ALU.mult).then_inc(proj_out, 1)

                for j in range(4):
                    projected(af[:, j, :], bank_a[:, j, :])
                for k in range(KT):
                    split2_lo(M_G + SLOTS + k)
                dve.wait_ge(w_used, M_G + KT)
                for j in range(4):
                    projected(gf[:, j, :], bank_b[:, j, :])
                for k in range(4):
                    split2_lo(M_Q + SLOTS + k)
                for j in range(4):
                    dve.wait_ge(glu_sig, j + 1)
                    tt(upad[:, j, HALO:HALO + S], af[:, j, :], gf[:, j, :], ALU.mult).then_inc(u_ready, 1)
                dve.wait_ge(pad_zero, 2)
                tap = 0

                def taps(count):
                    nonlocal tap
                    for n in range(tap, min(tap + count, HT * DVE_TAPS)):
                        i, m = n // DVE_TAPS, n % DVE_TAPS
                        acc = conv_odd[i % 2] if m % 2 else conv[:, i, :]
                        src = upad[:, i, m:m + S]
                        w = cols2[:, L_TAP + i * 32 + m:L_TAP + i * 32 + m + 1]
                        if m == 0:
                            dve.wait_ge(u_ready, i + 1)
                            ins = nc.vector.tensor_scalar(acc, src, w, cols2[:, L_BDW + i:L_BDW + i + 1], ALU.mult, ALU.add)
                        elif m == 1:
                            if i >= 2:
                                dve.wait_ge(conv_ready, i - 1)
                            ins = nc.vector.tensor_scalar(acc, src, w, None, ALU.mult)
                        else:
                            dve.wait_ge(tap_done, i * DVE_TAPS + m - 1)
                            ins = stt(acc, src, w, acc, ALU.mult, ALU.add)
                        ins.then_inc(tap_done, 1)
                        tap += 1

                for k in range(4, KT):
                    split2_lo(M_Q + SLOTS + k)
                    taps(1)
                dve.wait_ge(w_used, M_Q + KT)
                for t in range(QT):
                    projected(cq_f[:, t, :], bank_a[:, t, :])
                for t in range(QT):
                    add_square(t, KT, KT - 1, 1)
                for k in range(4):
                    split2_lo(M_KV + SLOTS + k)
                    taps(1)
                rstd_into(2, bank_a[:, 3, :], QL)
                for t in range(QT):
                    stt(cq_f[:, t, :], cq_f[:, t, :], cols2[:, L_GQ + t:L_GQ + t + 1], rstd[:, 0, :],
                        ALU.mult, ALU.mult).then_inc(cn_ready, 1)
                for k in range(4):
                    split2_lo(M_PAIR + k)
                for t in range(QT):
                    dve.wait_ge(lat_round, t + 1)
                    rest(lat_lo[:, t, :], cq_f[:, t, :], lat_hi[:, t, :]).then_inc(lat_ready, 1)
                dve.wait_ge(w_used, M_KV + KT)
                for t in range(KVT):
                    projected(ckv_f[:, t, :], bank_b[:, t, :])
                stt(krf[ND:P, :], bank_b[ND:P, 2, :], 1.0 / MLA_SCALE, norm[ND:P, :], ALU.mult, ALU.mult).then_inc(proj_out, 1)
                for t in range(KVT):
                    add_square(t, KT + QT, KT + QT - 2, 2)
                dve.wait_ge(proj_out, 8 + QT + KVT + 1)
                dve.wait_ge(trig_step, 12)
                first, second = slice(ND, ND + RD), slice(ND + RD, P)
                tt(rot[first, 0, :], krf[first, :], trig[first, :], ALU.mult).then_inc(kr_step, 1)
                tt(rot[first, 1, :], krf[second, :], trig[second, :], ALU.mult).then_inc(kr_step, 1)
                dve.wait_ge(kr_step, 2)
                tt(rot[first, 0, :], rot[first, 0, :], rot[first, 1, :], ALU.add).then_inc(kr_step, 1)
                dve.wait_ge(kr_step, 3)
                nc.vector.tensor_copy(rot[second, 0, :], rot[first, 0, :]).then_inc(kr_step, 1)
                rstd_into(3, bank_b[:, 3, :], KVL)
                for t in range(KVT):
                    stt(ckv_f[:, t, :], ckv_f[:, t, :], cols2[:, L_GKV + t:L_GKV + t + 1], rstd[:, 0, :],
                        ALU.mult, ALU.mult).then_inc(cn_ready, 1)

                def make_q(i, banks):
                    dve.wait_ge(w_used, M_PAIR + i * SLOTS + QT)
                    for hd in range(2):
                        tt(qf[:, hd, :], banks[hd], trig[:, :], ALU.mult).then_inc(q_made, 1)

                def stage_q_lo(i):
                    for hd in range(2):
                        dve.wait_ge(qk_round, i * 5 + hd + 1)
                        rest(kq_lo[i % 2][hd], qf[:, hd, :], kq_hi[i % 2][hd]).then_inc(qk_ready, 1)

                def stage_k_lo(i, hd, bank):
                    dve.wait_ge(qk_round, i * 5 + 3 + hd)
                    rest(kk_lo[i % 2][hd][0:ND, :], bank[0:ND, :], kk_hi[i % 2][hd][0:ND, :]).then_inc(qk_ready, 1)

                def stage_v_lo(i, bank):
                    dve.wait_ge(qk_round, i * 5 + 5)
                    rest(vv_lo, bank, vv_hi).then_inc(qk_ready, 1)

                for q in range(2):
                    for hd in range(2):
                        dve.wait_ge(kr_round, 2 * q + hd + 1)
                        rest(kk_lo[q][hd][ND:P, :], rot[ND:P, 0, :], kk_hi[q][hd][ND:P, :]).then_inc(kr_ready, 1)
                for t in range(KVT):
                    dve.wait_ge(lat_round, QT + t + 1)
                    rest(lat_lo[:, QT + t, :], ckv_f[:, t, :], lat_hi[:, QT + t, :]).then_inc(lat_ready, 1)
                make_q(0, first_banks[0])
                stage_q_lo(0)
                for hd in range(2):
                    stage_k_lo(0, hd, first_banks[1][hd])
                stage_v_lo(0, first_banks[2])
                for k in range(SLOTS):
                    split2_lo(M_PAIR + SLOTS + k)

                for g in range(BLOCKS + 2):
                    i, m = g // (2 * TT), g % (2 * TT)
                    if g < BLOCKS:
                        b = g % TT
                        dve.wait_ge(s_ready, g + 1)
                        nc.vector.tensor_reduce(soft[:, 1, b:b + 1], s_banks[g % 2], AX_X, ALU.max,
                                                negate=True).then_inc(mx_step, 1)
                    if 1 <= g <= BLOCKS:
                        b = (g - 1) % TT
                        dve.wait_ge(p_exp, g)
                        nc.vector.reciprocal(soft[:, 3, b:b + 1], soft[:, 2, b:b + 1]).then_inc(p_step, 1)
                        dve.wait_ge(p_step, g)
                        nc.vector.tensor_scalar(prob[:, b, :], prob[:, b, :], soft[:, 3, b:b + 1], None,
                                                ALU.mult).then_inc(p_ready, 1)
                    taps(1)
                    if g >= 2:
                        b = (g - 2) % TT
                        dve.wait_ge(pt_round, g - 1)
                        rest(pt_lo[:, :, b * P:b * P + P], bank_a[:, g % 2, :].rearrange("p (k q) -> p k q", k=TT),
                             pt_hi[:, :, b * P:b * P + P]).then_inc(pt_ready, 1)
                    if m == 3 and 1 <= i < PAIRS:
                        stage_v_lo(i, next_banks[2])
                    if i + 1 < PAIRS:
                        if m == 4:
                            make_q(i + 1, next_banks[0])
                        if m == 6:
                            stage_q_lo(i + 1)
                        if m in (6, 7):
                            stage_k_lo(i + 1, m - 6, next_banks[1][m - 6])
                        if m in (2, 3, 5, 7):
                            split2_lo(M_PAIR + (i + 2) * SLOTS + (2, 3, 5, 7).index(m))
                    elif m in (4, 5, 6) and i < PAIRS:
                        t = m - 4
                        dve.wait_ge(o_round, t + 1)
                        rest(h_lo[:, O_TILES[t], :], o2_f[:, t, :], h_hi[:, O_TILES[t], :]).then_inc(o_split, 1)
                taps(HT * DVE_TAPS)
                dve.wait_ge(o_round, HT)
                rest(h_lo[:, O_TILES[3], :], o2_f[:, 3, :], h_hi[:, O_TILES[3], :]).then_inc(o_split, 1)
                dve.wait_ge(mean_ready, 1)
                dve.wait_ge(conv_ready, HT)
                for j in range(HT):
                    stt(conv[:, j, :], bank_b[:, 0, :], -1.0 / HALF, conv[:, j, :], ALU.mult, ALU.add).then_inc(dev_ready, 1)
                split_lo(M_WO + 4)
                for j in range(HT):
                    add_square(j, KT + KVT + QT, KT + KVT + QT - 3, 3)
                for k in range(5, 8):
                    split_lo(M_WO + k)
                rstd_into(4, bank_b[:, 2, :], HALF)
                for j in range(HT):
                    tt(conv[:, j, :], conv[:, j, :], rstd[:, 0, :], ALU.mult).then_inc(ln_out, 1)
                for j in range(HT):
                    dve.wait_ge(cu_round, j + 1)
                    rest(h_lo[:, C_TILES[j], :], un[:, j, :], h_hi[:, C_TILES[j], :]).then_inc(cu_ready, 1)
                for n in range(M_WO + 8, M_WO + 12):
                    split_lo(n)

                def x_add(f, set_):
                    tt(x_t[:, f, :], x_t[:, f, :], set_[:, f % 4, :], ALU.add).then_inc(x_new, 1)

                dve.wait_ge(w_used, M_WO + KT)
                for f in range(4):
                    x_add(f, bank_a)
                for n in range(M_WO + 12, M_UP + SLOTS):
                    split_lo(n)
                dve.wait_ge(w_used, M_UP)
                for f in range(4, KT):
                    x_add(f, bank_b)
                for f in range(KT):
                    xg_lo(f, L_FFN)
                nc.vector.memset(zp[:, :, 0:1], 0.0).then_inc(zp_zero, 1)
                nc.vector.memset(zp[:, :, S + 1:ZPAD], 0.0).then_inc(zp_zero, 1)

                def ffn_tiles(g, i=0, gper=0):
                    def split(k):
                        split_lo(M_UP + SLOTS + (1 + g) * KT + k, CW, i, gper * KT)

                    z0 = i * (4 * gper) + 4 * g
                    dve.wait_ge(w_used, i * (gper * KT) + (M_UP + g * KT + KT))
                    for j in range(4):
                        tt(zp[:, j, 1:1 + S], sets[g % 2][:, j, :], rstd[:, 1, :], ALU.mult).then_inc(z_out, 1)
                    for tap, done in ((0, z_tap), (2, z_conv)):
                        for j in range(4):
                            tile = i * (2 * gper) + (2 * g + j % 2 + F2T * (j // 2))
                            dve.wait_ge(z_tap if tap else z_mid, z0 + (j + 1))
                            stt(cz[:, j, :], zp[:, j, tap:tap + S],
                                cols2[:, bass.ds(tile + (L_FTAP + tap * 2 * F2T), 1)], cz[:, j, :],
                                ALU.mult, ALU.add).then_inc(done, 1)
                        split(tap // 2)
                    for j in range(2):
                        dve.wait_ge(z_silu, i * (2 * gper) + (2 * g + j + 1))
                        dve.wait_ge(z_conv, z0 + (j + 3))
                        tt(act2[:, i * (2 * gper) + (2 * g + j), :], cz[:, j, :], cz[:, 2 + j, :],
                           ALU.mult).then_inc(a_ready, 1)
                    split(2)
                    split(3)

                for k in range(KT):
                    split_lo(M_UP + SLOTS + k)
                rstd_of(5, bank_b[:, 3, :])
                dve.wait_ge(rstd_ready, 5)
                dve.wait_ge(zp_zero, 2)
                ffn_tiles(0)
                with dve.Fori(0, F2G // 2 - 1) as i:
                    for g in range(1, 3):
                        for k in range(4, KT):
                            split_lo(M_UP + SLOTS + g * KT + k, CW, i, 2 * KT)
                        ffn_tiles(g, i, 2)
                for k in range(4, KT):
                    split_lo(M_UP + SLOTS + (F2G - 2) * KT + k)
                ffn_tiles(F2G - 2)
                for k in range(4, KT):
                    split_lo(M_UP + SLOTS + (F2G - 1) * KT + k)

                for k in range(2):
                    act_lo(act2, k)
                ffn_tiles(F2G - 1)
                for k in range(2):
                    act_lo(act2, k + 2)
                with dve.Fori(0, F2T // 2 - 2) as kk:
                    for k in range(2):
                        split_lo(M_DOWN + 2 * SLOTS + 2 * k, CW, kk, 4)
                        split_lo(M_DOWN + 2 * SLOTS + 2 * k + 1, CW, kk, 4)
                        act_lo(act2, k + 4, kk)
                dve.wait_ge(w_used, M_END - 1)
                for f in range(4):
                    x_add(f, bank_b)
                dve.wait_ge(w_used, M_END)
                for f in range(4, KT):
                    x_add(f, bank_a)
                meet(dve, l + 1)

            for t in range(KT):
                add_square(t, 0, 0, 0)
            rstd_of(1, bank_a[:, 0, :])
            dve.wait_ge(rstd_ready, 1)
            for f in range(KT):
                stt(yfin[:, f, :], x_t[:, f, :], cols1[:, C_FIN + f:C_FIN + f + 1], rstd[:, 1, :],
                    ALU.mult, ALU.mult).then_inc(y_made, 1)
            for t in range(TT):
                dve.wait_ge(yt_made, t + 1)
                nc.vector.tensor_copy(y_out[:, t, S:2 * S], sets[t % 2][:, 2 * (t // 2) + 1, :]).then_inc(yt_out_b, 1)

        @block.tensor
        def _(pe):
            def use(n, i=0, per=0):
                pe.wait_ge(w_split, i * per + (n + 1))
                return n % SLOTS

            def mm3(out_, a_hi, a_lo, b_hi, b_lo, start, stop, loose=False):
                nc.tensor.matmul(out_, a_hi, b_hi, start=start, stop=False, skip_group_check=loose)
                nc.tensor.matmul(out_, a_hi, b_lo, start=False, stop=False, skip_group_check=loose)
                return nc.tensor.matmul(out_, a_lo, b_hi, start=False, stop=stop, skip_group_check=loose)

            def wide(set_, s, b_hi, b_lo, start, stop, tiles=4):
                for j in range(tiles):
                    c = slice(j * P, j * P + P)
                    last = mm3(set_[:, j, :], w_hi[:, s, c], w_lo[:, s, c], b_hi, b_lo, start, stop)
                last.then_inc(w_used, 1)

            def total(bank, added):
                pe.wait_ge(sq_added, added)
                nc.tensor.matmul(bank, ones[:, :], ssum[:, :], start=True, stop=True).then_inc(stat_ready, 1)

            def total_squares(before_sq, before_mix):
                pe.wait_ge(mix_out, before_mix + 1)
                for f in range(KT):
                    pe.wait_ge(sq_ready, before_sq + f + 1)
                    nc.tensor.matmul(bank_a[:, 0, :], ones[:, :], sq[:, f % 4, :], start=f == 0,
                                     stop=f == KT - 1).then_inc(sq_added if f < KT - 1 else stat_ready, 1)

            pe.wait_ge(consts_made, 2)
            for half in range(2):
                for f in range(4):
                    for t in range(TT):
                        if half == 0 and f == 0:
                            pe.wait_ge(x_land[t], 16)
                        c = (4 * half + f) * P
                        last = nc.tensor.transpose(sets[half][:, f, t * P:t * P + P], x_in[:, t, c:c + P], ident[:, :])
                last.then_inc(xt_made, 1)
            pe.wait_ge(rows1_land, 16 * 7)
            pe.wait_ge(xt_out, 1)
            nc.tensor.transpose(bank_a[:, 0, 0:N_ROWS1], rows1, ident[0:N_ROWS1, 0:N_ROWS1]).then_inc(cols_made, 1)
            pe.wait_ge(rows2_land, 16 * 10 * DEPTH2)
            for n in range(DEPTH2):
                pe.wait_ge(xt_out, n + 2)
                bank = bank_a[:, 1 + n, :]
                nc.tensor.transpose(bank[:, 0:N_ROWS2], rows2[n], ident[0:N_ROWS2, 0:N_ROWS2])
                for c in range(HT):
                    nc.tensor.transpose(bank[:, L_TAP + 32 * c:L_TAP + 32 * c + CONV_K], rows_tap[n][:, c * P:c * P + P],
                                        ident[0:CONV_K, 0:CONV_K])
                for tap in range(3):
                    c = L_FTAP + tap * 2 * F2T
                    last = nc.tensor.transpose(bank[:, c:c + 2 * F2T], rows_ftap[n][:, tap, :],
                                               ident[0:2 * F2T, 0:2 * F2T])
                last.then_inc(cols_made, 1)
            pe.wait_ge(consts_made, 3)
            pe.wait_ge(xt_out_b, 4)
            total(bank_b[:, 0, :], KT - 1)
            pe.wait_ge(tri_made, 1)
            pe.wait_ge(xt_out, 4)
            pe.wait_ge(cols_out, 1 + 3 * DEPTH2)
            pe.wait_ge(var_ready, 1)

            with pe.Fori(0, PAIRS) as i:
                for k in range(KT):
                    s = use(N_PAIR + k, i, 2 * KT)
                    pe.wait_ge(h_ready, k + 1)
                    wide(bank_a, s, h_hi[:, k, :], h_lo[:, k, :], k == 0, k == KT - 1)

                def gate(k):
                    s = use(N_PAIR + KT + k, i, 2 * KT)
                    wide(bank_b, s, h_hi[:, k, :], h_lo[:, k, :], k == 0, k == KT - 1)

                def scores(s):
                    hd, kb = s // 4, 3 - s % 4
                    rows = slice(HEAD * hd, HEAD * hd + HEAD)
                    c = slice(kb * P, kb * P + P)
                    if s == 0:
                        pe.wait_ge(stage_ready, i * 3 + 2)
                        pe.wait_ge(u_out, i + 1)
                    if s >= 2:
                        pe.wait_ge(attn_exp, i * 8 + (s - 1))
                    mm3(bank_a[:, s % 2, 0:S - Q0[kb]], k_hi[rows, c], k_lo[rows, c], q_hi[rows, Q0[kb]:S],
                        q_lo[rows, Q0[kb]:S], True, True).then_inc(z_ready, 1)

                def log_sums(s):
                    hd, kb = s // 4, 3 - s % 4
                    pe.wait_ge(l_ready, i * 8 + (s + 1))
                    for kb2 in range(kb, TT):
                        off, n = L_OFF[kb2], S - Q0[kb2]
                        z0 = Q0[kb2] - Q0[kb]
                        for part in (l_hi, l_lo):
                            last = nc.tensor.matmul(bank_a[:, s % 2, z0:z0 + n], tri[:, 0 if kb2 == kb else 1, :],
                                                    part[:, hd, off:off + n], start=False,
                                                    stop=kb2 == TT - 1 and part is l_lo, skip_group_check=True)
                    last.then_inc(c_ready, 1)

                def values(s):
                    hd, kb = s // 4, 3 - s % 4
                    c = slice(kb * P, kb * P + P)
                    n = S - Q0[kb]
                    if s == 0:
                        pe.wait_ge(stage_ready, i * 3 + 3)
                    pe.wait_ge(attn_ready, i * 8 + (s + 1))
                    mm3(bank_a[:, 2 + hd, Q0[kb]:S], v_hi[:, c], v_lo[:, c], at_hi[:, s % 2, 0:n], at_lo[:, s % 2, 0:n],
                        kb == TT - 1, kb == 0, True).then_inc(av_done, 1)

                gate(0)
                scores(0)
                pe.wait_ge(v_out, i + 1)
                for j in range(TT):
                    c = slice(j * P, j * P + P)
                    last = nc.tensor.transpose(bank_a[:, 3, c], v_f[:, c], ident[:, :])
                last.then_inc(vt_made, 1)
                for s in range(8):
                    if s < 7:
                        gate(s + 1)
                        scores(s + 1)
                    log_sums(s)
                    if s >= 1:
                        values(s - 1)
                values(7)
                pe.wait_ge(attn_exp, i * 8 + 8)
                pe.wait_ge(o_out, i * 2 + 2)

            for k in range(HT):
                s = use(N_SB0 + k)
                pe.wait_ge(o_split, k + 1)
                wide(bank_a, s, o_hi[:, k, :], o_lo[:, k, :], k == 0, k == HT - 1)
            s = use(N_MIX)
            pe.wait_ge(gate_out, 16)
            for g in range(HT):
                pe.wait_ge(pool_split, g + 1)
                c = slice(g * P, g * P + P)
                last = mm3(bank_b[:, g, :], w_hi[:, s, c], w_lo[:, s, c], pool_hi[:, g, :], pool_lo[:, g, :], True, True)
            last.then_inc(w_used, 1)
            pe.wait_ge(y_ready, HT)
            for k in range(HT):
                s = use(N_PB0 + k)
                wide(bank_b, s, h_hi[:, HT + k, :], h_lo[:, HT + k, :], k == 0, k == HT - 1)
            pe.wait_ge(sb_out, 4)
            for k in range(HT):
                s = use(N_SB1 + k)
                wide(bank_a, s, o_hi[:, k, :], o_lo[:, k, :], k == 0, k == HT - 1)
            pe.wait_ge(pb_out, 4)
            for k in range(HT):
                s = use(N_PB1 + k)
                wide(bank_b, s, h_hi[:, HT + k, :], h_lo[:, HT + k, :], k == 0, k == HT - 1)
            for half, branch_out in enumerate((sb_out, pb_out)):
                pe.wait_ge(branch_out, 8)
                for k in range(KT):
                    s = use(N_OUT + half * KT + k)
                    pe.wait_ge(merge_split, k + 1)
                    wide(sets[half], s, h_hi[:, k, :], h_lo[:, k, :], k == 0, k == KT - 1)
            total_squares(KT, 0)

            def up1(set_, g, i=0, gper=0):
                for k in range(KT):
                    s = use(N_UP + g * KT + k, i, gper * KT)
                    if g == 0:
                        pe.wait_ge(xg_ready, k + 1)
                    wide(set_, s, h_hi[:, k, :], h_lo[:, k, :], k == 0, k == KT - 1)

            pe.wait_ge(var_ready, 2)
            pe.wait_ge(mix_out, KT)
            up1(bank_a, 0)
            total(bank_b[:, 3, :], 3 * (KT - 1))
            pe.wait_ge(var_ready, 3)
            with pe.Fori(0, F1G // 2 - 1) as i:
                up1(bank_b, 1, i, 2)
                pe.wait_ge(relu_out, i * 8 + 4)
                up1(bank_a, 2, i, 2)
                pe.wait_ge(relu_out, i * 8 + 8)
            up1(bank_b, F1G - 1)

            def down(order, n, k, half, start, stop, i=0):
                s = use(n + 2 * k + half, i, 4)
                pe.wait_ge(as_ready, i * 2 + (k + 1))
                wide(order[half], s, as_hi[:, k % 2, :], as_lo[:, k % 2, :], start, stop)

            def down_all(order, n, count, out_of_set, groups):
                for k in range(2):
                    for half in range(2):
                        if k == 0:
                            pe.wait_ge(out_of_set, 4 * (groups - 1 + half))
                        down(order, n, k, half, k == 0, False)
                with pe.Fori(0, count // 2 - 2) as kk:
                    for k in range(2, 4):
                        for half in range(2):
                            down(order, n, k, half, False, False, kk)
                for k in range(count - 2, count):
                    for half in range(2):
                        down(order, n, k, half, False, k == count - 1)

            down_all(sets, N_DOWN, F1T, relu_out, F1G)
            total_squares(3 * KT, KT)
            meet(pe, 0)

            with pe.Fori(0, DEPTH2) as l:
                def project(set_, n0, tiles):
                    for k in range(KT):
                        s = use(n0 + k)
                        pe.wait_ge(xg_ready, k + 1)
                        wide(set_, s, h_hi[:, k, :], h_lo[:, k, :], k == 0, k == KT - 1, tiles)

                project(bank_a, M_A, 4)
                total(bank_b[:, 3, :], KT - 1)
                pe.wait_ge(var_ready, 1)
                project(bank_b, M_G, 4)
                pe.wait_ge(proj_out, 4)
                project(bank_a, M_Q, QT)
                pe.wait_ge(proj_out, 8)
                for k in range(KT):
                    if k == 4:
                        total(bank_a[:, 3, :], KT + QT - 2)
                    s = use(M_KV + k)
                    for j in range(KVT + 1):
                        c = slice(j * P, j * P + P) if j < KVT else slice(KV_COLS - P, KV_COLS)
                        last = mm3(bank_b[:, j, :], w_hi[:, s, c], w_lo[:, s, c], h_hi[:, k, :], h_lo[:, k, :],
                                   k == 0, k == KT - 1)
                    last.then_inc(w_used, 1)

                def queries(i, k, banks):
                    s = use(M_PAIR + i * SLOTS + k)
                    pe.wait_ge(lat_ready, k + 1)
                    for hd in range(2):
                        c = slice(hd * P, hd * P + P)
                        last = mm3(banks[hd], w_hi[:, s, c], w_lo[:, s, c], lat_hi[:, k, :], lat_lo[:, k, :],
                                   k == 0, k == QT - 1)
                    last.then_inc(w_used, 1)

                def keys(i, hd, bank):
                    s = use(M_PAIR + i * SLOTS + QT)
                    pe.wait_ge(lat_ready, QT + KVT)
                    for kk in range(KVT):
                        c = slice(kk * 4 * ND + hd * 2 * ND, kk * 4 * ND + hd * 2 * ND + P)
                        last = mm3(bank, w_hi[:, s, c], w_lo[:, s, c], lat_hi[:, QT + kk, :], lat_lo[:, QT + kk, :],
                                   kk == 0, kk == KVT - 1)
                    last.then_inc(k_done if hd == 0 else w_used, 1)

                def values_of(i, bank):
                    pe.wait_ge(vt_out, 2 * i + 2)
                    for j in range(TT):
                        c = slice(j * P, j * P + P)
                        last = nc.tensor.transpose(bank[:, c], vt_f[:, c], ident[:, :])
                    last.then_inc(v_turned, 1)

                pe.wait_ge(proj_out, 8 + QT)
                for k in range(QT):
                    queries(0, k, first_banks[0])
                total(bank_b[:, 3, :], KT + QT + KVT - 3)
                pe.wait_ge(var_ready, 2)
                for hd in range(2):
                    keys(0, hd, first_banks[1][hd])
                values_of(0, first_banks[2])

                def scores2(g):
                    i, hd, b = g // (2 * TT), g // TT % 2, g % TT
                    c = slice(b * P, b * P + P)
                    if b == 0 and hd == 0:
                        pe.wait_ge(qk_ready, i * 5 + 4)
                        pe.wait_ge(kr_ready, 4)
                    if g >= 2:
                        pe.wait_ge(p_exp, g - 1)
                    q = i % 2
                    mm3(s_banks[g % 2], kq_hi[q][hd][:, c], kq_lo[q][hd][:, c], kk_hi[q][hd], kk_lo[q][hd],
                        True, True).then_inc(s_ready, 1)

                def transposed(g):
                    b = g % TT
                    if g >= 2:
                        pe.wait_ge(pt_ready, g - 1)
                    pe.wait_ge(p_ready, g + 1)
                    for kb in range(TT):
                        c = slice(kb * P, kb * P + P)
                        last = nc.tensor.transpose(bank_a[:, g % 2, c], prob[:, b, c], ident[:, :])
                    last.then_inc(pt_made, 1)

                def values2(i, hd):
                    pe.wait_ge(pt_ready, i * 8 + 4 * hd + 4)
                    if hd == 0:
                        pe.wait_ge(qk_ready, i * 5 + 5)
                    if i > 0 or hd > 0:
                        pe.wait_ge(o2_out, i * 2 + hd)
                    for kb in range(TT):
                        c = slice(kb * P, kb * P + P)
                        last = mm3(bank_b[:, 1, :], vv_hi[:, c], vv_lo[:, c], pt_hi[:, kb, :], pt_lo[:, kb, :],
                                   kb == 0, kb == TT - 1)
                    last.then_inc(pv_done, 1)

                def beside(i, m):
                    if m < QT:
                        if m == 0:
                            pe.wait_ge(qk_ready, i * 5 + 4)
                        queries(i + 1, m, next_banks[0])
                    elif m == 4:
                        pe.wait_ge(qk_ready, i * 5 + 5)
                        keys(i + 1, 0, next_banks[1][0])
                    elif m == 5:
                        pe.wait_ge(q_made, 2 * i + 4)
                        keys(i + 1, 1, next_banks[1][1])
                    elif m == 7:
                        pe.wait_ge(qk_ready, i * 5 + 8)
                        values_of(i + 1, next_banks[2])

                for g in range(2):
                    scores2(g)
                for g in range(BLOCKS):
                    i, m = g // (2 * TT), g % (2 * TT)
                    if g + 2 < BLOCKS:
                        scores2(g + 2)
                    if i + 1 < PAIRS:
                        beside(i, m)
                    transposed(g)
                    if m == TT:
                        values2(i, 0)
                    if m == 0 and i > 0:
                        values2(i - 1, 1)
                values2(PAIRS - 1, 1)
                for j in range(HT):
                    pe.wait_ge(conv_ready, j + 1)
                    last = nc.tensor.matmul(bank_b[:, 0, :], ones[:, :], conv[:, j, :], start=j == 0, stop=j == HT - 1)
                last.then_inc(mean_ready, 1)

                pe.wait_ge(pt_ready, 8 * PAIRS)
                for k in range(KT):
                    s = use(M_WO + k)
                    if k == HT:
                        total(bank_b[:, 2, :], KT + KVT + QT + HT - 4)
                    pe.wait_ge(o_split if k < HT else cu_ready, k % HT + 1)
                    t = (O_TILES + C_TILES)[k]
                    wide(bank_a, s, h_hi[:, t, :], h_lo[:, t, :], k == 0, k == KT - 1)
                pe.wait_ge(dev_ready, HT)
                pe.wait_ge(var_ready, 4)
                pe.wait_ge(o2_out, 2 * PAIRS)
                for k in range(KT):
                    s = use(M_WO + KT + k)
                    t = (O_TILES + C_TILES)[k]
                    wide(bank_b, s, h_hi[:, t, :], h_lo[:, t, :], k == 0, k == KT - 1)

                def up2(set_, g, i=0, gper=0):
                    for k in range(KT):
                        s = use(M_UP + g * KT + k, i, gper * KT)
                        if g == 0:
                            pe.wait_ge(xg_ready, KT + k + 1)
                        wide(set_, s, h_hi[:, k, :], h_lo[:, k, :], k == 0, k == KT - 1)

                pe.wait_ge(x_new, 4)
                up2(bank_a, 0)
                pe.wait_ge(x_new, KT)
                total(bank_b[:, 3, :], KT + KVT + QT + HT - 4 + KT - 1)
                pe.wait_ge(var_ready, 5)
                with pe.Fori(0, F2G // 2 - 1) as i:
                    up2(bank_b, 1, i, 2)
                    pe.wait_ge(z_out, i * 8 + 4)
                    up2(bank_a, 2, i, 2)
                    pe.wait_ge(z_out, i * 8 + 8)
                up2(bank_b, F2G - 2)
                pe.wait_ge(z_out, 4 * (F2G - 2))
                up2(bank_a, F2G - 1)
                down_all((bank_b, bank_a), M_DOWN, F2T, z_out, F2G)
                meet(pe, l + 1)

            total(bank_a[:, 0, :], KT - 1)
            pe.wait_ge(var_ready, 1)
            pe.wait_ge(y_made, KT)
            for t in range(TT):
                for f in range(KT):
                    last = nc.tensor.transpose(sets[t % 2][:, 2 * (t // 2) + f // 4, (f % 4) * P:(f % 4) * P + P],
                                               yfin[:, f, t * P:t * P + P], ident[:, :])
                last.then_inc(yt_made, 1)


_BLOCK1 = ["x", "g_pre_mix", "w_in", "w_pool_mix", "pool_scale", "w_br_pool", "w_br_sb", "w_gate", "b_gate", "w_out",
           "g_post_mix", "g_pre_mlp", "w_up", "w_down", "g_post_mlp"]
_BLOCK2 = ["positions_2", "g_mix_2", "w_in_2", "g_q_2", "w_uq_2", "g_kv_2", "w_ukv_2", "w_dw_conv_2", "b_dw_conv_2",
           "g_conv_ln_2", "b_conv_ln_2", "w_o_2", "g_ffn_2", "w_up_2", "w_dw_ffn_2", "b_dw_ffn_2", "w_down_2",
           "g_final_2"]


def shape_constants(np):
    row = np.arange(P)
    cosine = (row // RD) % 2 == 0
    freq = 1.0 / (np.float32(10000.0) ** (np.arange(0, RD, 2, dtype=np.float32) / np.float32(RD)))
    c = np.zeros((P, 4 + LEFT), np.float32)
    c[:, 0] = freq[row % (RD // 2)]
    c[:, 1] = np.where(cosine, 0.25, 0.0)
    c[:, 2] = np.where(cosine, np.pi / 2, 0.0)
    c[:, 3] = np.where(cosine | (row % RD >= RD // 2), 1.0, -1.0)
    c[:, 4:] = 1.0 / (np.arange(LEFT) + 1.0)
    return c


def kernel(**inputs):
    import numpy as _np
    import concourse.bacc as _bacc
    from concourse import mybir as _mybir
    from concourse.bass_utils import run_bass_kernel_spmd as _run

    nc = _bacc.Bacc("TRN2", target_bir_lowering=False, num_devices=1)
    arrays, args = {}, []
    given = [(name, _np.ascontiguousarray(inputs[name])) for name in _BLOCK1 + _BLOCK2]
    given.append(("shape_consts", shape_constants(_np)))
    for name, a in given:
        arrays[f"in_{name}_dram"] = a
        args.append(nc.dram_tensor(f"in_{name}_dram", a.shape, _mybir.dt.from_np(a.dtype), kind="ExternalInput").ap())
    args.append(nc.dram_tensor("out_dram", (1, S, D), _mybir.dt.float32, kind="ExternalOutput").ap())
    two_blocks(nc, *args)
    r = _run(nc, [arrays], core_ids=[0])
    return r.results[0]["out_dram"]
```

```python
from contextlib import ExitStack

import concourse.bass as bass
from concourse import mybir

P = 128
D = 1024
S = 512
KT = D // P
HALF_TILES = KT // 2
TT = S // P
EPS = 1e-6
SLOTS = 4
CW = 512

HALF = D // 2
HT = HALF // P
HEAD = 64
PAIRS = HALF // (2 * HEAD)
WINDOWS = (2, 4, 8, 16)
LEFT = 16
FF1 = 4096
F1T = FF1 // P
F1G = FF1 // CW
Q0 = (0, P, P, 3 * P)
L_OFF = (P + 6 * P, P + 3 * P, P, 0)
L_ALL = P + 6 * P + S
GATE_AT = (0, 1, 2, 3, 4, 5)
Q_SCALE = HEAD ** -0.5

DEPTH2 = 2
QL, KVL, RD = 384, 256, 32
QT, KVT = QL // P, KVL // P
ND = 64
MLA_SCALE = (ND + RD) ** -0.5
CONV_K = 31
POOL_TAPS = 17
DVE_TAPS = CONV_K - POOL_TAPS
HALO = CONV_K // 2
PV_BLOCKS = ((0, 1), (2, 3))
FIRST_PRODUCTS = 14
BLOCKS = PAIRS * 2 * TT
FF2 = 2816
F2T = FF2 // P
F2G = FF2 // 256

F32 = mybir.dt.float32
F32R = mybir.dt.float32r
I32 = mybir.dt.int32
ALU = mybir.AluOpType
ACT = mybir.ActivationFunctionType
AX_X = mybir.AxisListType.X
LN_EXP = "natural_log_exp_and_others"
BIG = 3.0e38

C_PRE, C_PSC, C_BG, C_POST, C_PMLP, C_QMLP = 0, 8, 12, 28, 36, 44
N_ROWS1 = 52
L_MIX, L_GQ, L_GKV, L_BDW, L_GLN, L_BLN, L_FFN, L_BFF = 0, 8, 11, 13, 17, 21, 25, 33
N_ROWS2 = 77
L_TAP, L_FTAP = 128, 256
N_COLS2 = L_FTAP + 3 * 2 * F2T

N_PAIR = 0
N_MIX = N_PAIR + PAIRS * 2 * KT
N_SB0 = N_MIX + 1
N_PB0 = N_SB0 + HT
N_SB1 = N_PB0 + HT
N_PB1 = N_SB1 + HT
N_OUT = N_PB1 + HT
N_UP = N_OUT + 2 * KT
N_DOWN = N_UP + F1G * KT
N_END1 = N_DOWN + 2 * F1T
M_A = 0
M_G = M_A + KT
M_Q = M_G + KT
M_KV = M_Q + KT
M_PAIR = M_KV + KT
M_WO = M_PAIR + PAIRS * SLOTS
M_UP = M_WO + 2 * KT
M_DOWN = M_UP + F2G * KT
M_END = M_DOWN + 2 * F2T

KV_COLS = KVL + 2 * RD
WO_ORDER = [(half, k) for rows in (range(HT), range(HT, KT)) for half in range(2) for k in rows]


def pieces2(n):
    if M_KV <= n < M_PAIR or M_PAIR <= n < M_WO and (n - M_PAIR) % SLOTS < QT:
        return 3
    return 1


def width2(n):
    if M_Q <= n < M_KV:
        return QL
    if M_KV <= n < M_PAIR:
        return KV_COLS
    if M_PAIR <= n < M_WO and (n - M_PAIR) % SLOTS < QT:
        return 2 * P
    return CW


def landed2(n):
    return 16 * sum(pieces2(m) for m in range(n % SLOTS, n + 1, SLOTS))


def two_blocks(nc, x, g_pre_mix, w_in, w_pool_mix, pool_scale, w_br_pool, w_br_sb, w_gate, b_gate,
               w_out, g_post_mix, g_pre_mlp, w_up, w_down, g_post_mlp, positions, g_mix, w_in2,
               g_q, w_uq, g_kv, w_ukv, w_dw_conv, b_dw_conv, g_conv_ln, b_conv_ln, w_o, g_ffn,
               w_up2, w_dw_ffn, b_dw_ffn, w_down2, g_final, shape_consts, out):
    with ExitStack() as ctx:
        def sb(name, shape, dt=F32):
            return ctx.enter_context(nc.sbuf_tensor(name, shape, dt))

        sems, late_sems = [], []

        def sem(name):
            s = ctx.enter_context(nc.semaphore(name))
            sems.append(s)
            return s

        def late_sem(name):
            s = ctx.enter_context(nc.semaphore(name))
            late_sems.append(s)
            return s

        def sem1(name):
            return ctx.enter_context(nc.semaphore(name))

        x_v = x.rearrange("b (t p) d -> p (b t) d", p=P)
        out_v = out.rearrange("b (t p) d -> p (b t) d", p=P)
        in_v = w_in.rearrange("(k p) (b i n) -> p k b i n", p=P, b=4, n=P)
        gate_v = w_gate.rearrange("(k p) (i n) -> p k i n", p=P, n=CW)
        sb_v = w_br_sb.rearrange("(k p) (h n) -> p k h n", p=P, n=CW)
        pb_v = w_br_pool.rearrange("(k p) (h n) -> p k h n", p=P, n=CW)
        mix_v = w_pool_mix.rearrange("g c d -> c g d")
        out_w_v = w_out.rearrange("(k p) (h n) -> p k h n", p=P, n=CW)
        up_v = w_up.rearrange("(k p) (g n) -> p k g n", p=P, n=CW)
        down_v = w_down.rearrange("(k p) (h n) -> p k h n", p=P, n=CW)
        in2_v = w_in2.rearrange("l (k p) c -> l p k c", p=P)
        uq_v = w_uq.rearrange("l (k p) (i h c) -> l p k i h c", p=P, h=2, c=ND + RD)
        ukv_v = w_ukv.rearrange("l (k p) (i n) -> l p k i n", p=P, n=4 * ND)
        wo_v = w_o.rearrange("l (k p) (h n) -> l p k h n", p=P, n=CW)
        up2_v = w_up2.rearrange("l (k p) (v g n) -> l p k v g n", p=P, v=2, n=256)
        down2_v = w_down2.rearrange("l (k p) (h n) -> l p k h n", p=P, n=CW)

        x_t = sb("x_t", [P, KT, S])
        h_hi = sb("h_hi", [P, KT, S], F32R)
        h_lo = sb("h_lo", [P, KT, S], F32R)
        w_raw = sb("w_raw", [P, SLOTS, CW])
        w_hi = sb("w_hi", [P, SLOTS, CW], F32R)
        w_lo = sb("w_lo", [P, SLOTS, CW], F32R)
        arena = sb("arena", [P, 32, S])
        split = sb("split", [P, 21, S], F32R)
        ident = sb("ident", [P, P])
        ones = sb("ones", [P, P])
        tri = sb("tri", [P, 2, P], F32R)
        cols1 = sb("cols1", [P, N_ROWS1])
        cols_all = sb("cols_all", [P, DEPTH2, N_COLS2])
        cols2 = sb("cols2", [P, N_COLS2])
        later = cols2[:, 0:2 * P]
        consts = sb("consts", [P, 4 + LEFT])
        trig = sb("trig", [P, S])
        sq = sb("sq", [P, 4, S])
        tri_f = sq[:, 3, 0:2 * P].rearrange("p (a n) -> p a n", a=2)
        ssum = sb("ssum", [P, S])
        var = sb("var", [P, S])
        rs0 = sb("rs0", [P, S])
        rs1 = sb("rs1", [P, S])
        rstd = sb("rstd", [P, 2, S])
        tok = sb("tok", [P, 8, TT])
        soft = sb("soft", [P, 4, 4])

        x_in = arena[:, 0:8, :].rearrange("p (t a) n -> p t (a n)", t=TT)
        pos_i = arena[:, 8, :].bitcast(I32)
        ang, turns, pos_f = trig[:, :], arena[:, 10, :], arena[:, 11, :]
        x_sq = arena[:, 20:28, :]
        rows1 = arena[0:N_ROWS1, 14, 0:P]
        rows2 = ssum[0:N_ROWS2, 0:DEPTH2 * P].rearrange("p (l n) -> p l n", l=DEPTH2)
        rows_tap = [rs0[0:CONV_K, :], rs1[0:CONV_K, :]]
        rows_ftap = [r[0:2 * F2T, 0:3 * P].rearrange("p (k n) -> p k n", k=3) for r in (var, rstd[:, 0, :])]
        arena_flat = arena[:, :, :].rearrange("p a n -> p (a n)")
        u_pad = arena_flat[:, 0:HT * (LEFT + S)].rearrange("p (g n) -> p g n", g=HT)
        gates = arena[:, 5:21, :]
        o_f = arena[:, 21:25, :]
        la = arena[:, 25:27, :]
        sp = arena[:, 27:29, :]
        at = arena[:, 29:31, :]
        sq_flat = sq[:, :, :].rearrange("p a n -> p (a n)")
        wsum = sq_flat[:, 0:2 * (LEFT + S)].rearrange("p (a n) -> p a n", a=2)
        head16 = sq_flat[:, 2 * (LEFT + S):2 * (LEFT + S) + LEFT]
        pooled = u_pad[:, :, LEFT:LEFT + S]
        t_sb = arena[:, 21:25, :]
        t_pb = arena[:, 25:27, :]
        merged = arena[:, 27:29, :]
        mixg = arena[:, 0:8, :]
        xinc = arena[:, 8:12, :]
        act1 = arena
        relu = sq

        split_flat = split[:, :, :].rearrange("p a n -> p (a n)")
        q_hi, q_lo, k_hi, k_lo, v_hi, v_lo = (split[:, n, :] for n in range(6))
        l_hi = split_flat[:, 6 * S:6 * S + 2 * L_ALL].rearrange("p (h n) -> p h n", h=2)
        l_lo = split_flat[:, 6 * S + 2 * L_ALL:6 * S + 4 * L_ALL].rearrange("p (h n) -> p h n", h=2)
        at_hi, at_lo = split[:, 17:19, :], split[:, 19:21, :]
        v_f = arena[:, 31, :]
        o_hi, o_lo = split[:, 6:10, :], split[:, 10:14, :]
        pool_hi, pool_lo = split[:, 0:4, :], split[:, 14:18, :]
        as_hi, as_lo = split[:, 0:2, :], split[:, 2:4, :]

        ckv_f = arena[:, 0:2, :]
        cq_f = arena[:, 2:5, :]
        af = arena[:, 5:9, :]
        gf = arena[:, 9:13, :]
        o2_f = arena[:, 9:13, :]
        CPAD = S + 2 * HALO
        upad = arena_flat[:, 13 * S:13 * S + 4 * CPAD].rearrange("p (j n) -> p j n", j=4)
        conv = arena[:, 18:22, :]
        conv_odd = (arena[:, 22, :], arena[:, 8, :])
        prob = arena[:, 23:27, :]
        qf = arena[:, 27:29, :]
        krf = arena[:, 5, :]
        vt_f = arena[:, 5, :]
        rot = arena[:, 6:8, :]
        prod = arena[:, 29:32, :]
        conv_pools = (sq[:, 3, :], ssum[:, :], ssum[:, :], ssum[:, :])
        un = arena[:, 0:4, :]
        lat_hi, lat_lo = split[:, 0:5, :], split[:, 5:10, :]
        vvs = (arena[:, 4, :], arena[:, 7, :])
        pts = (arena[:, 0:4, :], sq[:, :, :])
        kq_hi, kq_lo = ([[h[:, 2 * q + hd, :] for hd in range(2)] for q in range(2)] for h in (h_hi, h_lo))
        kk_hi, kk_lo = ([[h[:, 4 + 2 * q + hd, :] for hd in range(2)] for q in range(2)] for h in (h_hi, h_lo))
        O_TILES, C_TILES = (0, 1, 4, 5), (2, 3, 6, 7)
        act2 = arena
        ZPAD = S + 2
        zp = arena_flat[:, 22 * S:22 * S + 4 * ZPAD].rearrange("p (j n) -> p j n", j=4)
        cz = arena[:, 27:31, :]
        y_out = arena[:, 8:16, :].rearrange("p (t a) n -> p t (a n)", t=TT)
        y_sq = arena[:, 18:26, :]
        gain_fin = arena[:, 16:18, :].rearrange("p a n -> p (a n)")

        bank_a = ctx.enter_context(nc.psum_tensor("bank_a", [P, 4, S], F32))
        bank_b = ctx.enter_context(nc.psum_tensor("bank_b", [P, 4, S], F32))
        sets = (bank_a, bank_b)

        def y_bank(t, half):
            return sets[t % 2][:, 2 * (t // 2) + half, :]

        s_banks = (bank_a[:, 2, :], bank_a[:, 3, :])
        first_banks = ((bank_a[:, 0, :], bank_a[:, 1, :]), (bank_a[:, 2, :], bank_a[:, 3, :]), bank_b[:, 0, :])
        next_banks = ((bank_b[:, 2, :], bank_b[:, 3, :]), (bank_b[:, 0, :], bank_b[:, 2, :]), bank_b[:, 0, :])

        x_land = [ctx.enter_context(nc.semaphore(f"x_land{t}")) for t in range(TT)]
        rows1_land = ctx.enter_context(nc.semaphore("rows1_land"))
        rows2_land = ctx.enter_context(nc.semaphore("rows2_land"))
        pos_land = ctx.enter_context(nc.semaphore("pos_land"))
        consts_made = ctx.enter_context(nc.semaphore("consts_made"))
        tri_made = ctx.enter_context(nc.semaphore("tri_made"))
        trig_step = ctx.enter_context(nc.semaphore("trig_step"))
        trig_sin = ctx.enter_context(nc.semaphore("trig_sin"))
        seg_done = ctx.enter_context(nc.semaphore("seg_done"))
        seg_quiet = ctx.enter_context(nc.semaphore("seg_quiet"))
        seg_open = ctx.enter_context(nc.semaphore("seg_open"))
        y_stored = ctx.enter_context(nc.semaphore("y_stored"))
        gain_land = ctx.enter_context(nc.semaphore("gain_land"))
        yt_made = ctx.enter_context(nc.semaphore("yt_made"))
        tok_sq = ctx.enter_context(nc.semaphore("tok_sq"))
        tok_step = ctx.enter_context(nc.semaphore("tok_step"))
        tok_guess = ctx.enter_context(nc.semaphore("tok_guess"))
        y_made = ctx.enter_context(nc.semaphore("y_made"))

        w_land = [sem1(f"w_land{s}") for s in range(SLOTS)]
        w_round = sem("w_round")
        w_split = sem("w_split")
        w_used = sem("w_used")
        xt_made = sem1("xt_made")
        xn_made = sem1("xn_made")
        ht_made = sem1("ht_made")
        xt_out = sem1("xt_out")
        xt_out_b = sem1("xt_out_b")
        cols_zero = sem1("cols_zero")
        cols_made = sem1("cols_made")
        cols_out = sem("cols_out")
        sq_ready = sem("sq_ready")
        sq_added = sem("sq_added")
        stat_ready = sem("stat_ready")
        var_ready = sem("var_ready")
        ln_ready = sem("ln_ready")
        guess_ready = sem("guess_ready")
        newton = sem("newton")
        rstd_ready = sem("rstd_ready")
        h_round = sem1("h_round")
        h_ready = sem1("h_ready")
        stage_round = sem1("stage_round")
        stage_ready = sem1("stage_ready")
        u_out = sem1("u_out")
        v_out = sem1("v_out")
        vt_made = sem1("vt_made")
        z_ready = sem1("z_ready")
        soft_step = sem1("soft_step")
        soft_ready = sem1("soft_ready")
        sp_step = sem1("sp_step")
        l_round = sem1("l_round")
        l_ready = sem1("l_ready")
        c_ready = sem1("c_ready")
        attn_exp = sem1("attn_exp")
        attn_masked = sem1("attn_masked")
        attn_round = sem1("attn_round")
        attn_ready = sem1("attn_ready")
        av_done = sem1("av_done")
        o_out = sem1("o_out")
        gate_out = sem1("gate_out")
        gate_ready = sem1("gate_ready")
        o_round = late_sem("o_round")
        o_split = late_sem("o_split")
        pool_step = sem1("pool_step")
        pool_ready = sem1("pool_ready")
        pool_round = sem1("pool_round")
        pool_split = sem1("pool_split")
        y_round = sem1("y_round")
        y_ready = sem1("y_ready")
        sb_out = sem1("sb_out")
        pb_out = sem1("pb_out")
        merge_ready = sem1("merge_ready")
        merge_round = sem1("merge_round")
        merge_split = sem1("merge_split")
        mix_out = sem1("mix_out")
        xinc_ready = sem1("xinc_ready")
        x_new = sem("x_new")
        x_new_v = sem1("x_new_v")
        x_new_p = sem1("x_new_p")
        xg_round = sem("xg_round")
        xg_ready = sem("xg_ready")
        r2_ready = sem1("r2_ready")
        relu_out = sem1("relu_out")
        relu_sq = sem1("relu_sq")
        a_ready = late_sem("a_ready")
        as_round = late_sem("as_round")
        as_ready = late_sem("as_ready")

        proj_out = sem("proj_out")
        cn_ready = late_sem("cn_ready")
        kr_step = late_sem("kr_step")
        kr_round = late_sem("kr_round")
        kr_ready = late_sem("kr_ready")
        glu_sig = late_sem("glu_sig")
        u_ready = late_sem("u_ready")
        pad_zero = sem("pad_zero")
        lat_round = late_sem("lat_round")
        lat_ready = late_sem("lat_ready")
        q_made = late_sem("q_made")
        qk_round = late_sem("qk_round")
        qk_ready = late_sem("qk_ready")
        s_ready = late_sem("s_ready")
        mx_step = late_sem("mx_step")
        p_exp = late_sem("p_exp")
        p_step = late_sem("p_step")
        p_ready = late_sem("p_ready")
        pt_made = late_sem("pt_made")
        vv_ready = late_sem("vv_ready")
        pt_ready = late_sem("pt_ready")
        pv_done = late_sem("pv_done")
        o2_out = late_sem("o2_out")
        tap_done = late_sem("tap_done")
        prod_ready = late_sem("prod_ready")
        prod_used = late_sem("prod_used")
        conv_sum = late_sem("conv_sum")
        k_done = late_sem("k_done")
        vt_out = late_sem("vt_out")
        v_turned = late_sem("v_turned")
        conv_ready = late_sem("conv_ready")
        mean_ready = late_sem("mean_ready")
        dev_ready = late_sem("dev_ready")
        ln_out = late_sem("ln_out")
        silu_ready = late_sem("silu_ready")
        cu_round = late_sem("cu_round")
        cu_ready = late_sem("cu_ready")
        zp_zero = late_sem("zp_zero")
        z_out = late_sem("z_out")
        z_mid = late_sem("z_mid")
        z_tap = late_sem("z_tap")
        z_conv = late_sem("z_conv")
        z_silu = late_sem("z_silu")

        block = ctx.enter_context(nc.Block())

        def products_by(g):
            return min(HT * POOL_TAPS, FIRST_PRODUCTS + -(-(HT * POOL_TAPS - FIRST_PRODUCTS) * (g + 1) // (BLOCKS - 4)))

        def taps_by(g):
            return min(HT * DVE_TAPS, -(-(products_by(g) + 2) * DVE_TAPS // POOL_TAPS))

        def meet(eng, number, beside=None):
            eng.drain().then_inc(seg_done, 1)
            if beside is not None:
                beside()
            eng.wait_ge(seg_open, number + 1)

        @block.sync
        def _(sp_):
            def load1(n, src, i=0, per=0):
                dst = w_raw[:, n % SLOTS, :]
                if len(src.shape) == 3:
                    dst = dst.rearrange("p (a b) -> p a b", a=src.shape[1])
                if n >= SLOTS:
                    sp_.wait_ge(w_split, i * per + (n - SLOTS + 1))
                sp_.dma_start(dst, src).then_inc(w_land[n % SLOTS], 16)

            for t in range(TT):
                sp_.dma_start(x_in[:, t, :], x_v[:, t, :]).then_inc(x_land[t], 16)
            at_row = 0
            for vec in (g_pre_mix, pool_scale, b_gate, g_post_mix, g_pre_mlp, g_post_mlp):
                rows = vec.shape[0] // P
                sp_.dma_start(rows1[at_row:at_row + rows, :],
                              vec.rearrange("(r p) -> r p", p=P)).then_inc(rows1_land, 16)
                at_row += rows
            for k in range(SLOTS):
                sp_.dma_start(w_raw[:, k, :].rearrange("p (b n) -> p b n", b=4),
                              in_v[:, k, :, 0, :]).then_inc(w_land[k], 16)
            sp_.dma_start(consts[:, :], shape_consts).then_inc(pos_land, 16)
            sp_.dma_start(pos_i, positions.broadcast_to((P, S))).then_inc(pos_land, 16)

            r = 0
            for vec in (g_mix, g_q, g_kv, b_dw_conv, g_conv_ln, b_conv_ln, g_ffn, b_dw_ffn):
                rows = vec.shape[1] // P
                sp_.dma_start(rows2[r:r + rows, :, :], vec.rearrange("l (r p) -> r l p", p=P)).then_inc(rows2_land, 16)
                r += rows
            for n in range(DEPTH2):
                sp_.dma_start(rows_tap[n], w_dw_conv[n]).then_inc(rows2_land, 16)
                sp_.dma_start(rows_ftap[n], w_dw_ffn[n].rearrange("k (t p) -> t k p", p=P)).then_inc(rows2_land, 16)
            for k in range(SLOTS, KT):
                load1(N_PAIR + k, in_v[:, k, :, 0, :])
            for k in range(KT):
                load1(N_PAIR + KT + k, gate_v[:, k, 0, :])
            with sp_.Fori(1, PAIRS) as i:
                for k in range(KT):
                    sp_.wait_ge(w_split, i * (2 * KT) + (k - SLOTS + 1))
                    sp_.dma_start(w_raw[:, k % SLOTS, :].rearrange("p (b n) -> p b n", b=4),
                                  in_v[:, k, :, i, :]).then_inc(w_land[k % SLOTS], 16)
                for k in range(KT):
                    sp_.wait_ge(w_split, i * (2 * KT) + (KT + k - SLOTS + 1))
                    sp_.dma_start(w_raw[:, k % SLOTS, :], gate_v[:, k, i, :]).then_inc(w_land[k % SLOTS], 16)
            load1(N_MIX, mix_v)
            for k in range(HT):
                load1(N_SB0 + k, sb_v[:, k, 0, :])
            for k in range(HT):
                load1(N_PB0 + k, pb_v[:, k, 0, :])
            for k in range(HT):
                load1(N_SB1 + k, sb_v[:, k, 1, :])
            for k in range(HT):
                load1(N_PB1 + k, pb_v[:, k, 1, :])
            for half in range(2):
                for k in range(KT):
                    load1(N_OUT + half * KT + k, out_w_v[:, k, half, :])
            with sp_.Fori(0, F1G) as g:
                for k in range(KT):
                    load1(N_UP + k, up_v[:, k, g, :], g, KT)
            with sp_.Fori(0, F1T // 2) as kk:
                for k in range(2):
                    for half in range(2):
                        load1(N_DOWN + 2 * k + half,
                              down_v.rearrange("p (kk two) h n -> p kk two h n", two=2)[:, kk, k, half, :],
                              kk, 4)

            def quiet(engines):
                sp_.wait_ge(seg_done, engines)
                sp_.sem_inc(seg_quiet, 1)
                for s in w_land:
                    sp_.sem_clear(s)

            def reopen():
                for s in sems:
                    sp_.sem_clear(s)
                sp_.sem_inc(seg_open, 1)
                for s in late_sems:
                    sp_.sem_clear(s)

            quiet(4)

            with sp_.Fori(0, DEPTH2) as l:
                def load2(n, parts, i=0, per=0):
                    if n >= SLOTS:
                        sp_.wait_ge(w_split, i * per + (n - SLOTS + 1))
                    for dst, src in parts:
                        sp_.dma_start(dst, src).then_inc(w_land[n % SLOTS], 16)

                for part in range(2):
                    c0 = QL + KVL + RD + part * CW
                    for k in range(KT):
                        n = M_A + part * KT + k
                        load2(n, [(w_raw[:, n % SLOTS, :], in2_v[l, :, k, c0:c0 + CW])])
                        if n == SLOTS - 1:
                            reopen()
                for k in range(KT):
                    n = M_Q + k
                    load2(n, [(w_raw[:, n % SLOTS, 0:QL], in2_v[l, :, k, 0:QL])])
                for k in range(KT):
                    n = M_KV + k
                    slot = w_raw[:, n % SLOTS, :]
                    r0 = QL + KVL
                    load2(n, [(slot[:, 0:KVL + RD], in2_v[l, :, k, QL:r0 + RD]),
                              (slot[:, KVL + RD:KVL + RD + RD // 2], in2_v[l, :, k, r0 + RD // 2:r0 + RD]),
                              (slot[:, KVL + RD + RD // 2:KV_COLS], in2_v[l, :, k, r0:r0 + RD // 2])])
                for i in range(PAIRS):
                    for k in range(QT):
                        n = M_PAIR + i * SLOTS + k
                        slot = w_raw[:, n % SLOTS, 0:2 * P].rearrange("p (h c) -> p h c", h=2)
                        load2(n, [(slot[:, :, 0:ND + RD], uq_v[l, :, k, i, :, :]),
                                  (slot[:, :, ND + RD:ND + RD + RD // 2], uq_v[l, :, k, i, :, ND + RD // 2:ND + RD]),
                                  (slot[:, :, ND + RD + RD // 2:P], uq_v[l, :, k, i, :, ND:ND + RD // 2])])
                    n = M_PAIR + i * SLOTS + QT
                    load2(n, [(w_raw[:, n % SLOTS, :].rearrange("p (k c) -> p k c", k=KVT), ukv_v[l, :, :, i, :])])
                for n, (half, k) in enumerate(WO_ORDER, M_WO):
                    load2(n, [(w_raw[:, n % SLOTS, :], wo_v[l, :, k, half, :])])
                with sp_.Fori(0, F2G) as g:
                    for k in range(KT):
                        n = M_UP + k
                        load2(n, [(w_raw[:, n % SLOTS, :].rearrange("p (v c) -> p v c", v=2), up2_v[l, :, k, :, g, :])],
                              g, KT)
                d2 = down2_v.rearrange("l p (kk two) h n -> l p kk two h n", two=2)
                with sp_.Fori(0, F2T // 2) as kk:
                    for k in range(2):
                        for half in range(2):
                            n = M_DOWN + 2 * k + half
                            load2(n, [(w_raw[:, n % SLOTS, :], d2[l, :, kk, k, half, :])], kk, 4)
                quiet(l * 4 + 8)

            sp_.dma_start(gain_fin, g_final.rearrange("(a d) -> a d", a=1).broadcast_to((P, D))).then_inc(gain_land, 16)
            sp_.sem_inc(seg_open, 1)

            for t in range(TT):
                sp_.wait_ge(y_made, 2 * t + 2)
                sp_.dma_start(out_v[:, t, :], y_out[:, t, :]).then_inc(y_stored, 16)
            sp_.wait_ge(y_stored, 16 * TT)

        @block.gpsimd
        def _(pool):
            steps = 0

            def made(ins):
                nonlocal steps
                steps += 1
                ins.then_inc(consts_made, 1)
                pool.wait_ge(consts_made, steps)

            made(nc.gpsimd.memset(ident[:, :], 0.0))
            made(nc.gpsimd.affine_select(out=ident[:, :], in_=ident[:, :], compare_op=ALU.not_equal, fill=1.0,
                                         base=0, pattern=[[-1, P]], channel_multiplier=1))
            made(nc.gpsimd.memset(ones[:, :], 1.0))
            made(nc.gpsimd.memset(tri_f, -1.0))
            made(nc.gpsimd.affine_select(out=tri_f[:, 0, :], in_=tri_f[:, 0, :], compare_op=ALU.is_ge, fill=0.0,
                                         base=0, pattern=[[-1, P]], channel_multiplier=1))
            made(nc.gpsimd.memset(later, 1.0))
            made(nc.gpsimd.affine_select(out=later, in_=later, compare_op=ALU.is_gt, fill=0.0,
                                         base=-P, pattern=[[1, 2 * P]], channel_multiplier=-1))

            def add_squares(count, before_sq, before_add, before_stat):
                for t in range(1, count):
                    pool.wait_ge(sq_ready, before_sq + t + 1)
                    if t == 1 and before_stat:
                        pool.wait_ge(stat_ready, before_stat)
                    if t > 1:
                        pool.wait_ge(sq_added, before_add + t - 1)
                    nc.gpsimd.tensor_tensor(ssum[:, :], sq[:, 0, :] if t == 1 else ssum[:, :], sq[:, t % 4, :],
                                            ALU.add).then_inc(sq_added, 1)

            pool_steps = 1

            def pool_group(g):

                def pstep(ins):
                    nonlocal pool_steps
                    pool_steps += 1
                    ins.then_inc(pool_step, 1)
                    pool.wait_ge(pool_step, pool_steps)

                w = WINDOWS[g]
                src, d, turn = u_pad[:, g, :], 1, 0
                while d < w:
                    lo = LEFT - (w - 2 * d)
                    dst = wsum[:, turn % 2, :]
                    pstep(nc.gpsimd.tensor_tensor(dst[:, lo:LEFT + S], src[:, lo:LEFT + S], src[:, lo - d:LEFT + S - d],
                                                  ALU.add))
                    src, d, turn = dst, 2 * d, turn + 1
                pstep(nc.gpsimd.tensor_tensor(head16[:, 0:w], src[:, LEFT:LEFT + w], consts[:, 4:4 + w], ALU.mult))
                pstep(nc.gpsimd.tensor_tensor(pooled[:, g, 0:w], head16[:, 0:w], pooled[:, g, 0:w], ALU.subtract))
                dst = wsum[:, turn % 2, LEFT + w:LEFT + S]
                pstep(nc.gpsimd.tensor_scalar(dst, src[:, LEFT + w:LEFT + S], 1.0 / w, None, ALU.mult))
                nc.gpsimd.tensor_tensor(pooled[:, g, w:S], dst, pooled[:, g, w:S], ALU.subtract).then_inc(pool_ready, 1)
                pool.wait_ge(pool_ready, g + 1)

            def x_update(turn):
                for f in range(1, KT, 2):
                    pool.wait_ge(xinc_ready, turn * KT + f + 1)
                    nc.gpsimd.tensor_tensor(x_t[:, f, :], x_t[:, f, :], xinc[:, f % 4, :], ALU.add).then_inc(x_new_p, 1)

            pool.wait_ge(pos_land, 32)
            pool.wait_ge(pool_step, 1)
            for g in range(HT):
                pool.wait_ge(u_out, g + 1)
                pool_group(g)
            x_update(0)
            add_squares(KT, KT, KT - 1, 1)
            meet(pool, 0, lambda: x_update(1))
            with pool.Fori(0, DEPTH2) as l:
                add_squares(KT, 0, 0, 0)
                for i in range(HT):
                    for r in range(1, POOL_TAPS):
                        pool.wait_ge(prod_ready, i * POOL_TAPS + r + 1)
                        if i > 0 and r == 1:
                            pool.wait_ge(conv_ready, i)
                            pool.wait_ge(stat_ready, 3)
                        if r > 1:
                            pool.wait_ge(prod_used, i * (POOL_TAPS - 1) + r - 1)
                        nc.gpsimd.tensor_tensor(conv_pools[i], prod[:, i * POOL_TAPS % 3, :] if r == 1 else conv_pools[i],
                                                prod[:, (i * POOL_TAPS + r) % 3, :], ALU.add).then_inc(prod_used, 1)
                    pool.wait_ge(tap_done, (i + 1) * DVE_TAPS)
                    pool.wait_ge(prod_used, (i + 1) * (POOL_TAPS - 1))
                    nc.gpsimd.tensor_tensor(conv_pools[i], conv_pools[i], conv_odd[i % 2], ALU.add).then_inc(conv_sum, 1)
                    pool.wait_ge(conv_sum, i + 1)
                    nc.gpsimd.tensor_tensor(conv[:, i, :], conv[:, i, :], conv_pools[i], ALU.add).then_inc(conv_ready, 1)
                add_squares(KT, KT + KVT + QT + HT, KT + KVT + QT + HT - 4, 4)
                meet(pool, l + 1)

        @block.scalar
        def _(act):
            def split1(n, i=0, per=0):
                s = n % SLOTS
                act.wait_ge(w_land[s], i * (16 * per // SLOTS) + 16 * (n // SLOTS + 1))
                if n >= SLOTS:
                    act.wait_ge(w_used, i * per + (n - SLOTS + 1))
                nc.scalar.activation(w_hi[:, s, :], w_raw[:, s, :], ACT.Copy).then_inc(w_round, 1)

            def rsqrt_guess(number):
                act.wait_ge(var_ready, number)
                nc.scalar.activation(rs0[:, :], var[:, :], ACT.Ln).then_inc(ln_ready, 1)
                act.wait_ge(ln_ready, number)
                nc.scalar.activation(rs1[:, :], rs0[:, :], ACT.Exp, scale=-0.5).then_inc(guess_ready, 1)

            def square(src, t, before_sq, before_add, on_pe=False):
                if t >= 4:
                    act.wait_ge(sq_added, before_add + (t - 3 if on_pe else max(t - 4, 1)))
                nc.scalar.activation(sq[:, t % 4, :], src, ACT.Square).then_inc(sq_ready, 1)

            def tokens_guess(number, c):
                act.wait_ge(tok_step, 5 * (number - 1) + 2)
                nc.scalar.activation(tok[:, 3, c], tok[:, 2, c], ACT.Ln).then_inc(tok_guess, 1)
                act.wait_ge(tok_guess, 2 * number - 1)
                nc.scalar.activation(tok[:, 4, c], tok[:, 3, c], ACT.Exp, scale=-0.5).then_inc(tok_guess, 1)

            nc.scalar.preload_act_table_set(LN_EXP)
            for t in range(TT):
                act.wait_ge(x_land[t], 16)
                for half in range(2):
                    nc.scalar.activation(x_sq[:, 2 * t + half, :], x_in[:, t, half * S:half * S + S], ACT.Square,
                                         accum_out=tok[:, half, t:t + 1]).then_inc(tok_sq, 1)
            tokens_guess(1, slice(0, TT))
            act.wait_ge(xt_made, TT)
            for f in range(4):
                nc.scalar.activation(x_t[:, f, :], bank_a[:, f, :], ACT.Copy).then_inc(xt_out, 1)
            for n in range(SLOTS):
                split1(n)
            act.wait_ge(ht_made, TT)
            act.wait_ge(cols_out, 1)
            for f in range(KT):
                nc.scalar.activation(h_hi[:, f, :], sets[f // 4][:, f % 4, :], ACT.Copy,
                                     scale=cols1[:, C_PRE + f:C_PRE + f + 1]).then_inc(h_round, 1)
            act.wait_ge(consts_made, 5)
            nc.scalar.activation(tri[:, :, :], tri_f, ACT.Copy).then_inc(tri_made, 1)

            with act.Fori(0, PAIRS) as i:
                for k in range(KT):
                    split1(N_PAIR + SLOTS + k, i, 2 * KT)
                act.wait_ge(w_used, i * (2 * KT) + KT)
                nc.scalar.activation(q_hi, bank_a[:, 1, :], ACT.Copy, scale=Q_SCALE).then_inc(stage_round, 1)
                nc.scalar.activation(k_hi, bank_a[:, 2, :], ACT.Copy).then_inc(stage_round, 1)
                nc.scalar.activation(u_pad[:, i, LEFT:LEFT + S], bank_a[:, 0, :], ACT.Copy).then_inc(u_out, 1)
                nc.scalar.activation(v_f, bank_a[:, 3, :], ACT.Copy).then_inc(v_out, 1)
                act.wait_ge(vt_made, i + 1)
                nc.scalar.activation(v_hi, bank_a[:, 3, :], ACT.Copy).then_inc(stage_round, 1)
                for s in range(9):
                    if s < 7:
                        split1(N_PAIR + SLOTS + KT + s, i, 2 * KT)
                    if s < 8:
                        kb = 3 - s % 4
                        n = S - Q0[kb]
                        z = bank_a[:, s % 2, 0:n]
                        act.wait_ge(z_ready, i * 8 + (s + 1))
                        nc.scalar.activation(la[:, s % 2, 0:n], z, ACT.Abs).then_inc(soft_step, 1)
                        act.wait_ge(soft_step, i * 16 + (2 * s + 1))
                        nc.scalar.activation(la[:, s % 2, 0:n], la[:, s % 2, 0:n], ACT.Exp, scale=-1.0).then_inc(soft_step, 1)
                        act.wait_ge(soft_step, i * 16 + (2 * s + 2))
                        nc.scalar.activation(la[:, s % 2, 0:n], la[:, s % 2, 0:n], ACT.Ln, bias=1.0).then_inc(soft_ready, 1)
                    if s >= 1:
                        kb1 = 3 - (s - 1) % 4
                        n1 = S - Q0[kb1]
                        act.wait_ge(c_ready, i * 8 + s)
                        nc.scalar.activation(at[:, (s - 1) % 2, 0:n1], bank_a[:, (s - 1) % 2, 0:n1], ACT.Exp).then_inc(attn_exp, 1)
                    if s < 8:
                        act.wait_ge(sp_step, i * 16 + (2 * s + 2))
                        off = L_OFF[kb]
                        nc.scalar.activation(l_hi[:, s // 4, off:off + n], sp[:, s % 2, 0:n], ACT.Copy).then_inc(l_round, 1)
                    if s >= 1:
                        act.wait_ge(attn_masked, i * 8 + s)
                        if s >= 3:
                            act.wait_ge(av_done, i * 8 + (s - 2))
                        nc.scalar.activation(at_hi[:, (s - 1) % 2, 0:n1], at[:, (s - 1) % 2, 0:n1], ACT.Copy).then_inc(attn_round, 1)
                    if s == 5 or s == 8:
                        hd = 0 if s == 5 else 1
                        rows = slice(HEAD * hd, HEAD * hd + HEAD)
                        act.wait_ge(av_done, i * 8 + 4 * (hd + 1))
                        nc.scalar.activation(o_f[rows, i, :], bank_a[rows, 2 + hd, :], ACT.Copy).then_inc(o_out, 1)
                split1(N_PAIR + SLOTS + KT + 7, i, 2 * KT)
                act.wait_ge(w_used, i * (2 * KT) + 2 * KT)
                for j in range(4):
                    nc.scalar.activation(gates[:, i * 4 + j, :], bank_b[:, j, :], ACT.Identity,
                                         bias=cols1[:, bass.ds(i * 4 + (C_BG + j), 1)]).then_inc(gate_out, 1)

            for g in range(HT):
                act.wait_ge(pool_ready, g + 1)
                nc.scalar.activation(pool_hi[:, g, :], pooled[:, g, :], ACT.Copy).then_inc(pool_round, 1)
            act.wait_ge(o_out, 2 * PAIRS)
            for t in range(HT):
                nc.scalar.activation(o_hi[:, t, :], o_f[:, t, :], ACT.Copy).then_inc(o_round, 1)
            act.wait_ge(gate_out, 16)

            def sigmoid_gates(q):
                nc.scalar.activation(gates[:, 4 * q:4 * q + 4, :], gates[:, 4 * q:4 * q + 4, :],
                                     ACT.Sigmoid).then_inc(gate_ready, 1)

            split1(N_SB0 + HT - 1)
            act.wait_ge(w_used, N_MIX + 1)
            for g in range(HT):
                nc.scalar.activation(h_hi[:, HT + g, :], bank_b[:, g, :], ACT.Copy,
                                     scale=cols1[:, C_PSC + g:C_PSC + g + 1]).then_inc(y_round, 1)
            sigmoid_gates(2)
            for k in range(HT):
                split1(N_PB0 + k)
            sigmoid_gates(0)
            sigmoid_gates(3)
            sigmoid_gates(1)
            act.wait_ge(trig_step, 10)
            nc.scalar.activation(trig[ND:P, :], ang[ND:P, :], ACT.Sin).then_inc(trig_sin, 1)

            def merge_hi(half):
                for j in range(4):
                    act.wait_ge(merge_ready, 4 * half + j + 1)
                    nc.scalar.activation(h_hi[:, 4 * half + j, :], merged[:, j % 2, :], ACT.Copy).then_inc(merge_round, 1)

            for k in range(HT):
                split1(N_SB1 + k)
            merge_hi(0)
            for k in range(HT):
                split1(N_PB1 + k)
            for k in range(HT):
                split1(N_OUT + k)
            act.wait_ge(w_used, N_PB1 + HT)
            merge_hi(1)
            for k in range(N_OUT + SLOTS, N_OUT + KT + SLOTS):
                split1(k)
            nc.scalar.preload_act_table_set(LN_EXP)

            def post_squares(last_chunk, tiles, before_sq, before_add):
                act.wait_ge(w_used, last_chunk + 1)
                for f in tiles:
                    square(sets[f // 4][:, f % 4, :], f, before_sq, before_add, True)

            post_squares(N_OUT + KT - 1, range(4), 0, 0)
            for k in range(N_OUT + KT + SLOTS, N_UP + SLOTS):
                split1(k)
            post_squares(N_UP - 1, range(4, 8), 0, 0)
            rsqrt_guess(1)
            for f in range(KT):
                act.wait_ge(x_new_p if f % 2 else x_new_v, f // 2 + 1)
                nc.scalar.activation(h_hi[:, f, :], x_t[:, f, :], ACT.Copy,
                                     scale=cols1[:, C_PMLP + f:C_PMLP + f + 1]).then_inc(xg_round, 1)
                square(x_t[:, f, :], f, KT, KT - 1)

            def up1_out(g, i=0, gper=0):
                set_ = sets[g % 2]
                act.wait_ge(w_used, i * (gper * KT) + (N_UP + g * KT + KT))
                for j in range(4):
                    t = 4 * g + j
                    if t >= 4:
                        act.wait_ge(a_ready, i * (4 * gper) + (t - 3))
                    nc.scalar.activation(relu[:, j, :], set_[:, j, :], ACT.Relu).then_inc(relu_out, 1)
                split1(N_UP + SLOTS + (1 + g) * KT, i, gper * KT)
                for j in range(4):
                    t = 4 * g + j
                    act.wait_ge(relu_out, i * (4 * gper) + (t + 1))
                    nc.scalar.activation(relu[:, j, :], relu[:, j, :], ACT.Square).then_inc(relu_sq, 1)
                for k in range(1, 4):
                    split1(N_UP + SLOTS + (1 + g) * KT + k, i, gper * KT)

            for k in range(KT):
                split1(N_UP + SLOTS + k)
            rsqrt_guess(2)
            up1_out(0)
            with act.Fori(0, F1G // 2 - 1) as i:
                for g in range(1, 3):
                    for k in range(4, KT):
                        split1(N_UP + SLOTS + g * KT + k, i, 2 * KT)
                    up1_out(g, i, 2)
            for k in range(4, KT):
                split1(N_UP + SLOTS + (F1G - 1) * KT + k)

            def act_split(k, n, need_free, i=0):
                act.wait_ge(a_ready, i * 2 + (k + 1))
                if need_free:
                    act.wait_ge(w_used, i * 4 + n)
                nc.scalar.activation(as_hi[:, k % 2, :], act1[:, i * 2 + k, :], ACT.Copy).then_inc(as_round, 1)

            for k in range(2):
                act_split(k, 0, False)
            up1_out(F1G - 1)
            for k in range(2):
                act_split(k + 2, N_DOWN + 2 * k + 2, True)
            with act.Fori(0, F1T // 2 - 2) as kk:
                for k in range(2):
                    split1(N_DOWN + 2 * SLOTS + 2 * k, kk, 4)
                    split1(N_DOWN + 2 * SLOTS + 2 * k + 1, kk, 4)
                    act_split(k + 4, N_DOWN + SLOTS + 2 * k + 2, True, kk)
            post_squares(N_END1 - 2, range(4), 2 * KT, 2 * (KT - 1))
            post_squares(N_END1 - 1, range(4, 8), 2 * KT, 2 * (KT - 1))
            rsqrt_guess(3)
            meet(act, 0)

            with act.Fori(0, DEPTH2) as l:
                def split2(n, i=0, per=0):
                    s, c = n % SLOTS, width2(n)
                    act.wait_ge(w_land[s], i * (16 * pieces2(n) * per // SLOTS) + landed2(n))
                    if n >= SLOTS:
                        act.wait_ge(w_used, i * per + (n - SLOTS + 1))
                    nc.scalar.activation(w_hi[:, s, 0:c], w_raw[:, s, 0:c], ACT.Copy).then_inc(w_round, 1)

                act.wait_ge(cols_out, 1)
                for f in range(KT):
                    act.wait_ge(x_new_p if f % 2 else x_new_v, HALF_TILES + f // 2 + 1)
                    nc.scalar.activation(h_hi[:, f, :], x_t[:, f, :], ACT.Copy,
                                         scale=cols2[:, L_MIX + f:L_MIX + f + 1]).then_inc(xg_round, 1)
                    if f < SLOTS:
                        split2(f)
                for f in range(KT):
                    square(x_t[:, f, :], f, 0, 0)
                    if f >= 4:
                        split2(M_A + f)
                for k in range(4, KT):
                    split2(M_A + SLOTS + k)
                rsqrt_guess(1)
                for k in range(KT):
                    split2(M_G + SLOTS + k)
                for j in range(4):
                    act.wait_ge(proj_out, 4 + j + 1)
                    nc.scalar.activation(gf[:, j, :], gf[:, j, :], ACT.Sigmoid).then_inc(glu_sig, 1)
                nc.scalar.preload_act_table_set(LN_EXP)
                prods = 0

                def products(count):
                    nonlocal prods
                    for n in range(prods, min(prods + count, HT * POOL_TAPS)):
                        i, r = n // POOL_TAPS, n % POOL_TAPS
                        if r == 0:
                            act.wait_ge(u_ready, i + 1)
                            act.wait_ge(pad_zero, 2)
                        if n >= 3:
                            i3, r3 = (n - 3) // POOL_TAPS, (n - 3) % POOL_TAPS
                            act.wait_ge(prod_used, i3 * (POOL_TAPS - 1) + max(r3, 1))
                        nc.scalar.activation(prod[:, n % 3, :], upad[:, i, DVE_TAPS + r:DVE_TAPS + r + S], ACT.Copy,
                                             scale=cols2[:, L_TAP + i * 32 + DVE_TAPS + r:L_TAP + i * 32 + DVE_TAPS + r + 1]
                                             ).then_inc(prod_ready, 1)
                        prods += 1

                for k in range(KT):
                    split2(M_Q + SLOTS + k)
                    if k >= 4:
                        products(1)
                for t in range(QT):
                    act.wait_ge(proj_out, 8 + t + 1)
                    square(cq_f[:, t, :], t, KT, KT - 1)
                for k in range(4):
                    split2(M_KV + SLOTS + k)
                    products(1)
                rsqrt_guess(2)
                for t in range(QT):
                    act.wait_ge(cn_ready, t + 1)
                    nc.scalar.activation(lat_hi[:, t, :], cq_f[:, t, :], ACT.Copy).then_inc(lat_round, 1)
                for k in range(QT):
                    split2(M_PAIR + k)
                    products(1)
                for t in range(KVT):
                    act.wait_ge(proj_out, 8 + QT + t + 1)
                    square(ckv_f[:, t, :], t, KT + QT, KT + QT - 2)
                split2(M_PAIR + QT)
                rsqrt_guess(3)
                act.wait_ge(kr_step, 4)
                for q in range(2):
                    for hd in range(2):
                        nc.scalar.activation(kk_hi[q][hd][ND:P, :], rot[ND:P, 0, :], ACT.Copy).then_inc(kr_round, 1)
                for t in range(KVT):
                    act.wait_ge(cn_ready, QT + t + 1)
                    nc.scalar.activation(lat_hi[:, QT + t, :], ckv_f[:, t, :], ACT.Copy).then_inc(lat_round, 1)

                def stage_q(i):
                    for hd in range(2):
                        act.wait_ge(q_made, 2 * i + hd + 1)
                        nc.scalar.activation(kq_hi[i % 2][hd], qf[:, hd, :], ACT.Copy).then_inc(qk_round, 1)

                def stage_k(i, hd, bank):
                    if hd == 0:
                        act.wait_ge(k_done, i + 1)
                    else:
                        act.wait_ge(w_used, M_PAIR + (i + 1) * SLOTS)
                    nc.scalar.activation(kk_hi[i % 2][hd][0:ND, :], bank[0:ND, :], ACT.Copy).then_inc(qk_round, 1)
                    nc.scalar.activation(vt_f[hd * ND:hd * ND + ND, :], bank[ND:P, :], ACT.Copy).then_inc(vt_out, 1)

                def stage_v(i, bank):
                    act.wait_ge(v_turned, i + 1)
                    nc.scalar.activation(vvs[i % 2], bank, ACT.Copy).then_inc(vv_ready, 1)

                stage_q(0)
                products(3)
                for hd in range(2):
                    stage_k(0, hd, first_banks[1][hd])
                stage_v(0, first_banks[2])
                for k in range(SLOTS):
                    split2(M_PAIR + SLOTS + k)

                def out_of(i, hd):
                    rows = slice(ND * hd, ND * hd + ND)
                    act.wait_ge(pv_done, i * 2 + hd + 1)
                    nc.scalar.activation(o2_f[rows, i, :], bank_b[rows, 1, :], ACT.Copy).then_inc(o2_out, 1)

                for g in range(BLOCKS + 2):
                    i, m = g // (2 * TT), g % (2 * TT)
                    if g < BLOCKS:
                        b = g % TT
                        act.wait_ge(mx_step, g + 1)
                        nc.scalar.activation(prob[:, b, :], s_banks[g % 2], ACT.Exp,
                                             bias=soft[:, 1, b:b + 1], accum_out=soft[:, 2, b:b + 1]).then_inc(p_exp, 1)
                    if g >= 2:
                        b = (g - 2) % TT
                        act.wait_ge(pt_made, g - 1)
                        head = (g - 2) // TT
                        if b == 0 and head == 1:
                            act.wait_ge(conv_ready, 1)
                        if b == 0 and head >= 2:
                            act.wait_ge(pv_done, head - 1)
                        nc.scalar.activation(pts[head % 2][:, :, b * P:b * P + P],
                                             bank_a[:, g % 2, :].rearrange("p (k q) -> p k q", k=TT),
                                             ACT.Copy).then_inc(pt_ready, 1)
                    if m == 0 and i >= 1:
                        out_of(i - 1, 0)
                        if i < PAIRS:
                            stage_v(i, next_banks[2])
                    if m == TT and i >= 1:
                        out_of(i - 1, 1)
                    if i + 1 < PAIRS:
                        if m == 5:
                            stage_q(i + 1)
                            stage_k(i + 1, 0, next_banks[1][0])
                        if m == 6:
                            stage_k(i + 1, 1, next_banks[1][1])
                        if m in (2, 3, 4, 7):
                            split2(M_PAIR + (i + 2) * SLOTS + (2, 3, 4, 7).index(m))
                    elif m in (3, 4, 5) and i < PAIRS:
                        t = m - 3
                        act.wait_ge(o2_out, 2 * t + 2)
                        nc.scalar.activation(h_hi[:, O_TILES[t], :], o2_f[:, t, :], ACT.Copy).then_inc(o_round, 1)
                    products(products_by(g) - prods)
                out_of(PAIRS - 1, 1)
                products(HT * POOL_TAPS)

                act.wait_ge(o2_out, 2 * PAIRS)
                nc.scalar.activation(h_hi[:, O_TILES[3], :], o2_f[:, 3, :], ACT.Copy).then_inc(o_round, 1)
                split2(M_WO + 4)
                for j in range(HT):
                    act.wait_ge(dev_ready, j + 1)
                    square(conv[:, j, :], j, KT + KVT + QT, KT + KVT + QT - 3)
                for k in range(5, 8):
                    split2(M_WO + k)
                rsqrt_guess(4)
                nc.scalar.preload_act_table(ACT.Silu)
                for j in range(HT):
                    act.wait_ge(ln_out, j + 1)
                    nc.scalar.activation(un[:, j, :], conv[:, j, :], ACT.Silu, scale=cols2[:, L_GLN + j:L_GLN + j + 1],
                                         bias=cols2[:, L_BLN + j:L_BLN + j + 1]).then_inc(silu_ready, 1)
                for j in range(HT):
                    act.wait_ge(silu_ready, j + 1)
                    nc.scalar.activation(h_hi[:, C_TILES[j], :], un[:, j, :], ACT.Copy).then_inc(cu_round, 1)
                nc.scalar.preload_act_table_set(LN_EXP)
                for n in range(M_WO + 8, M_UP + SLOTS):
                    split2(n)
                act.wait_ge(w_used, M_UP)
                for f in range(KT):
                    act.wait_ge(x_new, f + 1)
                    nc.scalar.activation(h_hi[:, f, :], x_t[:, f, :], ACT.Copy,
                                         scale=cols2[:, L_FFN + f:L_FFN + f + 1]).then_inc(xg_round, 1)
                    square(x_t[:, f, :], f, KT + KVT + QT + HT, KT + KVT + QT + HT - 4)

                def mid_and_silu(g, i=0, gper=0):
                    if g:
                        act.wait_ge(a_ready, i * (2 * gper) + 2 * g)
                    for j in range(4):
                        tile = i * (2 * gper) + (2 * g + j % 2 + F2T * (j // 2))
                        act.wait_ge(z_out, i * (4 * gper) + (4 * g + j + 1))
                        nc.scalar.activation(cz[:, j, :], zp[:, j, 1:1 + S], ACT.Identity,
                                             scale=cols2[:, bass.ds(tile + (L_FTAP + 2 * F2T), 1)],
                                             bias=cols2[:, bass.ds(tile + L_BFF, 1)]).then_inc(z_mid, 1)
                    for k in range(2):
                        split2(M_UP + SLOTS + (1 + g) * KT + k, i, gper * KT)
                    for j in range(2):
                        act.wait_ge(z_conv, i * (4 * gper) + (4 * g + j + 1))
                        nc.scalar.activation(cz[:, j, :], cz[:, j, :], ACT.Silu).then_inc(z_silu, 1)
                    for k in range(2, 4):
                        split2(M_UP + SLOTS + (1 + g) * KT + k, i, gper * KT)

                for k in range(KT):
                    split2(M_UP + SLOTS + k)
                rsqrt_guess(5)
                nc.scalar.preload_act_table(ACT.Silu)
                mid_and_silu(0)
                with act.Fori(0, F2G // 2 - 1) as i:
                    for g in range(1, 3):
                        for k in range(4, KT):
                            split2(M_UP + SLOTS + g * KT + k, i, 2 * KT)
                        mid_and_silu(g, i, 2)
                for k in range(4, KT):
                    split2(M_UP + SLOTS + (F2G - 2) * KT + k)
                mid_and_silu(F2G - 2)
                for k in range(4, KT):
                    split2(M_UP + SLOTS + (F2G - 1) * KT + k)

                def act_split2(k, n, need_free, i=0):
                    act.wait_ge(a_ready, i * 2 + (k + 1))
                    if need_free:
                        act.wait_ge(w_used, i * 4 + n)
                    nc.scalar.activation(as_hi[:, k % 2, :], act2[:, i * 2 + k, :], ACT.Copy).then_inc(as_round, 1)

                for k in range(2):
                    act_split2(k, 0, False)
                mid_and_silu(F2G - 1)
                for k in range(2):
                    act_split2(k + 2, M_DOWN + 2 * k + 2, True)
                with act.Fori(0, F2T // 2 - 2) as kk:
                    for k in range(2):
                        split2(M_DOWN + 2 * SLOTS + 2 * k, kk, 4)
                        split2(M_DOWN + 2 * SLOTS + 2 * k + 1, kk, 4)
                        act_split2(k + 4, M_DOWN + SLOTS + 2 * k + 2, True, kk)
                nc.scalar.preload_act_table_set(LN_EXP)
                meet(act, l + 1)

            for pair in range(2):
                for t in range(2 * pair, 2 * pair + 2):
                    act.wait_ge(yt_made, t + 1)
                    for half in range(2):
                        nc.scalar.activation(y_sq[:, 2 * t + half, :], y_bank(t, half), ACT.Square,
                                             accum_out=tok[:, half, t:t + 1]).then_inc(tok_sq, 1)
                tokens_guess(2 + pair, slice(2 * pair, 2 * pair + 2))

        @block.vector
        def _(dve):
            def tt(out_, a, b, op):
                return nc.vector.tensor_tensor(out_, a, b, op)

            def stt(out_, a, s, b, op0, op1):
                return nc.vector.scalar_tensor_tensor(out=out_, in0=a, scalar=s, in1=b, op0=op0, op1=op1)

            def rest(out_, full, hi):
                return tt(out_, full, hi.bitcast(F32), ALU.subtract)

            def split_lo(n, c=CW, i=0, per=0):
                s = n % SLOTS
                dve.wait_ge(w_round, i * per + (n + 1))
                rest(w_lo[:, s, 0:c], w_raw[:, s, 0:c], w_hi[:, s, 0:c]).then_inc(w_split, 1)

            def rstd_of(number, bank, width=D):
                dve.wait_ge(stat_ready, number)
                nc.vector.tensor_scalar(var[:, :], bank, 1.0 / width, EPS, ALU.mult, ALU.add).then_inc(var_ready, 1)
                dve.wait_ge(guess_ready, number)
                tt(rs0[:, :], rs1[:, :], rs1[:, :], ALU.mult).then_inc(newton, 1)
                dve.wait_ge(newton, 2 * number - 1)
                stt(rs0[:, :], rs0[:, :], -0.5, var[:, :], ALU.mult, ALU.mult).then_inc(newton, 1)
                dve.wait_ge(newton, 2 * number)
                stt(rstd[:, number % 2, :], rs0[:, :], 1.5, rs1[:, :], ALU.add, ALU.mult).then_inc(rstd_ready, 1)

            def rstd_into(number, bank, width, beside=None):
                dve.wait_ge(stat_ready, number)
                nc.vector.tensor_scalar(var[:, :], bank, 1.0 / width, EPS, ALU.mult, ALU.add).then_inc(var_ready, 1)
                if beside is not None:
                    beside()
                dve.wait_ge(guess_ready, number)
                tt(rs0[:, :], rs1[:, :], rs1[:, :], ALU.mult).then_inc(newton, 1)
                dve.wait_ge(newton, 2 * number - 1)
                stt(rs0[:, :], rs0[:, :], -0.5, var[:, :], ALU.mult, ALU.mult).then_inc(newton, 1)
                dve.wait_ge(newton, 2 * number)
                stt(rstd[:, 0, :], rs0[:, :], 1.5, rs1[:, :], ALU.add, ALU.mult).then_inc(rstd_ready, 1)
                dve.wait_ge(rstd_ready, number)

            def add_square(t, before_sq, before_add, before_stat):
                if t == 0:
                    return
                dve.wait_ge(sq_ready, before_sq + t + 1)
                if t == 1 and before_stat:
                    dve.wait_ge(stat_ready, before_stat)
                if t > 1:
                    dve.wait_ge(sq_added, before_add + t - 1)
                tt(ssum[:, :], sq[:, 0, :] if t == 1 else ssum[:, :], sq[:, t % 4, :], ALU.add).then_inc(sq_added, 1)

            def tokens_var(number, c):
                tt(tok[:, 2, c], tok[:, 0, c], tok[:, 1, c], ALU.add).then_inc(tok_step, 1)
                dve.wait_ge(tok_step, 5 * number - 4)
                nc.vector.tensor_scalar(tok[:, 2, c], tok[:, 2, c], 1.0 / D, EPS, ALU.mult, ALU.add).then_inc(tok_step, 1)

            def tokens_rstd(number, c):
                dve.wait_ge(tok_guess, 2 * number)
                tt(tok[:, 5, c], tok[:, 4, c], tok[:, 4, c], ALU.mult).then_inc(tok_step, 1)
                dve.wait_ge(tok_step, 5 * number - 2)
                stt(tok[:, 5, c], tok[:, 5, c], -0.5, tok[:, 2, c], ALU.mult, ALU.mult).then_inc(tok_step, 1)
                dve.wait_ge(tok_step, 5 * number - 1)
                stt(tok[:, 6, c], tok[:, 5, c], 1.5, tok[:, 4, c], ALU.add, ALU.mult).then_inc(tok_step, 1)
                dve.wait_ge(tok_step, 5 * number)

            dve.wait_ge(xt_made, TT)
            for f in range(4, 6):
                nc.vector.tensor_copy(x_t[:, f, :], bank_b[:, f - 4, :]).then_inc(xt_out_b, 1)
            dve.wait_ge(tok_sq, 2 * TT)
            tokens_var(1, slice(0, TT))
            for f in range(6, KT):
                nc.vector.tensor_copy(x_t[:, f, :], bank_b[:, f - 4, :]).then_inc(xt_out_b, 1)
            tokens_rstd(1, slice(0, TT))
            for t in range(TT):
                nc.vector.tensor_scalar(x_in[:, t, :], x_in[:, t, :], tok[:, 6, t:t + 1], None, ALU.mult).then_inc(xn_made, 1)
            dve.wait_ge(cols_made, 1)
            nc.vector.tensor_copy(cols1[:, :], bank_a[:, 0, 0:N_ROWS1]).then_inc(cols_out, 1)
            for n in range(SLOTS):
                split_lo(n)
            dve.wait_ge(cols_out, 1)
            for f in range(KT):
                dve.wait_ge(h_round, f + 1)
                stt(h_lo[:, f, :], sets[f // 4][:, f % 4, :], cols1[:, C_PRE + f:C_PRE + f + 1],
                    h_hi[:, f, :].bitcast(F32), ALU.mult, ALU.subtract).then_inc(h_ready, 1)

            dve.wait_ge(pos_land, 32)
            magic = 1.5 * 2.0 ** 23
            two_pi = (6.28125, 0.0019350051879882812, 3.0199159819e-07)
            steps = 0

            def step(ins):
                nonlocal steps
                steps += 1
                ins.then_inc(trig_step, 1)
                dve.wait_ge(trig_step, steps)

            step(nc.vector.tensor_copy(pos_f, pos_i))
            step(nc.vector.tensor_scalar(ang, pos_f, consts[:, 0:1], None, ALU.mult))
            step(nc.vector.tensor_scalar(turns, ang, 1.0 / 6.283185307179586, consts[:, 1:2], ALU.mult, ALU.add))
            step(nc.vector.tensor_scalar(turns, turns, magic, None, ALU.add))
            step(nc.vector.tensor_scalar(turns, turns, -magic, None, ALU.add))
            for part in two_pi:
                step(stt(ang, turns, -part, ang, ALU.mult, ALU.add))
            step(nc.vector.tensor_scalar(ang, ang, consts[:, 2:3], 3.1415925, ALU.add, ALU.min))
            step(nc.vector.tensor_scalar(ang, ang, -3.1415925, None, ALU.max))
            nc.vector.memset(u_pad[:, :, 0:LEFT], 0.0).then_inc(pool_step, 1)
            nc.vector.memset(cols_all[:, :, :], 0.0).then_inc(cols_zero, 1)
            dve.wait_ge(consts_made, 7)

            with dve.Fori(0, PAIRS) as i:
                for k in range(KT):
                    split_lo(N_PAIR + SLOTS + k, CW, i, 2 * KT)
                dve.wait_ge(stage_round, i * 3 + 1)
                stt(q_lo, bank_a[:, 1, :], Q_SCALE, q_hi.bitcast(F32), ALU.mult, ALU.subtract).then_inc(stage_ready, 1)
                dve.wait_ge(stage_round, i * 3 + 2)
                rest(k_lo, bank_a[:, 2, :], k_hi).then_inc(stage_ready, 1)
                dve.wait_ge(stage_round, i * 3 + 3)
                rest(v_lo, bank_a[:, 3, :], v_hi).then_inc(stage_ready, 1)
                for s in range(9):
                    if s < 7:
                        split_lo(N_PAIR + SLOTS + KT + s, CW, i, 2 * KT)
                    if s < 8:
                        kb = 3 - s % 4
                        n = S - Q0[kb]
                        off = L_OFF[kb]
                        d = kb * P - Q0[kb] + P
                        dve.wait_ge(soft_ready, i * 8 + (s + 1))
                        stt(sp[:, s % 2, 0:n], bank_a[:, s % 2, 0:n], 0.0, la[:, s % 2, 0:n],
                            ALU.max, ALU.add).then_inc(sp_step, 1)
                        dve.wait_ge(sp_step, i * 16 + (2 * s + 1))
                        tt(sp[:, s % 2, 0:d], sp[:, s % 2, 0:d], later[:, 2 * P - d:], ALU.mult).then_inc(sp_step, 1)
                    if s >= 1:
                        kb1 = 3 - (s - 1) % 4
                        n1 = S - Q0[kb1]
                        dve.wait_ge(attn_exp, i * 8 + s)
                        d = kb1 * P - Q0[kb1] + P
                        stt(at[:, (s - 1) % 2, 0:d], at[:, (s - 1) % 2, 0:d], BIG, later[:, 2 * P - d:],
                            ALU.min, ALU.mult).then_inc(attn_masked, 1)
                    if s < 8:
                        dve.wait_ge(l_round, i * 8 + (s + 1))
                        rest(l_lo[:, s // 4, off:off + n], sp[:, s % 2, 0:n], l_hi[:, s // 4, off:off + n]).then_inc(l_ready, 1)
                    if s >= 1:
                        dve.wait_ge(attn_round, i * 8 + s)
                        rest(at_lo[:, (s - 1) % 2, 0:n1], at[:, (s - 1) % 2, 0:n1], at_hi[:, (s - 1) % 2, 0:n1]).then_inc(attn_ready, 1)
                split_lo(N_PAIR + SLOTS + KT + 7, CW, i, 2 * KT)

            for g in range(HT):
                dve.wait_ge(pool_round, g + 1)
                rest(pool_lo[:, g, :], pooled[:, g, :], pool_hi[:, g, :]).then_inc(pool_split, 1)
            for t in range(HT):
                dve.wait_ge(o_round, t + 1)
                rest(o_lo[:, t, :], o_f[:, t, :], o_hi[:, t, :]).then_inc(o_split, 1)
            split_lo(N_SB0 + HT - 1)
            for g in range(HT):
                dve.wait_ge(y_round, g + 1)
                stt(h_lo[:, HT + g, :], bank_b[:, g, :], cols1[:, C_PSC + g:C_PSC + g + 1],
                    h_hi[:, HT + g, :].bitcast(F32), ALU.mult, ALU.subtract).then_inc(y_ready, 1)
            split_lo(N_PB0)
            dve.wait_ge(cols_zero, 1)
            for n in range(DEPTH2):
                dve.wait_ge(cols_made, n + 2)
                bank, cols = bank_b[:, n, :], cols_all[:, n, :]
                taps_in, taps_out = (v[:, L_TAP:L_FTAP].rearrange("p (c k) -> p c k", c=HT)[:, :, 0:CONV_K]
                                     for v in (bank, cols))
                nc.vector.tensor_copy(cols[:, 0:N_ROWS2], bank[:, 0:N_ROWS2]).then_inc(cols_out, 1)
                nc.vector.tensor_copy(taps_out, taps_in).then_inc(cols_out, 1)
                nc.vector.tensor_copy(cols[:, L_FTAP:N_COLS2], bank[:, L_FTAP:N_COLS2]).then_inc(cols_out, 1)
            for k in range(1, HT):
                split_lo(N_PB0 + k)

            def attention_gated(half):
                dve.wait_ge(w_used, (N_SB0, N_SB1)[half] + HT)
                dve.wait_ge(gate_ready, (1, 3)[half])
                for j in range(4):
                    tt(t_sb[:, j, :], bank_a[:, j, :], gates[:, 8 + 4 * half + j, :], ALU.mult).then_inc(sb_out, 1)

            def merge(half):
                dve.wait_ge(w_used, (N_PB0, N_PB1)[half] + HT)
                dve.wait_ge(gate_ready, (2, 4)[half])
                for j in range(5):
                    if j < 4:
                        tt(t_pb[:, j % 2, :], bank_b[:, j, :], gates[:, 4 * half + j, :], ALU.mult).then_inc(pb_out, 1)
                    if j >= 1:
                        dve.wait_ge(merge_round, 4 * half + j)
                        rest(h_lo[:, 4 * half + j - 1, :], merged[:, (j - 1) % 2, :],
                             h_hi[:, 4 * half + j - 1, :]).then_inc(merge_split, 1)
                    if j < 4:
                        dve.wait_ge(pb_out, 4 * half + j + 1)
                        dve.wait_ge(sb_out, 4 * half + j + 1)
                        tt(merged[:, j % 2, :], t_pb[:, j % 2, :], t_sb[:, j, :], ALU.add).then_inc(merge_ready, 1)

            attention_gated(0)
            for k in range(HT):
                split_lo(N_SB1 + k)
            merge(0)
            for k in range(HT):
                split_lo(N_PB1 + k)
            dve.wait_ge(trig_sin, 1)
            nc.vector.tensor_scalar(trig[ND:P, :], trig[ND:P, :], consts[ND:P, 3:4], MLA_SCALE, ALU.mult, ALU.mult).then_inc(trig_step, 1)
            nc.vector.memset(trig[0:ND, :], MLA_SCALE).then_inc(trig_step, 1)
            attention_gated(1)
            for k in range(HT):
                split_lo(N_OUT + k)
            merge(1)
            for n in range(N_OUT + SLOTS, N_OUT + KT + SLOTS):
                split_lo(n)

            def post_out(tiles, col, before_sq):
                for f in tiles:
                    dve.wait_ge(sq_ready, before_sq + f + 1)
                    nc.vector.tensor_scalar(mixg[:, f, :], sets[f // 4][:, f % 4, :], cols1[:, col + f:col + f + 1],
                                            None, ALU.mult).then_inc(mix_out, 1)

            def x_update(number, turn, gain):
                dve.wait_ge(mix_out, KT * (turn + 1))
                for f in range(KT + 2):
                    if f < KT:
                        if f >= 4 and f % 2 == 1:
                            dve.wait_ge(x_new_p, turn * HALF_TILES + (f - 4) // 2 + 1)
                        tt(xinc[:, f % 4, :], mixg[:, f, :], rstd[:, number % 2, :], ALU.mult).then_inc(xinc_ready, 1)
                    e = f - 1
                    if 0 <= e < KT and e % 2 == 0:
                        dve.wait_ge(xinc_ready, turn * KT + e + 1)
                        tt(x_t[:, e, :], x_t[:, e, :], xinc[:, e % 4, :], ALU.add).then_inc(x_new_v, 1)
                    e = f - 2
                    if e >= 0 and gain is not None:
                        dve.wait_ge(xg_round, e + 1)
                        stt(h_lo[:, e, :], x_t[:, e, :], cols1[:, gain + e:gain + e + 1],
                            h_hi[:, e, :].bitcast(F32), ALU.mult, ALU.subtract).then_inc(xg_ready, 1)

            post_out(range(4), C_POST, 0)
            for n in range(N_OUT + KT + SLOTS, N_UP + SLOTS):
                split_lo(n)
            post_out(range(4, 8), C_POST, 0)
            rstd_of(1, bank_a[:, 0, :])
            dve.wait_ge(rstd_ready, 1)
            x_update(1, 0, C_PMLP)

            r2 = rstd[:, 1, :]

            def up1_act(g, i=0, gper=0):
                for j in range(4):
                    t = 4 * g + j
                    if j == 1:
                        split_lo(N_UP + SLOTS + (1 + g) * KT, CW, i, gper * KT)
                    dve.wait_ge(relu_sq, i * (4 * gper) + (t + 1))
                    tt(act1[:, i * (4 * gper) + t, :], relu[:, j, :], r2, ALU.mult).then_inc(a_ready, 1)
                for k in range(1, 4):
                    split_lo(N_UP + SLOTS + (1 + g) * KT + k, CW, i, gper * KT)

            for k in range(KT):
                split_lo(N_UP + SLOTS + k)
            rstd_of(2, bank_b[:, 3, :])
            dve.wait_ge(rstd_ready, 2)
            tt(r2, rstd[:, 0, :], rstd[:, 0, :], ALU.mult).then_inc(r2_ready, 1)
            dve.wait_ge(r2_ready, 1)
            up1_act(0)
            with dve.Fori(0, F1G // 2 - 1) as i:
                for g in range(1, 3):
                    for k in range(4, KT):
                        split_lo(N_UP + SLOTS + g * KT + k, CW, i, 2 * KT)
                    up1_act(g, i, 2)
            for k in range(4, KT):
                split_lo(N_UP + SLOTS + (F1G - 1) * KT + k)

            def act_lo(acts, k, i=0):
                dve.wait_ge(as_round, i * 2 + (k + 1))
                rest(as_lo[:, k % 2, :], acts[:, i * 2 + k, :], as_hi[:, k % 2, :]).then_inc(as_ready, 1)

            for k in range(2):
                act_lo(act1, k)
            up1_act(F1G - 1)
            for k in range(2):
                act_lo(act1, k + 2)
            with dve.Fori(0, F1T // 2 - 2) as kk:
                for k in range(2):
                    split_lo(N_DOWN + 2 * SLOTS + 2 * k, CW, kk, 4)
                    split_lo(N_DOWN + 2 * SLOTS + 2 * k + 1, CW, kk, 4)
                    act_lo(act1, k + 4, kk)
            post_out(range(KT), C_QMLP, 2 * KT)
            rstd_of(3, bank_a[:, 0, :])
            dve.wait_ge(rstd_ready, 3)
            meet(dve, 0, lambda: x_update(3, 1, None))

            with dve.Fori(0, DEPTH2) as l:
                nc.vector.tensor_copy(cols2[:, :], cols_all[:, bass.ds(l, 1), :].rearrange("p a n -> p (a n)")).then_inc(cols_out, 1)
                dve.wait_ge(cols_out, 1)
                def xg_lo(f, col):
                    dve.wait_ge(xg_round, (0 if col == L_MIX else KT) + f + 1)
                    stt(h_lo[:, f, :], x_t[:, f, :], cols2[:, col + f:col + f + 1], h_hi[:, f, :].bitcast(F32),
                        ALU.mult, ALU.subtract).then_inc(xg_ready, 1)

                for f in range(KT):
                    xg_lo(f, L_MIX)
                    if f < SLOTS:
                        split_lo(f)
                nc.vector.memset(upad[:, :, 0:HALO], 0.0).then_inc(pad_zero, 1)
                nc.vector.memset(upad[:, :, HALO + S:CPAD], 0.0).then_inc(pad_zero, 1)
                def split2_lo(n):
                    split_lo(n, width2(n))

                for k in range(KT):
                    split2_lo(M_A + SLOTS + k)
                rstd_of(1, bank_b[:, 3, :])
                dve.wait_ge(rstd_ready, 1)
                norm = rstd[:, 1, :]

                def projected(dst, bank):
                    tt(dst, bank, norm, ALU.mult).then_inc(proj_out, 1)

                for j in range(4):
                    projected(af[:, j, :], bank_a[:, j, :])
                for k in range(KT):
                    split2_lo(M_G + SLOTS + k)
                dve.wait_ge(w_used, M_G + KT)
                for j in range(4):
                    projected(gf[:, j, :], bank_b[:, j, :])
                for k in range(4):
                    split2_lo(M_Q + SLOTS + k)
                for j in range(4):
                    dve.wait_ge(glu_sig, j + 1)
                    tt(upad[:, j, HALO:HALO + S], af[:, j, :], gf[:, j, :], ALU.mult).then_inc(u_ready, 1)
                dve.wait_ge(pad_zero, 2)
                tap = 0

                def taps(count):
                    nonlocal tap
                    for n in range(tap, min(tap + count, HT * DVE_TAPS)):
                        i, m = n // DVE_TAPS, n % DVE_TAPS
                        acc = conv_odd[i % 2] if m % 2 else conv[:, i, :]
                        src = upad[:, i, m:m + S]
                        w = cols2[:, L_TAP + i * 32 + m:L_TAP + i * 32 + m + 1]
                        if m == 0:
                            dve.wait_ge(u_ready, i + 1)
                            ins = nc.vector.tensor_scalar(acc, src, w, cols2[:, L_BDW + i:L_BDW + i + 1], ALU.mult, ALU.add)
                        elif m == 1:
                            if i >= 2:
                                dve.wait_ge(conv_ready, i - 1)
                            ins = nc.vector.tensor_scalar(acc, src, w, None, ALU.mult)
                        else:
                            dve.wait_ge(tap_done, i * DVE_TAPS + m - 1)
                            ins = stt(acc, src, w, acc, ALU.mult, ALU.add)
                        ins.then_inc(tap_done, 1)
                        tap += 1

                for k in range(4, KT):
                    split2_lo(M_Q + SLOTS + k)
                    taps(1)
                dve.wait_ge(w_used, M_Q + KT)
                for t in range(QT):
                    projected(cq_f[:, t, :], bank_a[:, t, :])
                for t in range(QT):
                    add_square(t, KT, KT - 1, 1)
                for k in range(4):
                    split2_lo(M_KV + SLOTS + k)
                    if k < 3:
                        taps(1)
                rstd_into(2, bank_a[:, 3, :], QL, lambda: taps(2))
                for t in range(QT):
                    stt(cq_f[:, t, :], cq_f[:, t, :], cols2[:, L_GQ + t:L_GQ + t + 1], rstd[:, 0, :],
                        ALU.mult, ALU.mult).then_inc(cn_ready, 1)

                def query_latent(t):
                    dve.wait_ge(lat_round, t + 1)
                    rest(lat_lo[:, t, :], cq_f[:, t, :], lat_hi[:, t, :]).then_inc(lat_ready, 1)
                    split2_lo(M_PAIR + t)

                for t in range(QT - 1):
                    query_latent(t)
                dve.wait_ge(w_used, M_KV + KT)
                for t in range(KVT):
                    projected(ckv_f[:, t, :], bank_b[:, t, :])
                stt(krf[ND:P, :], bank_b[ND:P, 2, :], 1.0 / MLA_SCALE, norm[ND:P, :], ALU.mult, ALU.mult).then_inc(proj_out, 1)
                query_latent(QT - 1)
                for t in range(KVT):
                    add_square(t, KT + QT, KT + QT - 2, 2)
                split2_lo(M_PAIR + QT)

                def shared_key():
                    dve.wait_ge(proj_out, 8 + QT + KVT + 1)
                    dve.wait_ge(trig_step, 12)
                    first, second = slice(ND, ND + RD), slice(ND + RD, P)
                    tt(rot[first, 0, :], krf[first, :], trig[first, :], ALU.mult).then_inc(kr_step, 1)
                    tt(rot[first, 1, :], krf[second, :], trig[second, :], ALU.mult).then_inc(kr_step, 1)
                    dve.wait_ge(kr_step, 2)
                    tt(rot[first, 0, :], rot[first, 0, :], rot[first, 1, :], ALU.add).then_inc(kr_step, 1)
                    dve.wait_ge(kr_step, 3)
                    nc.vector.tensor_copy(rot[second, 0, :], rot[first, 0, :]).then_inc(kr_step, 1)

                rstd_into(3, bank_b[:, 3, :], KVL, shared_key)
                for t in range(KVT):
                    stt(ckv_f[:, t, :], ckv_f[:, t, :], cols2[:, L_GKV + t:L_GKV + t + 1], rstd[:, 0, :],
                        ALU.mult, ALU.mult).then_inc(cn_ready, 1)

                def make_q(i, banks):
                    dve.wait_ge(w_used, M_PAIR + i * SLOTS + QT)
                    for hd in range(2):
                        tt(qf[:, hd, :], banks[hd], trig[:, :], ALU.mult).then_inc(q_made, 1)

                def stage_q_lo(i):
                    for hd in range(2):
                        dve.wait_ge(qk_round, i * 4 + hd + 1)
                        rest(kq_lo[i % 2][hd], qf[:, hd, :], kq_hi[i % 2][hd]).then_inc(qk_ready, 1)

                def stage_k_lo(i, hd, bank):
                    dve.wait_ge(qk_round, i * 4 + 3 + hd)
                    rest(kk_lo[i % 2][hd][0:ND, :], bank[0:ND, :], kk_hi[i % 2][hd][0:ND, :]).then_inc(qk_ready, 1)

                def key_behind(q):
                    for hd in range(2):
                        dve.wait_ge(kr_round, 2 * q + hd + 1)
                        rest(kk_lo[q][hd][ND:P, :], rot[ND:P, 0, :], kk_hi[q][hd][ND:P, :]).then_inc(kr_ready, 1)

                make_q(0, first_banks[0])
                for t in range(KVT):
                    dve.wait_ge(lat_round, QT + t + 1)
                    rest(lat_lo[:, QT + t, :], ckv_f[:, t, :], lat_hi[:, QT + t, :]).then_inc(lat_ready, 1)
                key_behind(0)
                stage_q_lo(0)
                taps(taps_by(-1) - tap)
                for hd in range(2):
                    stage_k_lo(0, hd, first_banks[1][hd])
                key_behind(1)
                for k in range(SLOTS):
                    split2_lo(M_PAIR + SLOTS + k)

                for g in range(BLOCKS + 2):
                    i, m = g // (2 * TT), g % (2 * TT)
                    if g < BLOCKS:
                        b = g % TT
                        dve.wait_ge(s_ready, g + 1)
                        nc.vector.tensor_reduce(soft[:, 1, b:b + 1], s_banks[g % 2], AX_X, ALU.max,
                                                negate=True).then_inc(mx_step, 1)
                    if 1 <= g <= BLOCKS:
                        b = (g - 1) % TT
                        dve.wait_ge(p_exp, g)
                        nc.vector.reciprocal(soft[:, 3, b:b + 1], soft[:, 2, b:b + 1]).then_inc(p_step, 1)
                        dve.wait_ge(p_step, g)
                        nc.vector.tensor_scalar(prob[:, b, :], prob[:, b, :], soft[:, 3, b:b + 1], None,
                                                ALU.mult).then_inc(p_ready, 1)
                    taps(taps_by(g) - tap)
                    if i + 1 < PAIRS:
                        if m == 4:
                            make_q(i + 1, next_banks[0])
                        if m == 6:
                            stage_q_lo(i + 1)
                        if m in (6, 7):
                            stage_k_lo(i + 1, m - 6, next_banks[1][m - 6])
                        if m in (2, 3, 5, 7):
                            split2_lo(M_PAIR + (i + 2) * SLOTS + (2, 3, 5, 7).index(m))
                    elif m in (4, 5, 6) and i < PAIRS:
                        t = m - 4
                        dve.wait_ge(o_round, t + 1)
                        rest(h_lo[:, O_TILES[t], :], o2_f[:, t, :], h_hi[:, O_TILES[t], :]).then_inc(o_split, 1)
                taps(HT * DVE_TAPS)
                dve.wait_ge(o_round, HT)
                rest(h_lo[:, O_TILES[3], :], o2_f[:, 3, :], h_hi[:, O_TILES[3], :]).then_inc(o_split, 1)
                dve.wait_ge(mean_ready, 1)
                dve.wait_ge(conv_ready, HT)
                for j in range(HT):
                    stt(conv[:, j, :], bank_b[:, 0, :], -1.0 / HALF, conv[:, j, :], ALU.mult, ALU.add).then_inc(dev_ready, 1)
                split_lo(M_WO + 4)
                for j in range(HT):
                    add_square(j, KT + KVT + QT, KT + KVT + QT - 3, 3)
                for k in range(5, 8):
                    split_lo(M_WO + k)
                rstd_into(4, bank_b[:, 2, :], HALF)
                for j in range(HT):
                    tt(conv[:, j, :], conv[:, j, :], rstd[:, 0, :], ALU.mult).then_inc(ln_out, 1)
                for j in range(HT):
                    dve.wait_ge(cu_round, j + 1)
                    rest(h_lo[:, C_TILES[j], :], un[:, j, :], h_hi[:, C_TILES[j], :]).then_inc(cu_ready, 1)
                for n in range(M_WO + 8, M_WO + 16):
                    split_lo(n)

                def x_add(f, set_):
                    tt(x_t[:, f, :], x_t[:, f, :], set_[:, f % 4, :], ALU.add).then_inc(x_new, 1)

                dve.wait_ge(w_used, M_WO + 3 * HT)
                for f in range(4):
                    x_add(f, bank_a)
                for n in range(M_UP, M_UP + SLOTS):
                    split_lo(n)
                dve.wait_ge(w_used, M_UP)
                for f in range(KT):
                    if f < 4:
                        x_add(4 + f, bank_b)
                    xg_lo(f, L_FFN)
                nc.vector.memset(zp[:, :, 0:1], 0.0).then_inc(zp_zero, 1)
                nc.vector.memset(zp[:, :, S + 1:ZPAD], 0.0).then_inc(zp_zero, 1)

                def ffn_tiles(g, i=0, gper=0):
                    def split(k):
                        split_lo(M_UP + SLOTS + (1 + g) * KT + k, CW, i, gper * KT)

                    z0 = i * (4 * gper) + 4 * g
                    dve.wait_ge(w_used, i * (gper * KT) + (M_UP + g * KT + KT))
                    for j in range(4):
                        tt(zp[:, j, 1:1 + S], sets[g % 2][:, j, :], rstd[:, 1, :], ALU.mult).then_inc(z_out, 1)
                    for tap, done in ((0, z_tap), (2, z_conv)):
                        for j in range(4):
                            tile = i * (2 * gper) + (2 * g + j % 2 + F2T * (j // 2))
                            dve.wait_ge(z_tap if tap else z_mid, z0 + (j + 1))
                            stt(cz[:, j, :], zp[:, j, tap:tap + S],
                                cols2[:, bass.ds(tile + (L_FTAP + tap * 2 * F2T), 1)], cz[:, j, :],
                                ALU.mult, ALU.add).then_inc(done, 1)
                        split(tap // 2)
                    for j in range(2):
                        dve.wait_ge(z_silu, i * (2 * gper) + (2 * g + j + 1))
                        dve.wait_ge(z_conv, z0 + (j + 3))
                        tt(act2[:, i * (2 * gper) + (2 * g + j), :], cz[:, j, :], cz[:, 2 + j, :],
                           ALU.mult).then_inc(a_ready, 1)
                    split(2)
                    split(3)

                for k in range(KT):
                    split_lo(M_UP + SLOTS + k)
                rstd_of(5, bank_b[:, 3, :])
                dve.wait_ge(rstd_ready, 5)
                dve.wait_ge(zp_zero, 2)
                ffn_tiles(0)
                with dve.Fori(0, F2G // 2 - 1) as i:
                    for g in range(1, 3):
                        for k in range(4, KT):
                            split_lo(M_UP + SLOTS + g * KT + k, CW, i, 2 * KT)
                        ffn_tiles(g, i, 2)
                for k in range(4, KT):
                    split_lo(M_UP + SLOTS + (F2G - 2) * KT + k)
                ffn_tiles(F2G - 2)
                for k in range(4, KT):
                    split_lo(M_UP + SLOTS + (F2G - 1) * KT + k)

                for k in range(2):
                    act_lo(act2, k)
                ffn_tiles(F2G - 1)
                for k in range(2):
                    act_lo(act2, k + 2)
                with dve.Fori(0, F2T // 2 - 2) as kk:
                    for k in range(2):
                        split_lo(M_DOWN + 2 * SLOTS + 2 * k, CW, kk, 4)
                        split_lo(M_DOWN + 2 * SLOTS + 2 * k + 1, CW, kk, 4)
                        act_lo(act2, k + 4, kk)
                dve.wait_ge(w_used, M_END - 1)
                for f in range(4):
                    x_add(f, bank_b)
                dve.wait_ge(w_used, M_END)
                for f in range(4, KT):
                    x_add(f, bank_a)
                meet(dve, l + 1)

            dve.wait_ge(gain_land, 16)
            for pair in range(2):
                c = slice(2 * pair, 2 * pair + 2)
                dve.wait_ge(tok_sq, 2 * TT + 4 * pair + 4)
                tokens_var(2 + pair, c)
                tokens_rstd(2 + pair, c)
                for t in range(2 * pair, 2 * pair + 2):
                    for half in range(2):
                        c = slice(half * S, half * S + S)
                        stt(y_out[:, t, c], y_bank(t, half), tok[:, 6, t:t + 1], gain_fin[:, c],
                            ALU.mult, ALU.mult).then_inc(y_made, 1)

        @block.tensor
        def _(pe):
            def use(n, i=0, per=0):
                pe.wait_ge(w_split, i * per + (n + 1))
                return n % SLOTS

            def mm3(out_, a_hi, a_lo, b_hi, b_lo, start, stop, loose=False):
                nc.tensor.matmul(out_, a_hi, b_hi, start=start, stop=False, skip_group_check=loose)
                nc.tensor.matmul(out_, a_hi, b_lo, start=False, stop=False, skip_group_check=loose)
                return nc.tensor.matmul(out_, a_lo, b_hi, start=False, stop=stop, skip_group_check=loose)

            def wide(set_, s, b_hi, b_lo, start, stop, tiles=4):
                for j in range(tiles):
                    c = slice(j * P, j * P + P)
                    last = mm3(set_[:, j, :], w_hi[:, s, c], w_lo[:, s, c], b_hi, b_lo, start, stop)
                last.then_inc(w_used, 1)

            def total(bank, added):
                pe.wait_ge(sq_added, added)
                nc.tensor.matmul(bank, ones[:, :], ssum[:, :], start=True, stop=True).then_inc(stat_ready, 1)

            def total_squares(before_sq, before_mix):
                pe.wait_ge(mix_out, before_mix + 1)
                for f in range(KT):
                    pe.wait_ge(sq_ready, before_sq + f + 1)
                    nc.tensor.matmul(bank_a[:, 0, :], ones[:, :], sq[:, f % 4, :], start=f == 0,
                                     stop=f == KT - 1).then_inc(sq_added if f < KT - 1 else stat_ready, 1)

            pe.wait_ge(consts_made, 2)

            def turn_input(done):
                for f in range(KT):
                    last = nc.tensor.transpose(sets[f // 4][:, f % 4, t * P:t * P + P], x_in[:, t, f * P:f * P + P], ident[:, :])
                last.then_inc(done, 1)

            for t in range(TT):
                pe.wait_ge(x_land[t], 16)
                turn_input(xt_made)
            pe.wait_ge(rows1_land, 16 * 6)
            pe.wait_ge(xt_out, 1)
            nc.tensor.transpose(bank_a[:, 0, 0:N_ROWS1], rows1, ident[0:N_ROWS1, 0:N_ROWS1]).then_inc(cols_made, 1)
            pe.wait_ge(xt_out, 4)
            pe.wait_ge(xt_out_b, 4)
            pe.wait_ge(cols_out, 1)
            for t in range(TT):
                pe.wait_ge(xn_made, t + 1)
                turn_input(ht_made)
            pe.wait_ge(consts_made, 3)
            pe.wait_ge(h_ready, 4)

            with pe.Fori(0, PAIRS) as i:
                for k in range(KT):
                    s = use(N_PAIR + k, i, 2 * KT)
                    pe.wait_ge(h_ready, k + 1)
                    wide(bank_a, s, h_hi[:, k, :], h_lo[:, k, :], k == 0, k == KT - 1)

                def gate(k):
                    s = use(N_PAIR + KT + k, i, 2 * KT)
                    if k == 0:
                        pe.wait_ge(h_ready, KT)
                        pe.wait_ge(tri_made, 1)
                    wide(bank_b, s, h_hi[:, k, :], h_lo[:, k, :], k == 0, k == KT - 1)

                def scores(s):
                    hd, kb = s // 4, 3 - s % 4
                    rows = slice(HEAD * hd, HEAD * hd + HEAD)
                    c = slice(kb * P, kb * P + P)
                    if s == 0:
                        pe.wait_ge(stage_ready, i * 3 + 2)
                        pe.wait_ge(u_out, i + 1)
                    if s >= 2:
                        pe.wait_ge(attn_exp, i * 8 + (s - 1))
                    mm3(bank_a[:, s % 2, 0:S - Q0[kb]], k_hi[rows, c], k_lo[rows, c], q_hi[rows, Q0[kb]:S],
                        q_lo[rows, Q0[kb]:S], True, True).then_inc(z_ready, 1)

                def log_sums(s):
                    hd, kb = s // 4, 3 - s % 4
                    pe.wait_ge(l_ready, i * 8 + (s + 1))
                    for kb2 in range(kb, TT):
                        off, n = L_OFF[kb2], S - Q0[kb2]
                        z0 = Q0[kb2] - Q0[kb]
                        for part in (l_hi, l_lo):
                            last = nc.tensor.matmul(bank_a[:, s % 2, z0:z0 + n], tri[:, 0 if kb2 == kb else 1, :],
                                                    part[:, hd, off:off + n], start=False,
                                                    stop=kb2 == TT - 1 and part is l_lo, skip_group_check=True)
                    last.then_inc(c_ready, 1)

                def values(s):
                    hd, kb = s // 4, 3 - s % 4
                    c = slice(kb * P, kb * P + P)
                    n = S - Q0[kb]
                    if s == 0:
                        pe.wait_ge(stage_ready, i * 3 + 3)
                    pe.wait_ge(attn_ready, i * 8 + (s + 1))
                    mm3(bank_a[:, 2 + hd, Q0[kb]:S], v_hi[:, c], v_lo[:, c], at_hi[:, s % 2, 0:n], at_lo[:, s % 2, 0:n],
                        kb == TT - 1, kb == 0, True).then_inc(av_done, 1)

                gate(0)
                scores(0)
                pe.wait_ge(v_out, i + 1)
                for j in range(TT):
                    c = slice(j * P, j * P + P)
                    last = nc.tensor.transpose(bank_a[:, 3, c], v_f[:, c], ident[:, :])
                last.then_inc(vt_made, 1)
                for s in range(8):
                    if s in GATE_AT:
                        gate(1 + GATE_AT.index(s))
                    if s < 7:
                        scores(s + 1)
                    log_sums(s)
                    if s >= 1:
                        values(s - 1)
                gate(7)
                values(7)
                pe.wait_ge(attn_exp, i * 8 + 8)
                pe.wait_ge(o_out, i * 2 + 2)

            pe.wait_ge(gate_out, 4 * PAIRS)
            s = use(N_MIX)
            for g in range(HT):
                pe.wait_ge(pool_split, g + 1)
                c = slice(g * P, g * P + P)
                last = mm3(bank_b[:, g, :], w_hi[:, s, c], w_lo[:, s, c], pool_hi[:, g, :], pool_lo[:, g, :], True, True)
            last.then_inc(w_used, 1)
            for k in range(HT):
                if k == 2:
                    pe.wait_ge(y_ready, HT)
                    pe.wait_ge(rows2_land, 16 * (8 + 2 * DEPTH2))
                    for n in range(DEPTH2):
                        bank = bank_b[:, n, :]
                        nc.tensor.transpose(bank[:, 0:N_ROWS2], rows2[:, n, :], ident[0:N_ROWS2, 0:N_ROWS2])
                        for c in range(HT):
                            nc.tensor.transpose(bank[:, L_TAP + 32 * c:L_TAP + 32 * c + CONV_K], rows_tap[n][:, c * P:c * P + P],
                                                ident[0:CONV_K, 0:CONV_K])
                        for tap in range(3):
                            c = L_FTAP + tap * 2 * F2T
                            last = nc.tensor.transpose(bank[:, c:c + 2 * F2T], rows_ftap[n][:, tap, :],
                                                       ident[0:2 * F2T, 0:2 * F2T])
                        last.then_inc(cols_made, 1)
                s = use(N_SB0 + k)
                pe.wait_ge(o_split, k + 1)
                wide(bank_a, s, o_hi[:, k, :], o_lo[:, k, :], k == 0, k == HT - 1)
            pe.wait_ge(cols_out, 1 + 3 * DEPTH2)
            for k in range(HT):
                s = use(N_PB0 + k)
                wide(bank_b, s, h_hi[:, HT + k, :], h_lo[:, HT + k, :], k == 0, k == HT - 1)
            pe.wait_ge(sb_out, 4)
            for k in range(HT):
                s = use(N_SB1 + k)
                wide(bank_a, s, o_hi[:, k, :], o_lo[:, k, :], k == 0, k == HT - 1)
            pe.wait_ge(pb_out, 4)
            for k in range(HT):
                s = use(N_PB1 + k)
                wide(bank_b, s, h_hi[:, HT + k, :], h_lo[:, HT + k, :], k == 0, k == HT - 1)
            for half, branch_out in enumerate((sb_out, pb_out)):
                pe.wait_ge(branch_out, 8)
                for k in range(KT):
                    s = use(N_OUT + half * KT + k)
                    pe.wait_ge(merge_split, k + 1)
                    wide(sets[half], s, h_hi[:, k, :], h_lo[:, k, :], k == 0, k == KT - 1)
            total_squares(0, 0)

            def up1(set_, g, i=0, gper=0):
                for k in range(KT):
                    s = use(N_UP + g * KT + k, i, gper * KT)
                    if g == 0:
                        pe.wait_ge(xg_ready, k + 1)
                    wide(set_, s, h_hi[:, k, :], h_lo[:, k, :], k == 0, k == KT - 1)

            pe.wait_ge(var_ready, 1)
            pe.wait_ge(mix_out, KT)
            up1(bank_a, 0)
            total(bank_b[:, 3, :], 2 * (KT - 1))
            pe.wait_ge(var_ready, 2)
            with pe.Fori(0, F1G // 2 - 1) as i:
                up1(bank_b, 1, i, 2)
                pe.wait_ge(relu_out, i * 8 + 4)
                up1(bank_a, 2, i, 2)
                pe.wait_ge(relu_out, i * 8 + 8)
            up1(bank_b, F1G - 1)

            def down(order, n, k, half, start, stop, i=0):
                s = use(n + 2 * k + half, i, 4)
                pe.wait_ge(as_ready, i * 2 + (k + 1))
                wide(order[half], s, as_hi[:, k % 2, :], as_lo[:, k % 2, :], start, stop)

            def down_all(order, n, count, out_of_set, groups):
                for k in range(2):
                    for half in range(2):
                        if k == 0:
                            pe.wait_ge(out_of_set, 4 * (groups - 1 + half))
                        down(order, n, k, half, k == 0, False)
                with pe.Fori(0, count // 2 - 2) as kk:
                    for k in range(2, 4):
                        for half in range(2):
                            down(order, n, k, half, False, False, kk)
                for k in range(count - 2, count):
                    for half in range(2):
                        down(order, n, k, half, False, k == count - 1)

            down_all(sets, N_DOWN, F1T, relu_out, F1G)
            total_squares(2 * KT, KT)
            meet(pe, 0)

            with pe.Fori(0, DEPTH2) as l:
                def project(set_, n0, tiles):
                    for k in range(KT):
                        s = use(n0 + k)
                        pe.wait_ge(xg_ready, k + 1)
                        wide(set_, s, h_hi[:, k, :], h_lo[:, k, :], k == 0, k == KT - 1, tiles)

                project(bank_a, M_A, 4)
                total(bank_b[:, 3, :], KT - 1)
                pe.wait_ge(var_ready, 1)
                project(bank_b, M_G, 4)
                pe.wait_ge(proj_out, 4)
                project(bank_a, M_Q, QT)
                pe.wait_ge(proj_out, 8)
                for k in range(KT):
                    if k == 4:
                        total(bank_a[:, 3, :], KT + QT - 2)
                    s = use(M_KV + k)
                    for j in range(KVT + 1):
                        c = slice(j * P, j * P + P) if j < KVT else slice(KV_COLS - P, KV_COLS)
                        last = mm3(bank_b[:, j, :], w_hi[:, s, c], w_lo[:, s, c], h_hi[:, k, :], h_lo[:, k, :],
                                   k == 0, k == KT - 1)
                    last.then_inc(w_used, 1)

                def queries(i, k, banks):
                    s = use(M_PAIR + i * SLOTS + k)
                    pe.wait_ge(lat_ready, k + 1)
                    for hd in range(2):
                        c = slice(hd * P, hd * P + P)
                        last = mm3(banks[hd], w_hi[:, s, c], w_lo[:, s, c], lat_hi[:, k, :], lat_lo[:, k, :],
                                   k == 0, k == QT - 1)
                    last.then_inc(w_used, 1)

                def keys(i, hd, bank):
                    s = use(M_PAIR + i * SLOTS + QT)
                    pe.wait_ge(lat_ready, QT + KVT)
                    for kk in range(KVT):
                        c = slice(kk * 4 * ND + hd * 2 * ND, kk * 4 * ND + hd * 2 * ND + P)
                        last = mm3(bank, w_hi[:, s, c], w_lo[:, s, c], lat_hi[:, QT + kk, :], lat_lo[:, QT + kk, :],
                                   kk == 0, kk == KVT - 1)
                    last.then_inc(k_done if hd == 0 else w_used, 1)

                def values_of(i, bank):
                    pe.wait_ge(vt_out, 2 * i + 2)
                    for j in range(TT):
                        c = slice(j * P, j * P + P)
                        last = nc.tensor.transpose(bank[:, c], vt_f[:, c], ident[:, :])
                    last.then_inc(v_turned, 1)

                pe.wait_ge(proj_out, 8 + QT)
                for k in range(QT):
                    queries(0, k, first_banks[0])
                total(bank_b[:, 3, :], KT + QT + KVT - 3)
                pe.wait_ge(var_ready, 2)
                for hd in range(2):
                    keys(0, hd, first_banks[1][hd])
                values_of(0, first_banks[2])

                def scores2(g):
                    i, hd, b = g // (2 * TT), g // TT % 2, g % TT
                    c = slice(b * P, b * P + P)
                    if b == 0 and hd == 0:
                        pe.wait_ge(qk_ready, i * 4 + 4)
                        pe.wait_ge(kr_ready, 2 * min(i + 1, 2))
                    if g >= 2:
                        pe.wait_ge(p_exp, g - 1)
                    q = i % 2
                    mm3(s_banks[g % 2], kq_hi[q][hd][:, c], kq_lo[q][hd][:, c], kk_hi[q][hd], kk_lo[q][hd],
                        True, True).then_inc(s_ready, 1)

                def transposed(g):
                    b = g % TT
                    if g >= 2:
                        pe.wait_ge(pt_ready, g - 1)
                    pe.wait_ge(p_ready, g + 1)
                    for kb in range(TT):
                        c = slice(kb * P, kb * P + P)
                        last = nc.tensor.transpose(bank_a[:, g % 2, c], prob[:, b, c], ident[:, :])
                    last.then_inc(pt_made, 1)

                def values2(i, hd, blocks):
                    for kb in blocks:
                        if kb == 0:
                            pe.wait_ge(pt_ready, i * 8 + 4 * hd + 4)
                            pe.wait_ge(vv_ready, i + 1)
                            if i > 0 or hd > 0:
                                pe.wait_ge(o2_out, i * 2 + hd)
                        c = slice(kb * P, kb * P + P)
                        part = nc.tensor.matmul(bank_b[:, 1, :], vvs[i % 2][:, c], pts[hd][:, kb, :],
                                                start=kb == 0, stop=kb == TT - 1)
                    if kb == TT - 1:
                        part.then_inc(pv_done, 1)

                def beside(i, m):
                    if m < QT:
                        if m == 0:
                            pe.wait_ge(qk_ready, i * 4 + 4)
                        queries(i + 1, m, next_banks[0])
                    elif m == 4:
                        pe.wait_ge(vv_ready, i + 1)
                        keys(i + 1, 0, next_banks[1][0])
                    elif m == 5:
                        pe.wait_ge(q_made, 2 * i + 4)
                        keys(i + 1, 1, next_banks[1][1])
                    elif m == 7:
                        pe.wait_ge(qk_ready, i * 4 + 7)
                        values_of(i + 1, next_banks[2])

                for g in range(2):
                    scores2(g)
                for g in range(BLOCKS):
                    i, m = g // (2 * TT), g % (2 * TT)
                    if g + 2 < BLOCKS:
                        scores2(g + 2)
                    if i + 1 < PAIRS:
                        beside(i, m)
                    transposed(g)
                    if m % TT < len(PV_BLOCKS) and g >= TT:
                        values2((g - TT) // (2 * TT), 0 if m >= TT else 1, PV_BLOCKS[m % TT])
                values2(PAIRS - 1, 1, range(TT))
                for j in range(HT):
                    pe.wait_ge(conv_ready, j + 1)
                    last = nc.tensor.matmul(bank_b[:, 0, :], ones[:, :], conv[:, j, :], start=j == 0, stop=j == HT - 1)
                last.then_inc(mean_ready, 1)

                pe.wait_ge(pt_ready, 8 * PAIRS)
                for n, (half, k) in enumerate(WO_ORDER, M_WO):
                    s = use(n)
                    if n == M_WO + HT:
                        total(bank_b[:, 2, :], KT + KVT + QT + HT - 4)
                        pe.wait_ge(dev_ready, HT)
                        pe.wait_ge(var_ready, 4)
                        pe.wait_ge(o2_out, 2 * PAIRS)
                    pe.wait_ge(o_split if k < HT else cu_ready, k % HT + 1)
                    t = (O_TILES + C_TILES)[k]
                    wide(sets[half], s, h_hi[:, t, :], h_lo[:, t, :], k == 0, k == KT - 1)

                def up2(set_, g, i=0, gper=0):
                    for k in range(KT):
                        s = use(M_UP + g * KT + k, i, gper * KT)
                        if g == 0:
                            pe.wait_ge(xg_ready, KT + k + 1)
                        wide(set_, s, h_hi[:, k, :], h_lo[:, k, :], k == 0, k == KT - 1)

                pe.wait_ge(x_new, 4)
                up2(bank_a, 0)
                pe.wait_ge(x_new, KT)
                total(bank_b[:, 3, :], KT + KVT + QT + HT - 4 + KT - 1)
                pe.wait_ge(var_ready, 5)
                with pe.Fori(0, F2G // 2 - 1) as i:
                    up2(bank_b, 1, i, 2)
                    pe.wait_ge(z_out, i * 8 + 4)
                    up2(bank_a, 2, i, 2)
                    pe.wait_ge(z_out, i * 8 + 8)
                up2(bank_b, F2G - 2)
                pe.wait_ge(z_out, 4 * (F2G - 2))
                up2(bank_a, F2G - 1)
                down_all((bank_b, bank_a), M_DOWN, F2T, z_out, F2G)
                meet(pe, l + 1)

            for t in range(TT):
                for f in range(KT):
                    c = (f % 4) * P
                    last = nc.tensor.transpose(y_bank(t, f // 4)[:, c:c + P], x_t[:, f, t * P:t * P + P], ident[:, :])
                last.then_inc(yt_made, 1)


_BLOCK1 = ["x", "g_pre_mix", "w_in", "w_pool_mix", "pool_scale", "w_br_pool", "w_br_sb", "w_gate", "b_gate", "w_out",
           "g_post_mix", "g_pre_mlp", "w_up", "w_down", "g_post_mlp"]
_BLOCK2 = ["positions_2", "g_mix_2", "w_in_2", "g_q_2", "w_uq_2", "g_kv_2", "w_ukv_2", "w_dw_conv_2", "b_dw_conv_2",
           "g_conv_ln_2", "b_conv_ln_2", "w_o_2", "g_ffn_2", "w_up_2", "w_dw_ffn_2", "b_dw_ffn_2", "w_down_2",
           "g_final_2"]


def shape_constants(np):
    row = np.arange(P)
    cosine = (row // RD) % 2 == 0
    freq = 1.0 / (np.float32(10000.0) ** (np.arange(0, RD, 2, dtype=np.float32) / np.float32(RD)))
    c = np.zeros((P, 4 + LEFT), np.float32)
    c[:, 0] = freq[row % (RD // 2)]
    c[:, 1] = np.where(cosine, 0.25, 0.0)
    c[:, 2] = np.where(cosine, np.pi / 2, 0.0)
    c[:, 3] = np.where(cosine | (row % RD >= RD // 2), 1.0, -1.0)
    c[:, 4:] = 1.0 / (np.arange(LEFT) + 1.0)
    return c


def kernel(**inputs):
    import numpy as _np
    import concourse.bacc as _bacc
    from concourse import mybir as _mybir
    from concourse.bass_utils import run_bass_kernel_spmd as _run

    nc = _bacc.Bacc("TRN2", target_bir_lowering=False, num_devices=1)
    arrays, args = {}, []
    given = [(name, _np.ascontiguousarray(inputs[name])) for name in _BLOCK1 + _BLOCK2]
    given.append(("shape_consts", shape_constants(_np)))
    for name, a in given:
        arrays[f"in_{name}_dram"] = a
        args.append(nc.dram_tensor(f"in_{name}_dram", a.shape, _mybir.dt.from_np(a.dtype), kind="ExternalInput").ap())
    args.append(nc.dram_tensor("out_dram", (1, S, D), _mybir.dt.float32, kind="ExternalOutput").ap())
    two_blocks(nc, *args)
    r = _run(nc, [arrays], core_ids=[0])
    return r.results[0]["out_dram"]
```
